# Optimizing a Trainium2 kernel written in Bass

```python
import math
import jax, jax.numpy as jnp
from jax import lax
import numpy as np

D_MODEL = 1024
BATCH = 1
SEQ = 256
DEPTH = 1

CHUNK = 64
Q_BLOCK = 128
RMS_EPS = 1e-6
ROPE_THETA = 10000.0
MAX_STREAM_OFFSET_CHUNKS = 512

DA_HEADS = 8
DA_HEAD_DIM = 64
DA_QK_WIDTH = DA_HEADS * 2 * DA_HEAD_DIM
DA_V_DIM = 2 * DA_HEAD_DIM
DA_V_WIDTH = DA_HEADS * DA_V_DIM

MLA_HEADS = 8
MLA_Q_RANK = 384
MLA_KV_RANK = 256
MLA_NOPE_DIM = 128
MLA_ROPE_DIM = 64
MLA_V_DIM = 128
MLA_QK_DIM = MLA_NOPE_DIM + MLA_ROPE_DIM
MLA_V_WIDTH = MLA_HEADS * MLA_V_DIM

IN_SPLITS = (DA_QK_WIDTH, DA_QK_WIDTH, DA_V_WIDTH, MLA_Q_RANK, MLA_KV_RANK, MLA_ROPE_DIM,
             D_MODEL, D_MODEL)
IN_COLS = sum(IN_SPLITS)

D_FF = ((8 * D_MODEL // 3 + 255) // 256) * 256


def rms_norm(x, w):
    xf = x.astype(jnp.float32)
    y = xf * lax.rsqrt(jnp.mean(xf * xf, axis=-1, keepdims=True) + RMS_EPS)
    return (y * w.astype(jnp.float32)).astype(x.dtype)

def rope(x, positions):
    d = x.shape[-1]
    half = d // 2
    inv_freq = 1.0 / (ROPE_THETA ** (jnp.arange(half, dtype=jnp.float32) * (2.0 / d)))
    ang = positions.astype(jnp.float32)[:, None, :, None] * inv_freq
    cos, sin = jnp.cos(ang), jnp.sin(ang)
    x1 = x[..., :half].astype(jnp.float32)
    x2 = x[..., half:].astype(jnp.float32)
    out = jnp.concatenate([x1 * cos - x2 * sin, x2 * cos + x1 * sin], axis=-1)
    return out.astype(x.dtype)

def split_heads(t, n_heads):
    b, s, w = t.shape
    return t.reshape(b, s, n_heads, w // n_heads).transpose(0, 2, 1, 3)

def merge_heads(t):
    b, h, s, d = t.shape
    return t.transpose(0, 2, 1, 3).reshape(b, s, h * d)

def chunk_causal_attention(q, k, v, scale):
    b, h, s, dk = q.shape
    dv = v.shape[-1]
    nb = s // Q_BLOCK
    q_blocks = q.reshape(b, h, nb, Q_BLOCK, dk).transpose(2, 0, 1, 3, 4)
    key_chunk = jnp.arange(s) // CHUNK

    def one_block(args):
        qi, i = args
        q_chunk = (i * Q_BLOCK + jnp.arange(Q_BLOCK)) // CHUNK
        mask = key_chunk[None, :] <= q_chunk[:, None]
        sc = jnp.einsum('bhqd,bhkd->bhqk', qi, k,
                        preferred_element_type=jnp.float32) * scale
        sc = jnp.where(mask, sc, jnp.float32(-1e30))
        p = jax.nn.softmax(sc, axis=-1).astype(v.dtype)
        return jnp.einsum('bhqk,bhkd->bhqd', p, v)

    out = lax.map(one_block, (q_blocks, jnp.arange(nb)))
    return out.transpose(1, 2, 0, 3, 4).reshape(b, h, s, dv)

def first_inputs(seed: int = 0) -> dict:
    key = jax.random.key(seed)
    ks = jax.random.split(key, 32)

    def dense(k, shape):
        return jax.random.normal(k, (DEPTH,) + shape, jnp.float32) * (shape[0] ** -0.5)

    def gain(k, n):
        return 1.0 + 0.05 * jax.random.normal(k, (DEPTH, n), jnp.float32)

    x = jax.random.normal(ks[0], (BATCH, SEQ, D_MODEL), jnp.float32)
    offsets = jax.random.randint(ks[1], (BATCH, 1), 0, MAX_STREAM_OFFSET_CHUNKS) * CHUNK
    positions = (offsets + jnp.arange(SEQ, dtype=jnp.int32)[None, :]).astype(jnp.int32)

    return {
        "x": x,
        "positions": positions,
        "ln_mix_pre": gain(ks[2], D_MODEL),
        "w_in": dense(ks[3], (D_MODEL, IN_COLS)),
        "lambda_q1": 0.1 * jax.random.normal(ks[4], (DEPTH, DA_HEAD_DIM), jnp.float32),
        "lambda_k1": 0.1 * jax.random.normal(ks[5], (DEPTH, DA_HEAD_DIM), jnp.float32),
        "lambda_q2": 0.1 * jax.random.normal(ks[6], (DEPTH, DA_HEAD_DIM), jnp.float32),
        "lambda_k2": 0.1 * jax.random.normal(ks[7], (DEPTH, DA_HEAD_DIM), jnp.float32),
        "da_subln": gain(ks[8], DA_V_DIM),
        "q_a_norm": gain(ks[9], MLA_Q_RANK),
        "w_uq": dense(ks[10], (MLA_Q_RANK, MLA_HEADS * MLA_QK_DIM)),
        "kv_a_norm": gain(ks[11], MLA_KV_RANK),
        "w_ukv": dense(ks[12], (MLA_KV_RANK, MLA_HEADS * (MLA_NOPE_DIM + MLA_V_DIM))),
        "w_proj_a": dense(ks[13], (DA_V_WIDTH, D_MODEL)),
        "w_proj_b": dense(ks[14], (MLA_V_WIDTH, D_MODEL)),
        "w_o": dense(ks[15], (D_MODEL, D_MODEL)),
        "ln_mix_post": gain(ks[16], D_MODEL),
        "ln_ffn_pre": gain(ks[17], D_MODEL),
        "w_ffn_gate": dense(ks[18], (D_MODEL, D_FF)),
        "w_ffn_up": dense(ks[19], (D_MODEL, D_FF)),
        "w_ffn_down": dense(ks[20], (D_FF, D_MODEL)),
        "ln_ffn_post": gain(ks[21], D_MODEL),
    }

def first_block(x, positions, ln_mix_pre, w_in, lambda_q1, lambda_k1, lambda_q2, lambda_k2,
              da_subln, q_a_norm, w_uq, kv_a_norm, w_ukv, w_proj_a, w_proj_b, w_o,
              ln_mix_post, ln_ffn_pre, w_ffn_gate, w_ffn_up, w_ffn_down, ln_ffn_post):
    bsz, seq, _ = x.shape
    offs = np.cumsum(IN_SPLITS)[:-1].tolist()
    for l in range(DEPTH):
        h = rms_norm(x, ln_mix_pre[l])
        z = h @ w_in[l]
        qa, ka, va, cq, ckv, k_rope, g_a, g_b = jnp.split(z, offs, axis=-1)

        lambda_init = 0.8 - 0.6 * math.exp(-0.3 * l)
        qa = split_heads(qa, DA_HEADS)
        ka = split_heads(ka, DA_HEADS)
        va = split_heads(va, DA_HEADS)
        q1 = rope(qa[..., :DA_HEAD_DIM], positions)
        q2 = rope(qa[..., DA_HEAD_DIM:], positions)
        k1 = rope(ka[..., :DA_HEAD_DIM], positions)
        k2 = rope(ka[..., DA_HEAD_DIM:], positions)
        da_scale = DA_HEAD_DIM ** -0.5
        o1 = chunk_causal_attention(q1, k1, va, da_scale)
        o2 = chunk_causal_attention(q2, k2, va, da_scale)
        lam = (jnp.exp(jnp.sum(lambda_q1[l].astype(jnp.float32) * lambda_k1[l].astype(jnp.float32)))
               - jnp.exp(jnp.sum(lambda_q2[l].astype(jnp.float32) * lambda_k2[l].astype(jnp.float32)))
               + lambda_init)
        oa = o1 - lam.astype(o1.dtype) * o2
        oa = rms_norm(oa, da_subln[l]) * (1.0 - lambda_init)
        y_a = merge_heads(oa) @ w_proj_a[l]

        cq = rms_norm(cq, q_a_norm[l])
        qb = split_heads(cq @ w_uq[l], MLA_HEADS)
        qb_nope = qb[..., :MLA_NOPE_DIM]
        qb_rope = rope(qb[..., MLA_NOPE_DIM:], positions)
        ckv = rms_norm(ckv, kv_a_norm[l])
        kv = split_heads(ckv @ w_ukv[l], MLA_HEADS)
        kb_nope = kv[..., :MLA_NOPE_DIM]
        vb = kv[..., MLA_NOPE_DIM:]
        kb_rope = rope(k_rope[:, None, :, :], positions)
        kb_rope = jnp.broadcast_to(kb_rope, (bsz, MLA_HEADS, seq, MLA_ROPE_DIM))
        qb_full = jnp.concatenate([qb_nope, qb_rope], axis=-1)
        kb_full = jnp.concatenate([kb_nope, kb_rope], axis=-1)
        ob = chunk_causal_attention(qb_full, kb_full, vb, MLA_QK_DIM ** -0.5)
        y_b = merge_heads(ob) @ w_proj_b[l]

        merged = jax.nn.sigmoid(g_a) * y_a + jax.nn.sigmoid(g_b) * y_b
        x = x + rms_norm(merged @ w_o[l], ln_mix_post[l])

        h = rms_norm(x, ln_ffn_pre[l])
        f = (jax.nn.silu(h @ w_ffn_gate[l]) * (h @ w_ffn_up[l])) @ w_ffn_down[l]
        x = x + rms_norm(f, ln_ffn_post[l])
    return x


RET_HEADS = 8
RET_QK_DIM = 64
RET_V_DIM = 128
DSA_HEADS = 8
DSA_HEAD_DIM = 64
DSA_KV_LATENT = 128
IDX_HEADS = 8
IDX_DIM = 64
IDX_TOPK = 256
N_BUCKETS = 32
MAX_DISTANCE = 128
N_GROUPS = 4
EXPERTS_PER_GROUP = 4
N_EXPERTS = N_GROUPS * EXPERTS_PER_GROUP
EXPERT_FF = 256
EXPERT_TOPK = 2
MOE_BLOCK = 4096
ROPE_BASE = 10000.0
NORM_EPS = 1e-6
GN_EPS = 1e-5
IN_SPLITS_2 = (RET_HEADS * RET_QK_DIM, RET_HEADS * RET_QK_DIM, RET_HEADS * RET_V_DIM, RET_HEADS * RET_V_DIM,
             DSA_HEADS * DSA_HEAD_DIM, DSA_KV_LATENT, IDX_HEADS * IDX_DIM, IDX_DIM, IDX_HEADS)
D_IN = sum(IN_SPLITS_2)


def _split_cols(z, sizes):
    offs, acc = [], 0
    for s in sizes[:-1]:
        acc += s
        offs.append(acc)
    return jnp.split(z, offs, axis=-1)

def rmsnorm(x, g):
    xf = x.astype(jnp.float32)
    y = xf * lax.rsqrt(jnp.mean(xf * xf, axis=-1, keepdims=True) + NORM_EPS)
    return (y * g.astype(jnp.float32)).astype(x.dtype)

def modulate(xn, shift, scale):
    return xn * (1.0 + scale[:, None, :]) + shift[:, None, :]

def rope_2(x, pos):
    d = x.shape[-1]
    freqs = ROPE_BASE ** (-jnp.arange(0, d, 2, dtype=jnp.float32) / d)
    ang = pos.astype(jnp.float32)[:, None] * freqs[None, :]
    cos = jnp.cos(ang)[None, :, None, :]
    sin = jnp.sin(ang)[None, :, None, :]
    x1, x2 = jnp.split(x.astype(jnp.float32), 2, axis=-1)
    return jnp.concatenate([x1 * cos - x2 * sin, x2 * cos + x1 * sin], axis=-1).astype(x.dtype)

def rel_bucket(rel):
    nb = N_BUCKETS // 2
    ret = (rel > 0).astype(jnp.int32) * nb
    n = jnp.abs(rel)
    max_exact = nb // 2
    nf = jnp.maximum(n, 1).astype(jnp.float32)
    large = max_exact + (jnp.log(nf / max_exact) / math.log(MAX_DISTANCE / max_exact)
                         * (nb - max_exact)).astype(jnp.int32)
    large = jnp.minimum(large, nb - 1)
    return ret + jnp.where(n < max_exact, n, large)

def retention_branch(q, k, v, g, gn_gain):
    B, S, H, dk = q.shape
    dv = v.shape[-1]
    N = S // CHUNK
    dt = q.dtype
    log_gamma = jnp.log(1.0 - 2.0 ** (-5.0 - jnp.arange(H, dtype=jnp.float32)))
    idx = jnp.arange(CHUNK, dtype=jnp.float32)
    intra_decay = jnp.exp(log_gamma[:, None, None] * jnp.abs(idx[:, None] - idx[None, :])).astype(dt)
    k_decay = jnp.exp(log_gamma[:, None] * (CHUNK - 1 - idx)[None, :]).astype(dt)
    q_decay = jnp.exp(log_gamma[:, None] * (idx + 1)[None, :]).astype(dt)
    chunk_decay = jnp.exp(log_gamma * CHUNK)
    qc = q.reshape(B, N, CHUNK, H, dk)
    kc = k.reshape(B, N, CHUNK, H, dk)
    vc = v.reshape(B, N, CHUNK, H, dv)
    scores = jnp.einsum('bnihd,bnjhd->bhnij', qc, kc) * intra_decay[None, :, None]
    o_intra = jnp.einsum('bhnij,bnjhe->bnihe', scores, vc)
    kv = jnp.einsum('bnjhd,hj,bnjhe->nbhde', kc, k_decay, vc)
    cd = chunk_decay.astype(kv.dtype)[None, :, None, None]

    def step(state, kv_n):
        return state * cd + kv_n, state

    _, prev = lax.scan(step, jnp.zeros((B, H, dk, dv), kv.dtype), kv)
    o_inter = jnp.einsum('bnihd,hi,nbhde->bnihe', qc, q_decay, prev)
    o = (o_intra + o_inter).reshape(B, S, H, dv).astype(jnp.float32)
    mu = jnp.mean(o, axis=-1, keepdims=True)
    var = jnp.mean(jnp.square(o - mu), axis=-1, keepdims=True)
    o = ((o - mu) * lax.rsqrt(var + GN_EPS)).reshape(B, S, H * dv) * gn_gain.astype(jnp.float32)
    return (jax.nn.silu(g.astype(jnp.float32)) * o).astype(dt)

def dsa_branch(q, k, v, qi, kidx, wi, rel_bias):
    B, S, H, dh = q.shape
    topk = min(IDX_TOPK, S // 4)
    nblk = S // Q_BLOCK
    key_chunk = jnp.arange(S, dtype=jnp.int32) // CHUNK
    idx_scale = (IDX_DIM ** -0.5) * (IDX_HEADS ** -0.5)
    kidx_f = kidx.astype(jnp.float32)

    def to_blocks(a):
        return a.reshape((B, nblk, Q_BLOCK) + a.shape[2:]).swapaxes(0, 1)

    def one_block(args):
        qb, qib, wb, start = args
        qpos = start + jnp.arange(Q_BLOCK, dtype=jnp.int32)
        qchunk = qpos // CHUNK
        s = jnp.einsum('bqhd,bkd->bqhk', qib.astype(jnp.float32), kidx_f)
        score = jnp.einsum('bqhk,bqh->bqk', jax.nn.relu(s), wb.astype(jnp.float32)) * idx_scale
        admissible = key_chunk[None, :] <= qchunk[:, None]
        score = jnp.where(admissible[None], score, -jnp.inf)
        _, sel = lax.top_k(score, topk)
        valid = key_chunk[sel] <= qchunk[None, :, None]
        kg = jax.vmap(lambda a, i: a[i])(k, sel)
        vg = jax.vmap(lambda a, i: a[i])(v, sel)
        logits = jnp.einsum('bqhd,bqkd->bqhk', qb, kg).astype(jnp.float32) * (dh ** -0.5)
        bias = rel_bias[rel_bucket(sel - qpos[None, :, None])].astype(jnp.float32)
        logits = logits + jnp.transpose(bias, (0, 1, 3, 2))
        logits = jnp.where(valid[:, :, None, :], logits, -jnp.inf)
        p = jax.nn.softmax(logits, axis=-1).astype(vg.dtype)
        return jnp.einsum('bqhk,bqkd->bqhd', p, vg)

    starts = jnp.arange(nblk, dtype=jnp.int32) * Q_BLOCK
    out = lax.map(one_block, (to_blocks(q), to_blocks(qi), to_blocks(wi), starts))
    return out.swapaxes(0, 1).reshape(B, S, H * dh)

def hier_moe(u, w_gr, b_gr, w_er, b_er, w1, w3, w2):
    B, S, D = u.shape
    T = B * S
    t = u.reshape(T, D)
    gl = (t @ w_gr + b_gr).astype(jnp.float32)
    pg = jax.nn.softmax(gl, axis=-1)
    gsel = jnp.argmax(gl, axis=-1)
    gp = jnp.take_along_axis(pg, gsel[:, None], axis=1)[:, 0]
    el = (t @ w_er + b_er).astype(jnp.float32).reshape(T, N_GROUPS, EXPERTS_PER_GROUP)
    el_sel = jnp.take_along_axis(el, gsel[:, None, None], axis=1)[:, 0]
    vals, ids = lax.top_k(el_sel, EXPERT_TOPK)
    wts = jax.nn.softmax(vals, axis=-1) * gp[:, None]
    eid = gsel[:, None].astype(jnp.int32) * EXPERTS_PER_GROUP + ids
    gates = jnp.einsum('tke,tk->te', jax.nn.one_hot(eid, N_EXPERTS, dtype=jnp.float32), wts).astype(u.dtype)
    blk = math.gcd(T, MOE_BLOCK)
    nb = T // blk

    def expert_block(args):
        xb, gb = args
        a = jnp.einsum('td,edf->tef', xb, w1)
        b = jnp.einsum('td,edf->tef', xb, w3)
        hid = jax.nn.silu(a) * b * gb[:, :, None]
        return jnp.einsum('tef,efd->td', hid, w2)

    y = lax.map(expert_block, (t.reshape(nb, blk, D), gates.reshape(nb, blk, N_EXPERTS)))
    return y.reshape(B, S, D)

def second_inputs(seed: int = 0) -> dict:
    key = jax.random.key(seed)
    ks = jax.random.split(key, 24)
    f = jnp.float32
    L, D = DEPTH, D_MODEL
    RV = RET_HEADS * RET_V_DIM
    DV = DSA_HEADS * DSA_HEAD_DIM

    def nrm(k, shape, scale):
        return jax.random.normal(k, shape, f) * scale

    def gain(k, shape):
        return 1.0 + 0.05 * jax.random.normal(k, shape, f)

    return {
        "x": nrm(ks[0], (BATCH, SEQ, D), 1.0),
        "c": nrm(ks[1], (BATCH, D), 1.0),
        "w_ada": nrm(ks[2], (L, D, 6 * D), 0.5 * D ** -0.5),
        "b_ada": nrm(ks[3], (L, 6 * D), 0.01),
        "norm_mix_g": gain(ks[4], (L, D)),
        "w_in": nrm(ks[5], (L, D, D_IN), D ** -0.5),
        "ret_gn_g": gain(ks[6], (L, RV)),
        "dsa_kv_norm_g": gain(ks[7], (L, DSA_KV_LATENT)),
        "w_dsa_kv_up": nrm(ks[8], (L, DSA_KV_LATENT, 2 * DSA_HEAD_DIM), DSA_KV_LATENT ** -0.5),
        "rel_bias": nrm(ks[9], (N_BUCKETS, DSA_HEADS), 0.5),
        "w_ret_out": nrm(ks[10], (L, RV, D), RV ** -0.5),
        "w_dsa_out": nrm(ks[11], (L, DV, D), DV ** -0.5),
        "w_gate": nrm(ks[12], (L, D, 2 * D), D ** -0.5),
        "b_gate": nrm(ks[13], (L, 2 * D), 0.01),
        "w_o": nrm(ks[14], (L, D, D), D ** -0.5),
        "norm_ffn_g": gain(ks[15], (L, D)),
        "w_group_router": nrm(ks[16], (L, D, N_GROUPS), D ** -0.5),
        "b_group_router": nrm(ks[17], (L, N_GROUPS), 0.01),
        "w_expert_router": nrm(ks[18], (L, D, N_EXPERTS), D ** -0.5),
        "b_expert_router": nrm(ks[19], (L, N_EXPERTS), 0.01),
        "w_exp_gate": nrm(ks[20], (L, N_EXPERTS, D, EXPERT_FF), D ** -0.5),
        "w_exp_up": nrm(ks[21], (L, N_EXPERTS, D, EXPERT_FF), D ** -0.5),
        "w_exp_down": nrm(ks[22], (L, N_EXPERTS, EXPERT_FF, D), EXPERT_FF ** -0.5),
        "norm_final_g": gain(ks[23], (D,)),
    }

def second_block(x, c, w_ada, b_ada, norm_mix_g, w_in, ret_gn_g, dsa_kv_norm_g, w_dsa_kv_up, rel_bias,
              w_ret_out, w_dsa_out, w_gate, b_gate, w_o, norm_ffn_g, w_group_router, b_group_router,
              w_expert_router, b_expert_router, w_exp_gate, w_exp_up, w_exp_down, norm_final_g):
    B, S, D = x.shape
    pos = jnp.arange(S, dtype=jnp.int32)
    h = x
    for l in range(DEPTH):
        mod = jax.nn.silu(c) @ w_ada[l] + b_ada[l]
        sh1, sc1, g1, sh2, sc2, g2 = jnp.split(mod, 6, axis=-1)
        u = modulate(rmsnorm(h, norm_mix_g[l]), sh1, sc1)
        z = u @ w_in[l]
        rq, rk, rv, rg, dq, dkv, iq, ik, iw = _split_cols(z, IN_SPLITS_2)
        rq = rope_2(rq.reshape(B, S, RET_HEADS, RET_QK_DIM), pos)
        rk = rope_2(rk.reshape(B, S, RET_HEADS, RET_QK_DIM), pos) * (RET_QK_DIM ** -0.5)
        y_ret = retention_branch(rq, rk, rv.reshape(B, S, RET_HEADS, RET_V_DIM), rg, ret_gn_g[l]) @ w_ret_out[l]
        lat = rmsnorm(dkv, dsa_kv_norm_g[l]) @ w_dsa_kv_up[l]
        dk, dv = jnp.split(lat, 2, axis=-1)
        y_dsa = dsa_branch(dq.reshape(B, S, DSA_HEADS, DSA_HEAD_DIM), dk, dv,
                           iq.reshape(B, S, IDX_HEADS, IDX_DIM), ik, iw, rel_bias) @ w_dsa_out[l]
        ga, gb = jnp.split(jax.nn.sigmoid(u @ w_gate[l] + b_gate[l]), 2, axis=-1)
        h = h + g1[:, None, :] * ((ga * y_ret + gb * y_dsa) @ w_o[l])
        u2 = modulate(rmsnorm(h, norm_ffn_g[l]), sh2, sc2)
        h = h + g2[:, None, :] * hier_moe(u2, w_group_router[l], b_group_router[l], w_expert_router[l],
                                         b_expert_router[l], w_exp_gate[l], w_exp_up[l], w_exp_down[l])
    return rmsnorm(h, norm_final_g)


def setup_inputs(seed=0):
    out = dict(first_inputs(seed))
    for name, value in second_inputs(seed + 1).items():
        if name != "x":
            out[name + "_2"] = value
    return out


def reference(
    x, positions, ln_mix_pre, w_in, lambda_q1, lambda_k1, lambda_q2, lambda_k2, da_subln,
    q_a_norm, w_uq, kv_a_norm, w_ukv, w_proj_a, w_proj_b, w_o, ln_mix_post, ln_ffn_pre,
    w_ffn_gate, w_ffn_up, w_ffn_down, ln_ffn_post, c_2, w_ada_2, b_ada_2, norm_mix_g_2, w_in_2,
    ret_gn_g_2, dsa_kv_norm_g_2, w_dsa_kv_up_2, rel_bias_2, w_ret_out_2, w_dsa_out_2, w_gate_2,
    b_gate_2, w_o_2, norm_ffn_g_2, w_group_router_2, b_group_router_2, w_expert_router_2,
    b_expert_router_2, w_exp_gate_2, w_exp_up_2, w_exp_down_2, norm_final_g_2,
):
    x = first_block(
        x, positions, ln_mix_pre, w_in, lambda_q1, lambda_k1, lambda_q2, lambda_k2, da_subln,
        q_a_norm, w_uq, kv_a_norm, w_ukv, w_proj_a, w_proj_b, w_o, ln_mix_post, ln_ffn_pre,
        w_ffn_gate, w_ffn_up, w_ffn_down, ln_ffn_post,
    )
    return second_block(
        x, c_2, w_ada_2, b_ada_2, norm_mix_g_2, w_in_2, ret_gn_g_2, dsa_kv_norm_g_2,
        w_dsa_kv_up_2, rel_bias_2, w_ret_out_2, w_dsa_out_2, w_gate_2, b_gate_2, w_o_2,
        norm_ffn_g_2, w_group_router_2, b_group_router_2, w_expert_router_2, b_expert_router_2,
        w_exp_gate_2, w_exp_up_2, w_exp_down_2, norm_final_g_2,
    )


_drawn_inputs = setup_inputs


def setup_inputs(seed=0):
    import zlib

    import numpy as np

    out = dict(_drawn_inputs(seed))
    spreads = {}
    factors = {'q_a_norm': 6.802,
     'kv_a_norm': 4.676,
     'b_ada_2': 8.0,
     'norm_mix_g_2': 5.597,
     'ret_gn_g_2': 8.0,
     'dsa_kv_norm_g_2': 8.0,
     'rel_bias_2': 6.849,
     'b_gate_2': 8.0,
     'norm_ffn_g_2': 5.275,
     'b_group_router_2': 8.0,
     'b_expert_router_2': 8.0}
    for name, (base, spread) in spreads.items():
        noise = np.random.default_rng([zlib.crc32(name.encode()), seed]).standard_normal(out[name].shape)
        drawn = base * np.exp(spread * noise) if base else spread * noise
        out[name] = __import__('jax').numpy.asarray(drawn.astype(out[name].dtype))
    for name, factor in factors.items():
        out[name] = (out[name] * factor).astype(out[name].dtype)
    return out
```

```python
from contextlib import ExitStack

import numpy as np

import concourse.bass as bass
from concourse import mybir

F32 = mybir.dt.float32
F32R = mybir.dt.float32r
I32 = mybir.dt.int32
ALU = mybir.AluOpType
ACT = mybir.ActivationFunctionType
AX = mybir.AxisListType

P = 128
D = 1024
S = 256
NT = S // P
DK = D // P
CHUNK = 64
HEADS = 8
W = 512
UK = 2
UW = UK * W
NSLOT = 4
LEAD = 3
NEG = -1e30
TAKEN = -3e38
EPS = 1e-6
GN_EPS = 1e-5
LAMBDA_INIT = 0.8 - 0.6
DA_HD = 64
QR, KVR, ROPE, NOPE = 384, 256, 64, 128
MLA_QK = NOPE + ROPE
C_W = QR + KVR + ROPE
QKV_W = 3 * D
DFF = 2816
EW = 256
N_FFN = DFF // EW
N_EXP = 16
GROUPS, PER_GROUP = 4, 4
IN2_W = 4296
RQ, RK, RV, RG, DQ, DKV, IQ, IK, IW = 0, 512, 1024, 2048, 3072, 3584, 3712, 4224, 4288
TOPK = 64
N_ARENA = 14736
N_STAT = 300
BUCKETS = 32
REL_W = 384
SC_W = P + S
TWO_PI_PARTS = (6.28125, 0.0019350051879882812, 3.01991598819e-07)
ROUND = 12582912.0
SM_DA, SM_CQ, SM_CKV, SM_LT, SM_B, SM_END = 0, 128, 512, 768, 896, 916
JOBS = [("x1", D, EPS, 2), ("cq", QR, EPS, 2), ("ckv", KVR, EPS, 2)]
JOBS += [(f"da{n}", 2 * DA_HD, EPS, 2) for n in range(HEADS)]
JOBS += [("wo", D, EPS, 4), ("x2", D, EPS, 2), ("ffn", D, EPS, 4), ("u", D, EPS, 2), ("lt", P, EPS, 2)]
JOBS += [(f"ret{n}", 1, GN_EPS, 4) for n in range(HEADS)]
JOBS += [("v", D, EPS, 2), ("fin", D, EPS, 2)]
JOB_NAMES = [j[0] for j in JOBS]
DA_FILL = [(1, 1, 1)] * 6 + [(0, 1, 1)] * 4
MLA_FILL = [1] * 8 + [0, 0]
RET_FILL = [1] * 8 + [0]
IDX_FILL = [1] * 8
TOPK_FILL = 4
DSA_FILL = [1] * 4 + [0] * 6

C_ID, C_DIST, C_COS2, C_SIN2, C_FREQ, C_W4, C_W16, C_END = 0, 128, 512, 576, 640, 672, 676, 692


def shape_constants():
    c = np.zeros((P, C_END), np.float32)
    c[:, C_ID:C_ID + P] = np.eye(P, dtype=np.float32)
    k = np.arange(P)[:, None]
    q = np.arange(S)[None, :]
    d0 = np.abs(q - k).astype(np.float32)
    d0[(k // CHUNK) > (q // CHUNK)] = 1e30
    c[:, C_DIST:C_DIST + S] = d0
    d1 = np.abs(q[:, :P] - k).astype(np.float32)
    d1[(k // CHUNK) > (q[:, :P] // CHUNK)] = 1e30
    c[:, C_DIST + S:C_DIST + SC_W] = d1
    half = np.arange(32, dtype=np.float32)
    f2 = np.power(np.float32(10000.0), -(half * np.float32(2.0)) / np.float32(64)).astype(np.float32)
    for t in range(NT):
        ang = (np.arange(P, dtype=np.float32) + np.float32(t * P))[:, None] * f2[None, :]
        c[:, C_COS2 + 32 * t:C_COS2 + 32 * t + 32] = np.cos(ang.astype(np.float64))
        c[:, C_SIN2 + 32 * t:C_SIN2 + 32 * t + 32] = np.sin(ang.astype(np.float64))
    inv = np.float32(1.0) / np.power(np.float32(10000.0), half * np.float32(2.0 / 64)).astype(np.float32)
    c[:, C_FREQ:C_FREQ + 32] = inv
    c[:, C_W4:C_W4 + 4] = np.arange(4, 0, -1)
    c[:, C_W16:C_W16 + 16] = np.arange(16, 0, -1)
    rel = np.arange(REL_W) - (S - 1)
    nb = BUCKETS // 2
    n = np.abs(rel)
    ex = nb // 2
    nf = np.maximum(n, 1).astype(np.float32)
    large = ex + (np.log(nf / np.float32(ex)) / np.float32(np.log(128 / ex)) * np.float32(nb - ex)).astype(np.int32)
    bucket = (rel > 0) * nb + np.where(n < ex, n, np.minimum(large, nb - 1))
    one_hot = (bucket[None, :] == np.arange(BUCKETS)[:, None]).astype(np.float32)
    return c, one_hot


def plan_blocks():
    order = [(f"in{n}", DK, "act") for n in range(12)]
    order += [(f"uq{n}", QR // P, "act") for n in range(3)]
    order += [(f"ukv{n}", KVR // P, "dve") for n in range(4)]
    order += [(f"{n}", DK, "dve") for n in ("pa0", "pa1", "pb0", "pb1", "wo0", "wo1")]
    order += [("FFN", 6 * N_FFN, None)]
    order += [(f"jn{n}", DK, "act") for n in range(9)]
    order += [(f"gt{n}", DK, "dve") for n in range(4)]
    order += [("ro0", DK, "dve"), ("ro1", DK, "dve"), ("do0", DK // 2, "dve"), ("do1", DK // 2, "dve")]
    order += [("xo0", DK, "dve"), ("xo1", DK, "dve")]
    order += [("MOE", 6 * N_EXP, None)]
    blocks, number, unit, count = {}, 0, 0, {"act": 0, "dve": 0}
    names = []
    for name, nk, engine in order:
        if engine is None:
            blocks[name] = (None, unit, nk, None, None)
            unit += nk
            continue
        units = -(-nk // UK)
        count[engine] += 1
        blocks[name] = (number, unit, units, engine, count[engine])
        names.append(name)
        number += 1
        unit += units
    return blocks, names, unit


def plan_turns():
    order = [(f"x1.{g}", "dve") for g in range(4)]
    order += [(f"qk{h}", "act") for h in range(2)]
    order += [(f"cl.{g}", "dve") for g in range(3)]
    for h in range(HEADS + 2):
        if h + 2 < HEADS:
            order.append((f"qk{h + 2}", "act"))
        if 1 <= h <= HEADS:
            order.append((f"dap{h - 1}", "act"))
        if 2 <= h:
            order.append((f"dao{h - 2}", "dve"))
    order += [(f"oa.{g}", "dve") for g in range(4)]
    order += [(f"mr{g}", "act") for g in range(4)]
    order += [("kr", "act")]
    order += [(f"mq{h}", "act") for h in range(2)]
    for h in range(HEADS + 2):
        if h + 2 < HEADS:
            order.append((f"mq{h + 2}", "act"))
        if 1 <= h <= HEADS:
            order.append((f"mp{h - 1}", "act"))
        if 2 <= h:
            order.append((f"mo{h - 2}", "dve"))
    order += [(f"ob.{g}", "dve") for g in range(4)]
    order += [(f"mg.{g}", "dve") for g in range(4)]
    order += [(f"ad{n}", "act") for n in range(4)]
    order += [(f"x2.{g}", "dve") for g in range(4)]
    order += [(f"ffn{e}", "dve") for e in range(N_FFN)]
    order += [(f"ad{n}", "act") for n in range(4, 10)]
    order += [(f"u.{g}", "dve") for g in range(4)]
    order += [("bv", "act"), ("lt", "act"), ("lat", "act")]
    order += [(f"rt{g}", "act") for g in range(4)]
    order += [(f"dt{g}", "act") for g in range(5)]
    order += [(f"rto{h}", "dve") for h in range(HEADS)]
    order += [(f"re.{g}", "dve") for g in range(4)]
    for h in range(HEADS + 2):
        if 1 <= h <= HEADS:
            order.append((f"dsp{h - 1}", "act"))
        if 2 <= h:
            order.append((f"dso{h - 2}", "dve"))
    order += [(f"de.{g}", "dve") for g in range(2)]
    order += [(f"mh.{g}", "dve") for g in range(4)]
    order += [(f"ad{n}", "act") for n in (10, 11)]
    order += [(f"v.{g}", "dve") for g in range(4)]
    order += [("lg", "dve")]
    order += [(f"moe{e}", "dve") for e in range(N_EXP)]
    turns, count, names = {}, {"act": 0, "dve": 0}, []
    for number, (name, engine) in enumerate(order):
        count[engine] += 1
        turns[name] = (number, engine, count[engine])
        names.append(name)
    return turns, names


BLOCKS, BLOCK_NAMES, N_UNITS = plan_blocks()
TURNS, TURN_NAMES = plan_turns()


class Counted:

    def __init__(self, engine, done):
        self.engine, self.done, self.n, self.shift = engine, done, 0, 0

    def __call__(self, instruction):
        self.mark(instruction)
        self.wait()

    def mark(self, instruction):
        self.n += 1
        instruction.then_inc(self.done, 1)

    def wait(self):
        self.engine.wait_ge(self.done, self.n + self.shift)


def two_blocks(nc, ins, consts, one_hot_d, small_d, lambda_d, router_d, rel_rows, out):
    ctx = ExitStack()
    with ctx:
        def sb(name, shape, dt=F32):
            return ctx.enter_context(nc.sbuf_tensor(name, shape, dt))

        def psum(name, shape):
            return ctx.enter_context(nc.psum_tensor(name, shape, F32))

        def sem(name):
            return ctx.enter_context(nc.semaphore(name))

        raw = sb("raw", [P, NSLOT, UW])
        w_hi = sb("w_hi", [P, NSLOT, UW], F32R)
        w_lo = sb("w_lo", [P, NSLOT, UW], F32R)
        x = sb("x", [P, NT, D])
        a_hi = sb("a_hi", [P, DK, S], F32R)
        a_lo = sb("a_lo", [P, DK, S], F32R)
        b_hi = sb("b_hi", [P, 5, S], F32R)
        b_lo = sb("b_lo", [P, 5, S], F32R)
        c_col = sb("c_col", [P, DK])
        ones = sb("ones", [P, 1])
        mod = sb("mod", [P, 6 * D])
        rows = sb("rows", [P, 4, D])
        cst = sb("cst", [P, C_END])
        small = sb("small", [P, SM_END])
        probs = sb("probs", [P, 2, 2, SC_W])
        mix = sb("mix", [P, SC_W])
        probs_t = sb("probs_t", [P, 2, SC_W])
        dv = sb("dv", [P, NT, 64])
        router = sb("router", [P, DK, 20])
        router_hi = sb("router_hi", [P, DK, 20], F32R)
        router_lo = sb("router_lo", [P, DK, 20], F32R)
        trig = sb("trig", [P, 4, NT, 32])
        stat = sb("stat", [P, N_STAT])
        rel_bias = sb("rel_bias", [BUCKETS, HEADS])
        kv_up = sb("kv_up", [P, P])
        idk_t = sb("idk_t", [P, 2 * S])
        act_junk = idk_t[:, :].bitcast(mybir.dt.bfloat16)
        pos_i = sb("pos_i", [P, NT], I32)
        tmp = sb("tmp", [P, 2, W])
        arena = sb("arena", [P, N_ARENA])

        lin = psum("lin", [P, 4, W])
        turn = psum("turn", [P, 2, W])
        sco = psum("sco", [P, 2, W])

        ident = cst[:, C_ID:C_ID + P]

        def carve(at, *dims):
            n = int(np.prod(dims))
            v = arena[:, at:at + n]
            if len(dims) == 2:
                v = v.rearrange("p (a b) -> p a b", b=dims[1])
            return v, at + n

        xn, _ = carve(0, NT, D)

        qkv, at1 = carve(0, NT, QKV_W)
        qk_t, at2 = carve(at1, HEADS, 2 * S)
        lat, at3 = carve(at2, NT, C_W)
        qb, at4 = carve(at3, NT, HEADS * MLA_QK)
        head_out = qk_t[:, :, 0:S].rearrange("p h (t d) -> p t h d", t=NT)
        kvb = [qkv[:, t, 0:2 * D] for t in range(NT)]
        va = [qkv[:, t, 2 * D:3 * D] for t in range(NT)]
        kr_t = mix[0:ROPE, 0:S]
        qr_t = [va[h // 4][0:ROPE, (h % 4) * S:(h % 4 + 1) * S] for h in range(HEADS)]
        gate1 = mod[:, 2 * D:6 * D].rearrange("p (t n) -> p t n", t=NT)

        zz, bt1 = carve(0, NT, IN2_W)
        rt_t, bt2 = carve(bt1, 4, 2 * S)
        gate2, bt3 = carve(bt2, NT, 2 * D)
        idq_t = mod[:, 0:2 * D].rearrange("p (g n) -> p g n", g=8)
        assert max(at4, bt3) <= N_ARENA
        sel_mask, _ = carve(bt1, SC_W)
        rel_b = [arena[:, bt1 + 512 * (1 + n):bt1 + 512 * (1 + n) + SC_W] for n in range(2)]

        act_s, _ = carve(4096, NT, EW)
        hid, _ = carve(4608, NT, EW)
        y_bank = [[sco[:, 0, :], sco[:, 1, :]], [lin[:, 2, :], lin[:, 3, :]]]

        cols = {}
        for name, n in (("neg_half", 4), ("ms", 4), ("lam", 12), ("pos", 2), ("nmax", 8), ("rsum", 8), ("rinv", 8),
                        ("best", 8), ("bn", 12), ("route", 32), ("gates", 32), ("half_r", 2)):
            at = sum(cols[c][1] for c in cols)
            cols[name] = (at, n)
        ss_at = sum(n for _, n in cols.values())

        def st(name, a=0, n=None):
            at, size = cols[name]
            return stat[:, at + a:at + (size if n is None else a + n)]

        jobs = {}
        at, n_act, n_dve = ss_at, 0, 0
        for name, width, eps, n in JOBS:
            if name.startswith("ret"):
                n_dve += 1
            else:
                n_act += n
            jobs[name] = (len(jobs), at, width, eps, n, n_act, n_dve)
            at += n + 2
        assert at <= N_STAT, at

        logit = arena[:, 5120:5160].rearrange("p (t n) -> p t n", t=NT)
        r_em, r_oh = arena[:, 5160:5192], arena[:, 5192:5224]
        route_y, route_x, r_eq4 = st("route", 8, 2), st("route", 14, 8), st("route", 22, 8)

        def ss(name, a):
            return stat[:, jobs[name][1] + a:jobs[name][1] + a + 1]

        def rstd(name, t):
            at = jobs[name][1] + jobs[name][4] + t
            return stat[:, at:at + 1]

        landed = [sem(f"unit_landed{s}") for s in range(NSLOT)]
        hi_ready = sem("unit_hi_ready")
        lo_ready = sem("unit_lo_ready")
        used = sem("units_used")
        evac = {"act": sem("blocks_evacuated_by_act"), "dve": sem("blocks_evacuated_by_dve")}
        turned = sem("turn_bank_filled")
        freed = {"act": sem("turn_bank_freed_by_act"), "dve": sem("turn_bank_freed_by_dve")}
        turn_hi = sem("turned_hi_ready")
        consts_in = sem("constants_landed")
        x_in = sem("x_landed")
        rows_in = [sem(f"rows{r}_landed") for r in range(3)]
        mod_clear = sem("modulation_rows_cleared")
        bias_in = sem("b_ada_landed")
        ada_in = [sem(f"ada_weights{n}_landed") for n in range(4)]
        ada_done = sem("ada_products_accumulated")
        tables_in = sem("tables_landed")
        one_hot_in = sem("bucket_choice_landed")
        rows_used = sem("gain_rows_used")
        merged = sem("merged_rows_ready")
        dve_ret = sem("retention_rows_ready")
        tanh_ready = sem("gates_tanh_ready")
        sq_act = sem("squares_by_act")
        var_dve = sem("variances_by_dve")
        rstd_ready = sem("rstd_ready")
        silu_c = sem("silu_c_ready")
        half_ready = sem("half_rstd_ready")
        angles = sem("angles_ready")
        sines = sem("sines_ready")
        lam_in = sem("lambda_products_ready")
        lam_exp = sem("lambda_exponentials_ready")
        x_ready = sem("residual_updated")
        xn_ready = sem("normalised_rows_ready")
        lat_ready = sem("normalised_latents_ready")
        roped = sem("rotations_ready")
        scored = sem("attention_scores_ready")
        masked = sem("row_maxima_ready")
        expd = sem("exponentials_ready")
        mixed = sem("row_normalisers_ready")
        copied = sem("biased_scores_ready")
        ret_scored = sem("retention_scores_ready")
        decay = sem("retention_decays_ready")
        decayed = sem("decayed_scores_ready")
        idx_scored = sem("index_scores_ready")
        relud = sem("index_scores_rectified")
        idx_acc = sem("index_scores_summed")
        pairs_ready = sem("doubled_keys_ready")
        bv_in = sem("relative_rows_stored")
        rel_in = [sem(f"relative_tile{n}_landed") for n in range(2)]
        bm_ready = sem("biased_mask_ready")
        mask_ready = sem("selection_ready")
        silud = sem("silu_ready")
        hid_ready = sem("hidden_ready")
        route_hi = sem("router_hi_ready")
        route_lo = sem("router_lo_ready")
        route_in = sem("router_exponents_wanted")
        route_e = sem("router_exponentials_ready")
        dve_step = sem("dve_step")
        act_step = sem("act_step")
        pool_step = sem("pool_step")
        stored = sem("output_stored")

        block = ctx.enter_context(nc.Block())

        def row_source(name):
            v = ins[name]
            return bass.AP(v.tensor, 0, [[0, P], [1, D]])

        def k_tiles(name):
            return ins[name][0].rearrange("(k p) n -> p k n", p=P)

        IN1 = [(n * W, W) for n in range(6)] + [(QKV_W, W), (QKV_W + W, C_W - W)] \
            + [(QKV_W + C_W + n * W, W) for n in range(4)]
        LOADS = {}
        for n in range(12):
            LOADS[f"in{n}"] = ("w_in", *IN1[n], DK)
        for n in range(3):
            LOADS[f"uq{n}"] = ("w_uq", n * W, W, QR // P)
        for n in range(4):
            LOADS[f"ukv{n}"] = ("w_ukv", n * W, W, KVR // P)
            LOADS[f"gt{n}"] = ("w_gate_2", n * W, W, DK)
        for n in range(9):
            LOADS[f"jn{n}"] = ("w_in_2", n * W, min(W, IN2_W - n * W), DK)
        for n in range(2):
            LOADS[f"pa{n}"] = ("w_proj_a", n * W, W, DK)
            LOADS[f"pb{n}"] = ("w_proj_b", n * W, W, DK)
            LOADS[f"wo{n}"] = ("w_o", n * W, W, DK)
            LOADS[f"ro{n}"] = ("w_ret_out_2", n * W, W, DK)
            LOADS[f"do{n}"] = ("w_dsa_out_2", n * W, W, DK // 2)
            LOADS[f"xo{n}"] = ("w_o_2", n * W, W, DK)

        @block.sync
        def _(sp):
            def free_slot(u, shift=0, looped=False):
                if u >= NSLOT or looped:
                    sp.wait_ge(lo_ready, u - NSLOT + 1 + shift)

            def load(name, col=None, shift=0, first=None, looped=False):
                weight, c0, width, nk = LOADS[name]
                u = BLOCKS[name][1] if first is None else first
                src = k_tiles(weight)
                for part in range(-(-nk // UK)):
                    n = min(UK, nk - part * UK)
                    free_slot(u, shift, looped)
                    where = slice(c0, c0 + width) if col is None else bass.ds(col, width)
                    dst = raw[:, u % NSLOT, :].rearrange("p (k n) -> p k n", k=UK)[:, 0:n, 0:width]
                    sp.dma_start(dst, src[:, part * UK:part * UK + n, where]).then_inc(landed[u % NSLOT], 16)
                    u += 1

            def load_slice(u, e, moe, down, shift=0):
                if not down:
                    for half in range(2):
                        for w in ("w_exp_gate_2", "w_exp_up_2") if moe else ("w_ffn_gate", "w_ffn_up"):
                            free_slot(u, shift)
                            if moe:
                                src = ins[w][0, bass.ds(e, 1)].rearrange("e (k p) n -> p (e k) n", p=P)
                                src = src[:, 4 * half:4 * half + 4, :]
                            else:
                                src = k_tiles(w)[:, 4 * half:4 * half + 4, bass.ds(e * EW, EW)]
                            sp.dma_start(raw[:, u % NSLOT, :].rearrange("p (k n) -> p k n", k=4), src)\
                              .then_inc(landed[u % NSLOT], 16)
                            u += 1
                else:
                    for k in range(2):
                        free_slot(u, shift)
                        if moe:
                            src = ins["w_exp_down_2"][0, bass.ds(e, 1)].rearrange("e f n -> (e f) n")
                            src = src[k * P:(k + 1) * P, :]
                        else:
                            src = ins["w_ffn_down"][0, bass.ds(e * EW + k * P, P), :]
                        sp.dma_start(raw[:, u % NSLOT, :], src).then_inc(landed[u % NSLOT], 16)
                        u += 1
                return u

            def load_mlp(name, n, moe):
                u = load_slice(BLOCKS[name][1], 0, moe, False)
                u = load_slice(u, 1, moe, False)
                u = load_slice(u, 0, moe, True)
                pairs = (n - 3) // 2
                with sp.Fori(0, pairs) as i:
                    for j in range(2):
                        load_slice(u + 6 * j, i * 2 + (2 + j), moe, False, i * 12)
                        load_slice(u + 6 * j + 4, i * 2 + (1 + j), moe, True, i * 12)
                u += 12 * pairs
                for e in range(1 + 2 * pairs, n):
                    if e + 1 < n:
                        u = load_slice(u, e + 1, moe, False)
                    u = load_slice(u, e, moe, True)

            sp.dma_start(x[:, :, :], ins["x"][0].rearrange("(t p) n -> p t n", p=P)).then_inc(x_in, 16)
            sp.dma_start(rows[:, 0, :], row_source("ln_mix_pre")).then_inc(rows_in[0], 16)
            load("in0")
            load("in1")
            with sp.Fori(1, 3) as i:
                for j in range(2):
                    load("in0", i * (2 * W) + j * W, i * 8, BLOCKS["in0"][1] + 4 * j, True)
            for name in BLOCK_NAMES[BLOCK_NAMES.index("in6"):BLOCK_NAMES.index("pb1") + 1]:
                load(name)
            sp.dma_start(rows[:, 1, :], row_source("ln_mix_post")).then_inc(rows_in[1], 16)
            sp.wait_ge(ada_done, 2 * DK)
            sp.dma_start(rows[:, 2, :], row_source("ln_ffn_pre")).then_inc(rows_in[2], 16)
            sp.dma_start(rows[:, 3, :], row_source("ln_ffn_post")).then_inc(rows_in[2], 16)
            load("wo0")
            load("wo1")
            load_mlp("FFN", N_FFN, False)
            sp.wait_ge(rows_used, 3)
            sp.dma_start(rows[:, 0, :], row_source("norm_mix_g_2")).then_inc(rows_in[0], 16)
            sp.dma_start(rows[:, 1, :], row_source("ret_gn_g_2")).then_inc(rows_in[1], 16)
            with sp.Fori(0, 4) as i:
                for j in range(2):
                    load("jn0", i * (2 * W) + j * W, i * 8, BLOCKS["jn0"][1] + 4 * j)
            load("jn8")
            sp.wait_ge(rows_used, 4)
            gate_src = bass.AP(ins["b_gate_2"].tensor, 0, [[0, P], [1, 2 * D]])
            sp.dma_start(rows[:, 2:4, :].rearrange("p a n -> p (a n)"), gate_src).then_inc(rows_in[2], 16)
            for n in range(4):
                load(f"gt{n}")
            sp.wait_ge(rows_used, 6)
            sp.dma_start(rows[:, 0, :], row_source("norm_ffn_g_2")).then_inc(rows_in[0], 16)
            sp.dma_start(rows[:, 1, :], row_source("norm_final_g_2")).then_inc(rows_in[1], 16)
            for name in ("ro0", "ro1", "do0", "do1", "xo0", "xo1"):
                load(name)
            load_mlp("MOE", N_EXP, True)
            out_d = out[0].rearrange("(t p) n -> p t n", p=P)
            for t in range(NT):
                sp.wait_ge(xn_ready, 4 + t + 1)
                sp.dma_start(out_d[:, t, :], xn[:, t, :]).then_inc(stored, 16)
            sp.wait_ge(stored, 16 * NT)

        def ada_slots(g):
            return [rows[:, 2, :], rows[:, 3, :]] if g < 2 else [carve(5632 + n * D, D)[0] for n in range(4)]

        @block.gpsimd
        def _(pool):
            pool.dma_start(cst[:, :], consts).then_inc(tables_in, 16)
            with nc.allow_non_contiguous_dma(reason="a column a K tile, a position a partition"):
                pool.dma_start(probs[:, 0, 0, 0:DK], ins["c_2"].rearrange("a (k p) -> p (a k)", p=P))\
                    .then_inc(consts_in, 16)
                pool.dma_start(pos_i[:, :], ins["positions"].rearrange("a (t p) -> p (a t)", p=P))\
                    .then_inc(consts_in, 16)
            pool.dma_start(small[:, :], bass.AP(small_d.tensor, 0, [[0, P], [1, SM_END]])).then_inc(consts_in, 16)
            pool.dma_start(probs[:, 1, 0, 0:S], bass.AP(lambda_d.tensor, 0, [[0, P], [1, S]])).then_inc(consts_in, 16)
            pool.dma_start(router[:, :, :], router_d.rearrange("(k p) n -> p k n", p=P)).then_inc(consts_in, 16)
            pool.dma_start(rel_bias[:, :], ins["rel_bias_2"]).then_inc(consts_in, 16)
            pool.dma_start(kv_up[:, :], ins["w_dsa_kv_up_2"][0]).then_inc(consts_in, 16)
            step = Counted(pool, pool_step)
            step(pool.memset(st("neg_half"), -0.5))
            pool.memset(ones[:, :], 1.0).then_inc(mod_clear, 1)

            def clear_rows(n, c):
                pool.memset(mod[:, c], 0.0).then_inc(mod_clear, 1)
                pool.wait_ge(mod_clear, n)
                pool.dma_start(mod[0:1, c], ins["b_ada_2"][:, c]).then_inc(bias_in, 16)
                pool.wait_ge(bias_in, 16 * (n - 1))

            def ada_source(k, c):
                return ins["w_ada_2"][0, k * P:(k + 1) * P, c]

            def norm_job(name):
                number, at, width, eps, n, n_act, n_dve = jobs[name]
                source = stat[:, at:at + 2]
                if name.startswith("ret"):
                    pool.wait_ge(var_dve, n_dve)
                    source = stat[:, at + 1:at + 4:2]
                else:
                    pool.wait_ge(sq_act, n_act)
                    if n == 4:
                        step(pool.tensor_tensor(st("ms", 2, 2), stat[:, at:at + 4:2], stat[:, at + 1:at + 4:2],
                                                ALU.add))
                        source = st("ms", 2, 2)
                step(pool.tensor_scalar(st("ms", 0, 2), source, 1.0 / width, eps, ALU.mult, ALU.add))
                pool.tensor_tensor(stat[:, at + n:at + n + 2], st("ms", 0, 2), st("neg_half", 0, 2), ALU.pow)\
                    .then_inc(rstd_ready, 1)
                pool.wait_ge(rstd_ready, number + 1)

            def norm_jobs(first, last):
                for name in JOB_NAMES[JOB_NAMES.index(first):JOB_NAMES.index(last) + 1]:
                    norm_job(name)

            norm_jobs("x1", "x1")
            pool.tensor_scalar(st("half_r"), stat[:, jobs["x1"][1] + 2:jobs["x1"][1] + 4], 0.5, None, ALU.mult)\
                .then_inc(half_ready, 1)
            clear_rows(2, slice(0, 2 * D))
            for n in range(2 * DK):
                if n >= 2:
                    pool.wait_ge(ada_done, n - 1)
                pool.dma_start(ada_slots(0)[n % 2], ada_source(n % DK, slice(n // DK * D, (n // DK + 1) * D)))\
                    .then_inc(ada_in[n % 2], 16)
            norm_jobs("cq", "x2")
            pool.wait_ge(turned, TURNS["mg.3"][0] + 1)
            clear_rows(3, slice(2 * D, 6 * D))
            with pool.Fori(0, 4) as i:
                for k in range(DK):
                    pool.wait_ge(ada_done, i * DK + (2 * DK + k - 3))
                    pool.dma_start(ada_slots(2)[k % 4], ada_source(k, bass.ds(i * D + 2 * D, D)))\
                        .then_inc(ada_in[k % 4], 16)
            pool.dma_start(mix[0:BUCKETS, :], one_hot_d).then_inc(one_hot_in, 16)
            norm_jobs("ffn", "u")
            pool.wait_ge(freed["act"], TURNS["bv"][2])
            row = probs[0:HEADS, 1, 0, :]
            pool.dma_start(rel_rows, bass.AP(row.tensor, row.offset, [row.ap[0], [0, P], row.ap[1]])).then_inc(bv_in, 16)
            norm_jobs("lt", "ret7")
            pool.wait_ge(bv_in, 16)

            def load_rel(h):
                n = h % 2
                b0 = bass.AP(rel_rows.tensor, h * P * REL_W + S - 1, [[REL_W - 1, P], [1, P]])
                b1 = bass.AP(rel_rows.tensor, h * P * REL_W + P - 1, [[REL_W - 1, P], [1, S]])
                pool.dma_start(rel_b[n][:, 0:P], b0).then_inc(rel_in[n], 16)
                pool.dma_start(rel_b[n][:, P:SC_W], b1).then_inc(rel_in[n], 16)

            load_rel(0)
            load_rel(1)
            pool.wait_ge(mask_ready, 1)
            for h in range(HEADS):
                pool.wait_ge(rel_in[h % 2], 32 * (h // 2 + 1))
                if h >= 2:
                    pool.wait_ge(copied, h - 1)
                pool.tensor_tensor(probs[:, h % 2, 1, :], rel_b[h % 2], sel_mask, ALU.add).then_inc(bm_ready, 1)
                if h + 2 < HEADS:
                    pool.wait_ge(bm_ready, h + 1)
                    load_rel(h + 2)
            norm_jobs("v", "fin")

        @block.scalar
        def _(act):
            split_at = [0]
            unit_at = [0]
            sq_at = [0]

            def split(u, shift=0, looped=False):
                s = u % NSLOT
                act.wait_ge(landed[s], 16 * (u // NSLOT + 1) + shift * 4)
                if u >= NSLOT or looped:
                    act.wait_ge(used, u - NSLOT + 1 + shift)
                act.activation(w_hi[:, s, :], raw[:, s, :], ACT.Copy).then_inc(hi_ready, 1)

            def split_to(n):
                while split_at[0] < min(n, N_UNITS):
                    split(split_at[0])
                    split_at[0] += 1

            def fill(n, until=None):
                end = unit_at[0] + n if until is None else BLOCKS[until][1] + BLOCKS[until][2]
                while unit_at[0] < end:
                    split_to(unit_at[0] + LEAD + 1)
                    unit_at[0] += 1
                    for name in BLOCK_NAMES:
                        if BLOCKS[name][1] + BLOCKS[name][2] == unit_at[0]:
                            if BLOCKS[name][3] == "act":
                                evacuate(name)
                            elif name[:2] == "gt":
                                gate_tanh(name)

            def evacuate(name):
                number, u0, units, _, _ = BLOCKS[name]
                act.wait_ge(used, u0 + units)
                bank = 2 * (number % 2)
                kind, n = name[:2], int(name[2:])
                for t in range(NT):
                    if kind == "in" and n >= 8:
                        c = (n - 8) * W
                        i = act.activation(gate1[:, t, c:c + W], lin[:, bank + t, :], ACT.Tanh,
                                           scale=st("half_r", t, 1))
                    elif kind == "in":
                        c, w = (n - 6) * W, IN1[n][1]
                        i = act.activation(lat[:, t, c:c + w], lin[:, bank + t, 0:w], ACT.Copy, scale=rstd("x1", t))
                    elif kind == "uq":
                        i = act.activation(qb[:, t, n * W:(n + 1) * W], lin[:, bank + t, :], ACT.Copy)
                    else:
                        w = LOADS[name][2]
                        i = act.activation(zz[:, t, n * W:n * W + w], lin[:, bank + t, 0:w], ACT.Copy)
                i.then_inc(evac["act"], 1)

            def gate_tanh(name):
                n = int(name[2:])
                act.wait_ge(evac["dve"], BLOCKS[name][4])
                g = gate2[:, :, n * W:(n + 1) * W]
                act.activation(g, g, ACT.Tanh, scale=0.5).then_inc(tanh_ready, 1)

            def block_loop(first, pairs, target, scale=lambda t: 1.0):
                number, u0, units, _, _ = BLOCKS[first]
                assert split_at[0] == u0 + LEAD and unit_at[0] == u0

                def pair(i, looped):
                    for j in range(2):
                        for k in range(4):
                            split(u0 + LEAD + 4 * j + k, i * 8, looped)
                        act.wait_ge(used, i * 8 + (u0 + 4 * j + 4))
                        act.nop()
                        bank = 2 * ((number + j) % 2)
                        for t in range(NT):
                            e = act.activation(target[:, t, bass.ds(i * (2 * W) + j * W, W)],
                                               lin[:, bank + t, :], ACT.Copy, scale=scale(t))
                        e.then_inc(evac["act"], 1)

                pair(0, False)
                with act.Fori(1, pairs) as i:
                    pair(i, True)
                split_at[0] += 8 * pairs
                unit_at[0] += 8 * pairs

            def bank_of(name):
                return turn[:, TURNS[name][0] % 2, :]

            def turned_hi(name, hi, k0, nk, scale=1.0):
                act.wait_ge(turned, TURNS[name][0] + 1)
                src = bank_of(name)[:, 0:nk * S].rearrange("p (k n) -> p k n", k=nk)
                act.activation(hi[:, k0:k0 + nk, :], src, ACT.Copy, scale=scale).then_inc(turn_hi, 1)

            def turned_copy(name, targets):
                act.wait_ge(turned, TURNS[name][0] + 1)
                for dst, src, scale in targets:
                    i = act.activation(dst, src, ACT.Copy, scale=scale)
                i.then_inc(freed["act"], 1)

            def squares(name, sources):
                for a, src in enumerate(sources):
                    n = src.shape[-1]
                    if sq_at[0]:
                        act.wait_ge(sq_act, sq_at[0])
                    sq_at[0] += 1
                    act.activation(act_junk[:, 0:n], src, ACT.Square, accum_out=ss(name, a)).then_inc(sq_act, 1)

            def exps(n, comps):
                act.wait_ge(masked, n + 1)
                if n >= 2:
                    act.wait_ge(mixed, n - 1)
                for j in range(comps):
                    for t in range(NT):
                        c = slice(0, P) if t == 0 else slice(P, SC_W)
                        k = 4 * (n % 2) + 2 * t + j
                        dst = probs[:, n % 2, j, c]
                        if comps == 2:
                            src = sco[:, j, c]
                        elif n < 2 * HEADS:
                            src = sco[:, n % 2, c]
                        else:
                            src = dst
                        i = act.activation(dst, src, ACT.Exp, bias=st("nmax", k, 1), accum_out=st("rsum", k, 1))
                i.then_inc(expd, 1)

            def probs_out(name, i, before):
                if i >= 2:
                    act.wait_ge(turned, TURNS[f"{before}{i - 2}"][0] + 1)
                turned_copy(name, [(probs_t[:, i % 2, :], bank_of(name)[:, 0:SC_W], 1.0)])

            split_to(LEAD)
            act.wait_ge(x_in, 16)
            squares("x1", [x[:, t, :] for t in range(NT)])
            for g in range(4):
                turned_hi(f"x1.{g}", a_hi, 2 * g, 2)
            act.wait_ge(consts_in, 112)
            act.activation(c_col[:, :], probs[:, 0, 0, 0:DK], ACT.Silu).then_inc(silu_c, 1)
            act.activation(router_hi[:, :, :], router[:, :, :], ACT.Copy).then_inc(route_hi, 1)
            act.wait_ge(angles, 1)
            act.activation(trig[:, 0:2, :, :].rearrange("p a t n -> p (a t n)"), mix[:, 0:P], ACT.Sin)\
                .then_inc(sines, 1)
            act.wait_ge(lam_in, 1)
            act.activation(st("lam", 2, 2), st("lam", 0, 2), ACT.Exp).then_inc(lam_exp, 1)
            act.wait_ge(rstd_ready, 1)
            act.wait_ge(half_ready, 1)
            block_loop("in0", 3, qkv, lambda t: rstd("x1", t))
            fill(0, "in7")
            squares("cq", [lat[:, t, 0:QR] for t in range(NT)])
            squares("ckv", [lat[:, t, QR:QR + KVR] for t in range(NT)])

            def q_and_k_out(name, h, scale):
                b = bank_of(name)
                turned_copy(name, [(qk_t[:, h, 0:S], b[:, 0:S], scale), (qk_t[:, h, S:2 * S], b[:, S:2 * S], 1.0)])

            q_and_k_out("qk0", 0, DA_HD ** -0.5)
            q_and_k_out("qk1", 1, DA_HD ** -0.5)
            turned_hi("cl.0", b_hi, 0, 2)
            turned_hi("cl.1", b_hi, 2, 2)
            turned_hi("cl.2", b_hi, 4, 1)
            for i in range(HEADS + 2):
                if i + 2 < HEADS:
                    q_and_k_out(f"qk{i + 2}", i + 2, DA_HD ** -0.5)
                fill(DA_FILL[i][0])
                if i < HEADS:
                    exps(i, 2)
                fill(DA_FILL[i][1])
                if 1 <= i <= HEADS:
                    probs_out(f"dap{i - 1}", i - 1, "dao")
                if i >= 2:
                    act.wait_ge(turned, TURNS[f"dao{i - 2}"][0] + 1)
                    squares(f"da{i - 2}", [bank_of(f"dao{i - 2}")[:, P * t:P * t + P] for t in range(NT)])
                fill(DA_FILL[i][2])
            for g in range(4):
                turned_hi(f"oa.{g}", a_hi, 2 * g, 2)

            scale = MLA_QK ** -0.5
            for g in range(4):
                b = bank_of(f"mr{g}")
                turned_copy(f"mr{g}", [(qr_t[2 * g + a], b[0:ROPE, a * S:(a + 1) * S], scale) for a in range(2)])
            turned_copy("kr", [(kr_t, bank_of("kr")[0:ROPE, 0:S], 1.0)])
            q_and_k_out("mq0", 0, scale)
            q_and_k_out("mq1", 1, scale)
            for i in range(HEADS + 2):
                if i + 2 < HEADS:
                    q_and_k_out(f"mq{i + 2}", i + 2, scale)
                if i < HEADS:
                    exps(HEADS + i, 1)
                fill(MLA_FILL[i])
                if 1 <= i <= HEADS:
                    probs_out(f"mp{i - 1}", i - 1, "mo")
            for g in range(4):
                turned_hi(f"ob.{g}", a_hi, 2 * g, 2)
            fill(0, "pb1")
            for g in range(4):
                turned_hi(f"mg.{g}", a_hi, 2 * g, 2, 0.5)
            fill(0, "wo1")
            act.wait_ge(used, BLOCKS["wo1"][1] + 4)
            banks = [2 * (BLOCKS[f"wo{n}"][0] % 2) for n in range(2)]
            squares("wo", [lin[:, b + t, :] for t in range(NT) for b in banks])

            def ada_out(n0, n1):
                for n in range(n0, n1):
                    turned_copy(f"ad{n}", [(mod[:, n * W:(n + 1) * W], bank_of(f"ad{n}"), 1.0)])

            ada_out(0, 4)
            for g in range(4):
                turned_hi(f"x2.{g}", a_hi, 2 * g, 2)
            act.wait_ge(x_ready, 1)
            squares("x2", [x[:, t, :] for t in range(NT)])

            def silu_step(scale, u_end, shift=0):
                act.wait_ge(used, u_end + shift)
                for t in range(NT):
                    act.activation(act_s[:, t, :], lin[:, t, 0:EW], ACT.Silu, scale=scale(t)).then_inc(silud, 1)

            def mlp(name, label, n, scale=lambda t: 1.0):
                u = BLOCKS[name][1]
                turn0 = TURNS[f"{label}0"][0]
                assert split_at[0] == u + LEAD
                split_to(u + 6)
                silu_step(scale, u + 4)
                split_to(u + 4 + LEAD)
                u += 4

                def one(e, u, last=False, shift=0, shift_e=0):
                    act.wait_ge(turned, turn0 + e + 1 + shift_e)
                    act.activation(b_hi[:, 0:2, :], turn[:, 0, :].rearrange("p (k n) -> p k n", k=2), ACT.Copy)\
                        .then_inc(turn_hi, 1)
                    n_units = 2 if last else 6
                    for j in range(n_units):
                        if j == 3:
                            silu_step(scale, u + 4, shift)
                        if u + LEAD + j < N_UNITS:
                            split(u + LEAD + j, shift)

                one(0, u)
                u += 6
                pairs = (n - 3) // 2
                with act.Fori(0, pairs) as i:
                    for j in range(2):
                        one(1 + j, u + 6 * j, False, i * 12, i * 2)
                u += 12 * pairs
                for e in range(1 + 2 * pairs, n):
                    one(e, u, e == n - 1)
                    u += 2 if e == n - 1 else 6
                split_at[0] = u + LEAD
                unit_at[0] = u

            act.wait_ge(rstd_ready, jobs["x2"][0] + 1)
            mlp("FFN", "ffn", N_FFN, lambda t: rstd("x2", t))
            act.wait_ge(used, BLOCKS["FFN"][1] + 6 * N_FFN)
            squares("ffn", [y_bank[t][n] for t in range(NT) for n in range(2)])
            ada_out(4, 6)
            act.wait_ge(x_ready, 2)
            squares("u", [x[:, t, :] for t in range(NT)])
            ada_out(6, 10)
            for g in range(4):
                turned_hi(f"u.{g}", a_hi, 2 * g, 2)

            turned_copy("bv", [(probs[0:HEADS, 1, 0, :], bank_of("bv")[0:HEADS, 0:SC_W], 1.0)])
            block_loop("jn0", 4, zz)
            fill(0, "jn8")
            squares("lt", [zz[:, t, DKV:DKV + P] for t in range(NT)])
            for t in range(NT):
                act.activation(gate2[:, t, 0:D], zz[:, t, RG:RG + D], ACT.Tanh, scale=0.5).then_inc(tanh_ready, 1)
            turned_copy("lt", [(idk_t[:, 0:S], bank_of("lt")[:, 0:S], 1.0)])
            b = bank_of("lat")[:, 0:S].rearrange("p (t n) -> p t n", t=NT)
            turned_copy("lat", [(zz[:, :, DKV:DKV + 64], b[:, :, 0:64], 1.0),
                                (zz[:, :, DKV + 64:DKV + 128], b[:, :, 0:64], 1.0),
                                (probs_t[:, :, 0:64], zz[:, :, IK:IK + 64], 1.0),
                                (probs_t[:, :, 64:128], zz[:, :, IK:IK + 64], 1.0),
                                (dv[:, :, :], b[:, :, 64:128], 1.0)])
            for g in range(4):
                turned_copy(f"rt{g}", [(rt_t[:, g, :], bank_of(f"rt{g}"), 1.0)])
            for g in range(5):
                name = f"dt{g}"
                dst = idk_t[:, :] if g == 4 else idq_t[:, 2 * g:2 * g + 2, :].rearrange("p a n -> p (a n)")
                turned_copy(name, [(dst, bank_of(name), 1.0)])

            pool_rows = 16
            act.wait_ge(bv_in, pool_rows)
            for i in range(HEADS + 1):
                if i < HEADS:
                    if i >= 2:
                        act.wait_ge(decayed, i - 1)
                    g = float(np.log(np.float32(1.0 - 2.0 ** (-5.0 - i))))
                    act.activation(probs[:, i % 2, 0, :], cst[:, C_DIST:C_DIST + SC_W], ACT.Exp, scale=g)\
                        .then_inc(decay, 1)
                fill(RET_FILL[i])
            act.wait_ge(decayed, HEADS)
            for i in range(HEADS):
                act.wait_ge(idx_scored, i + 1)
                if i >= 2:
                    act.wait_ge(idx_acc, i - 1)
                act.activation(probs[:, i % 2, 0, :], sco[:, i % 2, 0:SC_W], ACT.Relu).then_inc(relud, 1)
                fill(IDX_FILL[i])
            for g in range(4):
                turned_hi(f"re.{g}", a_hi, 2 * g, 2)
            fill(TOPK_FILL)
            for i in range(HEADS + 2):
                fill(DSA_FILL[i])
                if i < HEADS:
                    exps(2 * HEADS + i, 1)
                if 1 <= i <= HEADS:
                    probs_out(f"dsp{i - 1}", i - 1, "dso")
            turned_hi("de.0", b_hi, 0, 2)
            turned_hi("de.1", b_hi, 2, 2)
            fill(0, "do1")
            for g in range(4):
                turned_hi(f"mh.{g}", a_hi, 2 * g, 2, 0.5)
            fill(0, "xo1")
            act.wait_ge(x_ready, 3)
            squares("v", [x[:, t, :] for t in range(NT)])
            ada_out(10, 12)
            for g in range(4):
                turned_hi(f"v.{g}", a_hi, 2 * g, 2)
            act.wait_ge(route_in, 1)
            act.activation(route_x, route_x, ACT.Exp).then_inc(route_e, 1)
            act.wait_ge(route_in, 2)
            act.activation(route_y, route_y, ACT.Exp).then_inc(route_e, 1)
            mlp("MOE", "moe", N_EXP)
            act.wait_ge(x_ready, 4)
            squares("fin", [x[:, t, :] for t in range(NT)])

        @block.vector
        def _(dve):
            split_at = [0]
            unit_at = [0]
            step = Counted(dve, dve_step)

            def split(u, shift=0):
                s = u % NSLOT
                dve.wait_ge(hi_ready, u + 1 + shift)
                dve.tensor_tensor(w_lo[:, s, :], raw[:, s, :], w_hi[:, s, :].bitcast(F32), ALU.subtract)\
                   .then_inc(lo_ready, 1)

            def split_to(n):
                while split_at[0] < min(n, N_UNITS):
                    split(split_at[0])
                    split_at[0] += 1

            def fill(n, until=None):
                end = unit_at[0] + n if until is None else BLOCKS[until][1] + BLOCKS[until][2]
                while unit_at[0] < end:
                    split_to(unit_at[0] + LEAD + 1)
                    unit_at[0] += 1
                    for name in BLOCK_NAMES:
                        if BLOCKS[name][1] + BLOCKS[name][2] == unit_at[0] and BLOCKS[name][3] == "dve":
                            evacuate(name)

            def evacuate(name):
                number, u0, units, _, _ = BLOCKS[name]
                dve.wait_ge(used, u0 + units)
                bank = 2 * (number % 2)
                kind = name.rstrip("0123456789")
                n = int(name[len(kind):])
                c = slice(n * W, (n + 1) * W)
                done = evac["dve"]
                if kind == "ukv":
                    for t in range(NT):
                        i = dve.tensor_copy(kvb[t][:, c], lin[:, bank + t, :])
                    i.then_inc(done, 1)
                elif kind == "gt":
                    dve.wait_ge(rows_in[2], 48)
                    bias = rows[:, 2 + n // 2, (n % 2) * W:(n % 2) * W + W]
                    for t in range(NT):
                        i = dve.tensor_tensor(gate2[:, t, c], lin[:, bank + t, :], bias, ALU.add)
                    i.then_inc(done, 1)
                elif kind in ("pa", "ro"):
                    gate = gate1 if kind == "pa" else gate2
                    if kind == "ro":
                        dve.wait_ge(tanh_ready, NT + 4)
                    for t in range(NT):
                        i = dve.scalar_tensor_tensor(out=gate[:, t, c], in0=gate[:, t, c], scalar=1.0,
                                                     in1=lin[:, bank + t, :], op0=ALU.add, op1=ALU.mult)
                    i.then_inc(done, 1)
                elif kind in ("pb", "do"):
                    gate = gate1 if kind == "pb" else gate2
                    cb = slice(D + n * W, D + (n + 1) * W)
                    for t in range(NT):
                        i = dve.scalar_tensor_tensor(out=gate[:, t, cb], in0=gate[:, t, cb], scalar=1.0,
                                                     in1=lin[:, bank + t, :], op0=ALU.add, op1=ALU.mult)
                    i.then_inc(done, 1)
                    dve.wait_ge(done, BLOCKS[name][4])
                    for t in range(NT):
                        dve.tensor_tensor(gate[:, t, c], gate[:, t, c], gate[:, t, cb], ALU.add).then_inc(merged, 1)
                elif kind == "wo":
                    pass
                else:
                    dve.wait_ge(freed["act"], TURNS["ad5"][2])
                    for t in range(NT):
                        dve.tensor_tensor(tmp[:, t, :], lin[:, bank + t, :],
                                          mod[:, 2 * D + n * W:2 * D + (n + 1) * W], ALU.mult).then_inc(dve_step, 1)
                        step.n += 1
                    step.wait()
                    for t in range(NT):
                        i = dve.tensor_tensor(x[:, t, c], x[:, t, c], tmp[:, t, :], ALU.add)
                        if t == NT - 1:
                            i.then_inc(done, 1)
                    if n == 1:
                        dve.wait_ge(done, BLOCKS[name][4])
                        dve.nop().then_inc(x_ready, 1)

            def ada_part(g0, i, k):
                slots = ada_slots(g0)
                n_s = len(slots)
                before = 16 * DK if g0 and k % n_s < 2 else 0
                dve.wait_ge(ada_in[k % n_s], i * (16 * DK // n_s) + (before + 16 * (k // n_s + 1)))
                if k:
                    dve.wait_ge(ada_done, i * DK + (g0 * DK + k))
                acc = mod[:, bass.ds(i * D + g0 * D, D)]
                dve.scalar_tensor_tensor(out=acc, in0=slots[k % n_s], scalar=c_col[:, k:k + 1], in1=acc,
                                         op0=ALU.mult, op1=ALU.add).then_inc(ada_done, 1)

            def block_loop(first, pairs, beside=None):
                u0 = BLOCKS[first][1]
                assert split_at[0] == u0 + LEAD and unit_at[0] == u0
                for k in range(8):
                    split(u0 + LEAD + k)
                with dve.Fori(1, pairs) as i:
                    for k in range(8):
                        split(u0 + LEAD + k, i * 8)
                        if beside is not None:
                            beside(i - 1, k)
                split_at[0] += 8 * pairs
                unit_at[0] += 8 * pairs

            def bank_of(name):
                return turn[:, TURNS[name][0] % 2, :]

            turn_pairs = [0]

            def turned_lo(name, hi, lo, k0, nk, scale=None):
                turn_pairs[0] += 1
                dve.wait_ge(turn_hi, turn_pairs[0])
                src = bank_of(name)[:, 0:nk * S].rearrange("p (k n) -> p k n", k=nk)
                up = hi[:, k0:k0 + nk, :].bitcast(F32)
                if scale is None:
                    i = dve.tensor_tensor(lo[:, k0:k0 + nk, :], src, up, ALU.subtract)
                else:
                    flat = "p k n -> p (k n)"
                    i = dve.scalar_tensor_tensor(out=lo[:, k0:k0 + nk, :].rearrange(flat), in0=src.rearrange(flat),
                                                 scalar=scale, in1=up.rearrange(flat), op0=ALU.mult,
                                                 op1=ALU.subtract)
                i.then_inc(freed["dve"], 1)

            def wait_norm(name):
                dve.wait_ge(rstd_ready, jobs[name][0] + 1)

            def rotate(v, t, cos, sin, nsin, groups):
                def over(table, *dims):
                    return bass.AP(table.tensor, table.offset, [table.ap[0]] + [[0, n] for n in dims] + [[1, 32]])
                n = groups * 64
                by_cos = tmp[:, 0, 0:n].rearrange("p (g a n) -> p g a n", g=groups, a=2)
                by_sin = tmp[:, 1, 0:n].rearrange("p (g a n) -> p g a n", g=groups, a=2)
                dve.tensor_tensor(by_cos, v, over(cos, groups, 2), ALU.mult)
                dve.tensor_tensor(by_sin[:, :, 0, :], v[:, :, 1, :], over(nsin, groups), ALU.mult)
                step(dve.tensor_tensor(by_sin[:, :, 1, :], v[:, :, 0, :], over(sin, groups), ALU.mult))
                step(dve.tensor_tensor(v, by_cos, by_sin, ALU.add))

            def rotate1(v, t, groups):
                rotate(v, t, trig[:, 0, t, :], trig[:, 1, t, :], trig[:, 2, t, :], groups)

            def row_maxima(n, comps):
                dve.wait_ge(scored, n + 1)
                b = slice(0, 2) if comps == 2 else slice(n % 2, n % 2 + 1)
                late = sco[0:CHUNK, b, :].rearrange("p j (b c) -> p j b c", c=S)[:, :, :, CHUNK:P]
                step(dve.memset(late, NEG))
                maxima(n, comps, sco[:, b, 0:SC_W])

            def maxima(n, comps, s):
                k = 4 * (n % 2)
                for t in range(NT):
                    c = slice(0, P) if t == 0 else slice(P, SC_W)
                    i = dve.tensor_reduce(st("nmax", k + 2 * t, comps), s[:, :, c], AX.X, ALU.max, negate=True)
                i.then_inc(masked, 1)

            def head_scaled(name, n, dst, width):
                dve.wait_ge(mixed, n + 1)
                dve.wait_ge(turned, TURNS[name][0] + 1)
                b = bank_of(name)
                for t in range(NT):
                    i = dve.tensor_scalar(dst(t), b[:, width * t:width * t + width],
                                          st("rinv", 4 * (n % 2) + 2 * t, 1), None, ALU.mult)
                i.then_inc(freed["dve"], 1)
                dve.wait_ge(freed["dve"], TURNS[name][2])

            def row_sums(n):
                dve.wait_ge(expd, n + 1)
                k = 4 * (n % 2)
                dve.reciprocal(st("rinv", k, 4)[:, 0:4:2], st("rsum", k, 4)[:, 0:4:2]).then_inc(mixed, 1)

            def gained(gain):
                for t in range(NT):
                    i = dve.tensor_tensor(xn[:, t, :], x[:, t, :], gain, ALU.mult)
                return i

            def normalise(name, gain, shift):
                wait_norm(name)
                for t in range(NT):
                    step.mark(dve.scalar_tensor_tensor(out=xn[:, t, :], in0=x[:, t, :], scalar=rstd(name, t), in1=gain,
                                                       op0=ALU.mult, op1=ALU.mult))
                step.wait()
                for t in range(NT):
                    i = dve.tensor_tensor(xn[:, t, :], xn[:, t, :], shift, ALU.add)
                return i

            def add_normed(name, parts, gain):
                wait_norm(name)
                for n in range(2):
                    c = slice(n * W, (n + 1) * W)
                    for t in range(NT):
                        step.mark(dve.scalar_tensor_tensor(out=tmp[:, t, :], in0=parts[t][n], scalar=rstd(name, t),
                                                           in1=gain[:, c], op0=ALU.mult, op1=ALU.mult))
                    step.wait()
                    for t in range(NT):
                        i = dve.tensor_tensor(x[:, t, c], x[:, t, c], tmp[:, t, :], ALU.add)
                        step.mark(i)
                    step.wait()

            dve.wait_ge(rows_in[0], 16)
            dve.wait_ge(x_in, 16)
            gained(rows[:, 0, :]).then_inc(xn_ready, 1)
            dve.wait_ge(xn_ready, 1)
            dve.nop().then_inc(rows_used, 1)
            split_to(2)
            for g in range(4):
                turned_lo(f"x1.{g}", a_hi, a_lo, 2 * g, 2)
            split_to(LEAD)
            dve.wait_ge(tables_in, 16)
            dve.wait_ge(consts_in, 112)
            step(dve.tensor_copy(st("pos"), pos_i[:, :]))
            half, two, whole = mix[:, 0:64], mix[:, 64:128], mix[:, 0:128]
            kmul = tmp[:, 0, 0:P]
            for t in range(NT):
                for a in range(2):
                    step.mark(dve.tensor_scalar(mix[:, 64 * a + 32 * t:64 * a + 32 * t + 32],
                                                cst[:, C_FREQ:C_FREQ + 32], st("pos", t, 1), None, ALU.mult))
            step.wait()
            step.mark(dve.tensor_scalar(kmul[:, 0:64], half, 1.0 / (2 * np.pi), 0.25, ALU.mult, ALU.add))
            step.mark(dve.tensor_scalar(kmul[:, 64:128], two, 1.0 / (2 * np.pi), None, ALU.mult))
            step.wait()
            step(dve.tensor_scalar(kmul, kmul, ROUND, None, ALU.add))
            step(dve.tensor_scalar(kmul, kmul, ROUND, None, ALU.subtract))
            for part in TWO_PI_PARTS:
                step(dve.scalar_tensor_tensor(out=whole, in0=kmul, scalar=-part, in1=whole, op0=ALU.mult,
                                              op1=ALU.add))
            step(dve.tensor_scalar(half, half, float(np.float32(np.pi / 2)), None, ALU.add))
            dve.tensor_scalar(whole, whole, 3.1415925, -3.1415925, ALU.min, ALU.max).then_inc(angles, 1)
            for a in range(2):
                lq, lk = (probs[:, 1, 0, 128 * a + 64 * b:128 * a + 64 * b + 64] for b in range(2))
                step(dve.tensor_tensor(tmp[:, 1, 0:64], lq, lk, ALU.mult))
                i = dve.tensor_reduce(st("lam", a, 1), tmp[:, 1, 0:64], AX.X, ALU.add)
                if a == 0:
                    step(i)
                else:
                    i.then_inc(lam_in, 1)
            dve.wait_ge(route_hi, 1)
            dve.tensor_tensor(router_lo[:, :, :], router[:, :, :], router_hi[:, :, :].bitcast(F32), ALU.subtract)\
               .then_inc(route_lo, 1)
            dve.wait_ge(sines, 1)
            step(dve.tensor_scalar(trig[:, 2, :, :], trig[:, 1, :, :], -1.0, None, ALU.mult))
            cst_sin2 = cst[:, C_SIN2:C_SIN2 + 64].rearrange("p (t n) -> p t n", t=NT)
            step(dve.tensor_scalar(trig[:, 3, :, :], cst_sin2, -1.0, None, ALU.mult))
            dve.wait_ge(lam_exp, 1)
            step(dve.tensor_tensor(st("lam", 4, 1), st("lam", 3, 1), st("lam", 2, 1), ALU.subtract))
            step(dve.tensor_scalar(st("lam", 5, 1), st("lam", 4, 1), -LAMBDA_INIT, None, ALU.add))
            step(dve.tensor_scalar(small[:, SM_DA:SM_DA + P], small[:, SM_DA:SM_DA + P], 1.0 - LAMBDA_INIT, None,
                                   ALU.mult))
            dve.wait_ge(silu_c, 1)
            dve.wait_ge(bias_in, 16)
            block_loop("in0", 3, lambda i, k: ada_part(0, i, k))

            for n in range(4):
                dve.wait_ge(evac["act"], 4 if n >= 2 else 3)
                c = (0, 2, 1, 3)[n] * W
                for t in range(NT):
                    rotate1(qkv[:, t, c:c + W].rearrange("p (g a n) -> p g a n", g=8, a=2), t, 8)
                    fill(1)
            dve.nop().then_inc(roped, 1)
            for name, at, n, gain in (("cq", 0, QR, SM_CQ), ("ckv", QR, KVR, SM_CKV)):
                wait_norm(name)
                for t in range(NT):
                    i = dve.scalar_tensor_tensor(out=lat[:, t, at:at + n], in0=lat[:, t, at:at + n],
                                                 scalar=rstd(name, t), in1=small[:, gain:gain + n], op0=ALU.mult,
                                                 op1=ALU.mult)
                    i.then_inc(lat_ready, 1)
            for t in range(NT):
                rotate1(lat[:, t, QR + KVR:C_W].rearrange("p (g a n) -> p g a n", g=1, a=2), t, 1)
            for g, nk in ((0, 2), (1, 2), (2, 1)):
                turned_lo(f"cl.{g}", b_hi, b_lo, 2 * g, nk)

            for i in range(HEADS + 2):
                fill(DA_FILL[i][0])
                if i < HEADS:
                    row_maxima(i, 2)
                fill(DA_FILL[i][1])
                if i < HEADS:
                    dve.wait_ge(expd, i + 1)
                    k, h = 4 * (i % 2), i % 2
                    step(dve.reciprocal(st("rinv", k, 4), st("rsum", k, 4)))
                    step(dve.tensor_scalar(st("rinv", k, 4)[:, 1:4:2], st("rinv", k, 4)[:, 1:4:2],
                                           st("lam", 5, 1), None, ALU.mult))
                    if i >= 1:
                        dve.wait_ge(turned, TURNS[f"dap{i - 1}"][0] + 1)
                    cs = (slice(0, P), slice(P, SC_W))
                    for t in range(NT):
                        step.mark(dve.tensor_scalar(mix[:, cs[t]], probs[:, h, 0, cs[t]],
                                                    st("rinv", k + 2 * t, 1), None, ALU.mult))
                    step.wait()
                    for t in range(NT):
                        j = dve.scalar_tensor_tensor(out=mix[:, cs[t]], in0=probs[:, h, 1, cs[t]],
                                                     scalar=st("rinv", k + 2 * t + 1, 1), in1=mix[:, cs[t]],
                                                     op0=ALU.mult, op1=ALU.add)
                    j.then_inc(mixed, 1)
                if i >= 2:
                    n = i - 2
                    wait_norm(f"da{n}")
                    b = bank_of(f"dao{n}")
                    for t in range(NT):
                        j = dve.scalar_tensor_tensor(out=head_out[:, t, n, :], in0=b[:, P * t:P * t + P],
                                                     scalar=rstd(f"da{n}", t), in1=small[:, SM_DA:SM_DA + P],
                                                     op0=ALU.mult, op1=ALU.mult)
                    j.then_inc(freed["dve"], 1)
                fill(DA_FILL[i][2])
            dve.wait_ge(evac["act"], BLOCKS["uq2"][4])
            for t in range(NT):
                v = qb[:, t, :].rearrange("p (h n) -> p h n", h=HEADS)[:, :, NOPE:MLA_QK]
                rotate1(v.rearrange("p h (a n) -> p h a n", a=2), t, HEADS)
            dve.nop().then_inc(roped, 1)
            for g in range(4):
                turned_lo(f"oa.{g}", a_hi, a_lo, 2 * g, 2)

            for i in range(HEADS + 2):
                if i < HEADS:
                    row_maxima(HEADS + i, 1)
                fill(MLA_FILL[i])
                if i >= 2:
                    head_scaled(f"mo{i - 2}", HEADS + i - 2, lambda t: head_out[:, t, i - 2, :], P)
                if i < HEADS:
                    row_sums(HEADS + i)
            for g in range(4):
                turned_lo(f"ob.{g}", a_hi, a_lo, 2 * g, 2)
            fill(0, "pb1")
            for g in range(4):
                turned_lo(f"mg.{g}", a_hi, a_lo, 2 * g, 2, 0.5)
            fill(0, "wo1")
            dve.wait_ge(rows_in[1], 16)
            banks = [2 * (BLOCKS[f"wo{n}"][0] % 2) for n in range(2)]
            add_normed("wo", [[lin[:, b + t, :] for b in banks] for t in range(NT)], rows[:, 1, :])
            for counted in (evac["dve"], evac["dve"], x_ready, rows_used):
                dve.nop().then_inc(counted, 1)
            dve.wait_ge(rows_in[2], 32)
            gained(rows[:, 2, :]).then_inc(xn_ready, 1)
            dve.wait_ge(xn_ready, 2)
            dve.nop().then_inc(rows_used, 1)
            for g in range(4):
                turned_lo(f"x2.{g}", a_hi, a_lo, 2 * g, 2)

            def hidden(e, gate):
                dve.wait_ge(silud, 2 * e)
                for t in range(NT):
                    i = dve.scalar_tensor_tensor(out=hid[:, t, :], in0=act_s[:, t, :], scalar=gate(t),
                                                 in1=lin[:, t, EW:2 * EW], op0=ALU.mult, op1=ALU.mult)
                i.then_inc(hid_ready, 1)

            def mlp(name, n, e0, gated, beside=None):
                u = BLOCKS[name][1]
                pairs0 = turn_pairs[0]

                def gate_of(e):
                    if not gated:
                        return lambda t: rstd("x2", t)
                    if isinstance(e, int):
                        return lambda t: st("gates", N_EXP * t + e, 1)
                    return lambda t: stat[:, bass.ds(e + (cols["gates"][0] + N_EXP * t), 1)]

                assert split_at[0] == u + LEAD
                split_to(u + 6)
                hidden(e0 + 1, gate_of(0))
                split_to(u + 4 + LEAD)
                u += 4

                def one(e, u, last=False, shift=0, shift_e=0, beside=None):
                    dve.wait_ge(turn_hi, pairs0 + e + 1 + shift_e)
                    dve.tensor_tensor(b_lo[:, 0:2, :], turn[:, 0, :].rearrange("p (k n) -> p k n", k=2),
                                      b_hi[:, 0:2, :].bitcast(F32), ALU.subtract).then_inc(freed["dve"], 1)
                    for j in range(2 if last else 6):
                        if j == 3:
                            hidden(e0 + e + 2 + shift_e, gate_of(shift_e + (e + 1)))
                        if u + LEAD + j < N_UNITS:
                            split(u + LEAD + j, shift)
                        if beside is not None and j in (0, 1, 3, 4):
                            beside((0, 1, None, 2, 3)[j])

                one(0, u)
                u += 6
                pairs = (n - 3) // 2
                with dve.Fori(0, pairs) as i:
                    for j in range(2):
                        one(1 + j, u + 6 * j, False, i * 12, i * 2,
                            None if beside is None else lambda k: beside(i, 4 * j + k))
                u += 12 * pairs
                for e in range(1 + 2 * pairs, n):
                    one(e, u, e == n - 1)
                    u += 2 if e == n - 1 else 6
                turn_pairs[0] += n
                split_at[0] = u + LEAD
                unit_at[0] = u

            wait_norm("x2")
            dve.wait_ge(bias_in, 32)
            mlp("FFN", N_FFN, 0, False, lambda i, k: ada_part(2, i, k))
            add_normed("ffn", y_bank, rows[:, 3, :])
            for counted in (x_ready, rows_used):
                dve.nop().then_inc(counted, 1)
            dve.wait_ge(freed["act"], TURNS["ad3"][2])
            dve.wait_ge(rows_in[0], 32)
            step(dve.scalar_tensor_tensor(out=mod[:, D:2 * D], in0=mod[:, D:2 * D], scalar=1.0, in1=rows[:, 0, :],
                                          op0=ALU.add, op1=ALU.mult))
            dve.nop().then_inc(rows_used, 1)
            normalise("u", mod[:, D:2 * D], mod[:, 0:D]).then_inc(xn_ready, 1)
            for g in range(4):
                turned_lo(f"u.{g}", a_hi, a_lo, 2 * g, 2)
            block_loop("jn0", 4)

            dve.wait_ge(evac["act"], BLOCKS["jn1"][4])
            for n in range(2):
                for t in range(NT):
                    rotate(zz[:, t, n * W:(n + 1) * W].rearrange("p (g a n) -> p g a n", g=8, a=2), t,
                           cst[:, C_COS2 + 32 * t:C_COS2 + 32 * t + 32], cst[:, C_SIN2 + 32 * t:C_SIN2 + 32 * t + 32],
                           trig[:, 3, t, :], 8)
                    fill(1)
            dve.nop().then_inc(roped, 1)
            wait_norm("lt")
            for t in range(NT):
                dve.scalar_tensor_tensor(out=zz[:, t, DKV:DKV + P], in0=zz[:, t, DKV:DKV + P], scalar=rstd("lt", t),
                                         in1=small[:, SM_LT:SM_LT + P], op0=ALU.mult, op1=ALU.mult)\
                   .then_inc(lat_ready, 1)
            dve.wait_ge(tanh_ready, NT)
            dve.wait_ge(rows_in[1], 32)
            for t in range(NT):
                g = zz[:, t, RG:RG + D]
                step(dve.scalar_tensor_tensor(out=g, in0=gate2[:, t, 0:D], scalar=1.0, in1=g, op0=ALU.add,
                                              op1=ALU.mult))
                step(dve.scalar_tensor_tensor(out=g, in0=g, scalar=0.5, in1=rows[:, 1, :], op0=ALU.mult,
                                              op1=ALU.mult))
            dve.nop().then_inc(rows_used, 1)

            def ret_out(n):
                wait_norm(f"ret{n}")
                b = bank_of(f"rto{n}")
                for t in range(NT):
                    i = dve.tensor_scalar(zz[:, t, RV + n * P:RV + (n + 1) * P], b[:, P * t:P * t + P],
                                          ss(f"ret{n}", 2 * t), rstd(f"ret{n}", t), ALU.subtract, ALU.mult)
                i.then_inc(freed["dve"], 1)
                dve.wait_ge(freed["dve"], TURNS[f"rto{n}"][2])
                for t in range(NT):
                    v = zz[:, t, RV + n * P:RV + (n + 1) * P]
                    step.mark(dve.tensor_tensor(v, v, zz[:, t, RG + n * P:RG + (n + 1) * P], ALU.mult))

            dve.wait_ge(turned, TURNS["dt4"][0] + 1)
            for i in range(HEADS + 1):
                if i < HEADS:
                    dve.wait_ge(ret_scored, i + 1)
                    dve.wait_ge(decay, i + 1)
                    dve.scalar_tensor_tensor(out=probs_t[:, i % 2, :], in0=sco[:, i % 2, 0:SC_W],
                                             scalar=64 ** -0.5, in1=probs[:, i % 2, 0, :], op0=ALU.mult,
                                             op1=ALU.mult).then_inc(decayed, 1)
                fill(RET_FILL[i])
                if i >= 1:
                    n = i - 1
                    dve.wait_ge(turned, TURNS[f"rto{n}"][0] + 1)
                    b = bank_of(f"rto{n}")
                    for t in range(NT):
                        step.mark(dve.bn_stats(st("bn", 6 * t, 6), b[:, P * t:P * t + P]))
                    step.wait()
                    at = jobs[f"ret{n}"][1]
                    for t in range(NT):
                        j = dve.bn_aggr(stat[:, at + 2 * t:at + 2 * t + 2], st("bn", 6 * t, 6))
                    j.then_inc(var_dve, 1)
                    ret_out(n)

            step.wait()
            dve.nop().then_inc(dve_ret, 1)

            for i in range(HEADS):
                dve.wait_ge(relud, i + 1)
                for t in range(NT):
                    c = slice(0, P) if t == 0 else slice(P, SC_W)
                    w = zz[:, t, IW + i:IW + i + 1]
                    if i == 0:
                        step.mark(dve.tensor_scalar(mix[:, c], probs[:, i % 2, 0, c], w, None, ALU.mult))
                    else:
                        step.mark(dve.scalar_tensor_tensor(out=mix[:, c], in0=probs[:, i % 2, 0, c], scalar=w,
                                                           in1=mix[:, c], op0=ALU.mult, op1=ALU.add))
                step.wait()
                dve.nop().then_inc(idx_acc, 1)
                fill(IDX_FILL[i])
            for g in range(4):
                turned_lo(f"re.{g}", a_hi, a_lo, 2 * g, 2)
            step(dve.tensor_scalar(mix[:, :], mix[:, :], (64 ** -0.5) * (HEADS ** -0.5), None, ALU.mult))
            for c in (CHUNK, P + P + CHUNK):
                step.mark(dve.memset(mix[0:CHUNK, c:c + CHUNK], NEG))
            step.wait()
            for t in range(NT):
                c = slice(0, P) if t == 0 else slice(P, SC_W)
                here, there = mix[:, c], probs[:, 0, 0, c]
                for r in range(TOPK // 8):
                    step(dve.max(st("best"), here))
                    step(dve.match_replace(there, st("best"), here, TAKEN))
                    here, there = there, here
                    if r % 4 == 3:
                        fill(TOPK_FILL // 4)
                i = dve.tensor_scalar(sel_mask[:, c], here, TAKEN / 2, NEG, ALU.is_gt, ALU.mult)
                if t == 0:
                    step(i)
                else:
                    i.then_inc(mask_ready, 1)

            for i in range(HEADS + 2):
                fill(DSA_FILL[i])
                if i < HEADS:
                    n, h = 2 * HEADS + i, i % 2
                    dve.wait_ge(scored, n + 1)
                    dve.wait_ge(bm_ready, i + 1)
                    if i >= 2:
                        dve.wait_ge(turned, TURNS[f"dsp{i - 2}"][0] + 1)
                    dve.scalar_tensor_tensor(out=probs[:, h, 0, :], in0=sco[:, h, 0:SC_W], scalar=64 ** -0.5,
                                             in1=probs[:, h, 1, :], op0=ALU.mult, op1=ALU.add).then_inc(copied, 1)
                    dve.wait_ge(copied, i + 1)
                    maxima(n, 1, probs[:, h, 0:1, :])
                if i >= 2:
                    head_scaled(f"dso{i - 2}", 2 * HEADS + i - 2,
                                lambda t: zz[:, t, DQ + 64 * (i - 2):DQ + 64 * (i - 1)], 64)
                if i < HEADS:
                    row_sums(2 * HEADS + i)
            turned_lo("de.0", b_hi, b_lo, 0, 2)
            turned_lo("de.1", b_hi, b_lo, 2, 2)
            fill(0, "do1")
            for g in range(4):
                turned_lo(f"mh.{g}", a_hi, a_lo, 2 * g, 2, 0.5)
            fill(0, "xo1")
            dve.wait_ge(rows_in[0], 48)
            step(dve.scalar_tensor_tensor(out=mod[:, 4 * D:5 * D], in0=mod[:, 4 * D:5 * D], scalar=1.0,
                                          in1=rows[:, 0, :], op0=ALU.add, op1=ALU.mult))
            normalise("v", mod[:, 4 * D:5 * D], mod[:, 3 * D:4 * D]).then_inc(xn_ready, 1)
            for g in range(4):
                turned_lo(f"v.{g}", a_hi, a_lo, 2 * g, 2)

            def per(v, n):
                return v.rearrange("p (t n) -> p t n", t=NT)

            def over(v, n):
                return bass.AP(v.tensor, v.offset, [v.ap[0], v.ap[1], [0, n]])

            def first_of(eq, weights, n, m):
                w = bass.AP(weights.tensor, weights.offset, [weights.ap[0], [0, NT], [1, n]])
                step(dve.tensor_tensor(eq, eq, w, ALU.mult))
                step(dve.tensor_reduce(m, eq, AX.X, ALU.max))
                step(dve.tensor_tensor(eq, eq, over(m, n), ALU.is_equal))

            dve.wait_ge(turned, TURNS["lg"][0] + 1)
            b = bank_of("lg")[:, 0:40].rearrange("p (t n) -> p t n", t=NT)
            bias = small[:, SM_B:SM_B + 20]
            dve.tensor_tensor(logit, b, bass.AP(bias.tensor, bias.offset, [bias.ap[0], [0, NT], [1, 20]]), ALU.add)\
               .then_inc(freed["dve"], 1)
            dve.wait_ge(freed["dve"], TURNS["lg"][2])
            gl = logit[:, :, 0:4]
            top, m = st("route", 0, 2), st("route", 2, 2)
            step(dve.tensor_reduce(top, gl, AX.X, ALU.max))
            step(dve.tensor_tensor(per(r_eq4, 4), gl, over(top, 4), ALU.is_ge))
            dve.tensor_tensor(per(route_x, 4), gl, over(top, 4), ALU.subtract).then_inc(route_in, 1)
            first_of(per(r_eq4, 4), cst[:, C_W4:C_W4 + 4], 4, m)
            spread = bass.AP(r_eq4.tensor, r_eq4.offset, [r_eq4.ap[0], [4, NT], [1, GROUPS], [0, PER_GROUP]])
            four = "p t (g n) -> p t g n"
            e4 = per(r_em, 16).rearrange(four, g=GROUPS)
            o4 = per(r_oh, 16).rearrange(four, g=GROUPS)
            step.mark(dve.tensor_tensor(e4, logit[:, :, 4:20].rearrange(four, g=GROUPS), spread, ALU.mult))
            step.mark(dve.tensor_scalar(o4, spread, -1.0, -NEG, ALU.add, ALU.mult))
            step.wait()
            step(dve.tensor_tensor(r_em, r_em, r_oh, ALU.add))
            v1, v2 = st("route", 4, 2), st("route", 6, 2)
            step(dve.tensor_reduce(v1, per(r_em, 16), AX.X, ALU.max))
            step(dve.tensor_tensor(per(r_oh, 16), per(r_em, 16), over(v1, 16), ALU.is_equal))
            first_of(per(r_oh, 16), cst[:, C_W16:C_W16 + 16], 16, m)
            step(dve.scalar_tensor_tensor(out=r_em, in0=r_oh, scalar=2 * NEG, in1=r_em, op0=ALU.mult, op1=ALU.add))
            step(dve.tensor_reduce(v2, per(r_em, 16), AX.X, ALU.max))
            step(dve.tensor_tensor(per(r_em, 16), per(r_em, 16), over(v2, 16), ALU.is_equal))
            dve.tensor_tensor(route_y, v2, v1, ALU.subtract).then_inc(route_in, 1)
            first_of(per(r_em, 16), cst[:, C_W16:C_W16 + 16], 16, m)
            dve.wait_ge(route_e, 2)
            total, w1 = st("route", 10, 2), st("route", 12, 2)
            step.mark(dve.tensor_reduce(total, per(route_x, 4), AX.X, ALU.add))
            step.mark(dve.tensor_scalar(w1, route_y, 1.0, None, ALU.add))
            step.wait()
            step(dve.tensor_tensor(w1, w1, total, ALU.mult))
            step(dve.reciprocal(w1, w1))
            step(dve.tensor_tensor(route_y, route_y, w1, ALU.mult))
            step.mark(dve.tensor_tensor(per(r_oh, 16), per(r_oh, 16), over(w1, 16), ALU.mult))
            step.mark(dve.tensor_tensor(per(r_em, 16), per(r_em, 16), over(route_y, 16), ALU.mult))
            step.wait()
            step(dve.tensor_tensor(st("gates"), r_oh, r_em, ALU.add))
            mlp("MOE", N_EXP, N_FFN, True)

            dve.wait_ge(freed["act"], TURNS["ad11"][2])
            dve.wait_ge(used, N_UNITS)
            for n in range(2):
                c = slice(n * W, (n + 1) * W)
                for t in range(NT):
                    step.mark(dve.tensor_tensor(tmp[:, t, :], y_bank[t][n], mod[:, 5 * D + n * W:5 * D + (n + 1) * W],
                                                ALU.mult))
                step.wait()
                for t in range(NT):
                    step.mark(dve.tensor_tensor(x[:, t, c], x[:, t, c], tmp[:, t, :], ALU.add))
                step.wait()
            dve.nop().then_inc(x_ready, 1)
            wait_norm("fin")
            dve.wait_ge(rows_in[1], 48)
            for t in range(NT):
                dve.scalar_tensor_tensor(out=xn[:, t, :], in0=x[:, t, :], scalar=rstd("fin", t), in1=rows[:, 1, :],
                                         op0=ALU.mult, op1=ALU.mult).then_inc(xn_ready, 1)

        @block.tensor
        def _(pe):
            turn_at = [0]
            unit_at = [0]

            def three(dst, l_hi, l_lo, r_hi, r_lo, start, stop):
                pe.matmul(dst, l_hi, r_hi, start=start, stop=False)
                pe.matmul(dst, l_hi, r_lo, start=False, stop=False)
                return pe.matmul(dst, l_lo, r_hi, start=False, stop=stop)

            def bank_free(name):
                number = BLOCKS[name][0]
                if number >= 2:
                    before = BLOCKS[BLOCK_NAMES[number - 2]]
                    pe.wait_ge(evac[before[3]], before[4])

            def left(name):
                kind = name.rstrip("0123456789")
                if kind in ("uq", "ukv", "do"):
                    return b_hi, b_lo, 3 if kind == "ukv" else 0
                return a_hi, a_lo, 0

            def product_unit(name, part, shift=0, first=None):
                number, u0, units, _, _ = BLOCKS[name]
                if first is not None:
                    number, u0 = first
                nk_all, width = LOADS[name][3], LOADS[name][2]
                u = u0 + part
                pe.wait_ge(lo_ready, u + 1 + shift)
                hi, lo, k0 = left(name)
                wh = w_hi[:, u % NSLOT, :].rearrange("p (k n) -> p k n", k=UK)
                wl = w_lo[:, u % NSLOT, :].rearrange("p (k n) -> p k n", k=UK)
                for k in range(min(UK, nk_all - part * UK)):
                    kt = part * UK + k
                    start, stop = kt == 0, kt == nk_all - 1
                    for t in range(NT):
                        c = slice(t * P, (t + 1) * P)
                        i = three(lin[:, 2 * (number % 2) + t, 0:width], hi[:, k0 + kt, c], lo[:, k0 + kt, c],
                                  wh[:, k, 0:width], wl[:, k, 0:width], start, stop)
                i.then_inc(used, 1)

            def fill(n, until=None):
                end = unit_at[0] + n if until is None else BLOCKS[until][1] + BLOCKS[until][2]
                while unit_at[0] < end:
                    for name in BLOCK_NAMES:
                        _, u0, units, _, _ = BLOCKS[name]
                        if u0 <= unit_at[0] < u0 + units:
                            if unit_at[0] == u0:
                                bank_free(name)
                            product_unit(name, unit_at[0] - u0)
                    unit_at[0] += 1

            def block_loop(first, pairs):
                number, u0, units, engine, count = BLOCKS[first]
                for before in BLOCK_NAMES[max(0, number - 2):number]:
                    pe.wait_ge(evac[BLOCKS[before][3]], BLOCKS[before][4])
                for j in range(2):
                    for part in range(4):
                        product_unit(first, part, 0, (number + j, u0 + 4 * j))
                with pe.Fori(1, pairs) as i:
                    for j in range(2):
                        pe.wait_ge(evac[engine], i * 2 + (count - 2 + j))
                        for part in range(4):
                            product_unit(first, part, i * 8, (number + j, u0 + 4 * j))
                unit_at[0] += 8 * pairs

            def turn_bank(name):
                number = TURNS[name][0]
                assert number == turn_at[0], (name, number, turn_at[0])
                turn_at[0] += 1
                if number >= 2:
                    _, engine, count = TURNS[TURN_NAMES[number - 2]]
                    pe.wait_ge(freed[engine], count)
                return turn[:, number % 2, :]

            def turn_all(name, sources):
                b = turn_bank(name)
                at = 0
                for src in sources:
                    n, m = src.shape[-1], src.shape[0]
                    i = pe.transpose(b[0:n, at:at + m], src, ident[0:m, 0:m])
                    at += m
                i.then_inc(turned, 1)

            def turn_rows(label, source, n_k=DK):
                for g in range(-(-n_k // 2)):
                    turn_all(f"{label}.{g}", [source(t, k) for k in range(2 * g, min(n_k, 2 * g + 2))
                                              for t in range(NT)])

            def pairs_freed(name):
                _, engine, count = TURNS[name]
                pe.wait_ge(freed[engine], count)

            def col(v, k, n=P):
                return v[:, k * n:(k + 1) * n]

            def scores(bank, q, k):
                pe.matmul(bank[:, 0:P], q[:, 0:P], k[:, 0:P], start=True, stop=True)
                return pe.matmul(bank[:, P:SC_W], q[:, P:S], k[:, 0:S], start=True, stop=True)

            def turn_probs(name, p):
                turn_all(name, [p[:, 0:P], p[:, P:2 * P], p[:, 2 * P:3 * P]])

            def weigh(name, p, v, width):
                b = turn_bank(name)
                pe.matmul(b[:, 0:width], p[:, 0:P], v[0], start=True, stop=True)
                pe.matmul(b[:, width:2 * width], p[:, P:2 * P], v[0], start=True, stop=False)
                pe.matmul(b[:, width:2 * width], p[:, 2 * P:3 * P], v[1], start=False, stop=True).then_inc(turned, 1)

            def ada_sums(n0, n1):
                pe.wait_ge(ada_done, DK * ((n1 + 1) // 2))
                for n in range(n0, n1):
                    pe.matmul(turn_bank(f"ad{n}"), ones[:, :].broadcast_to([P, P]), mod[:, n * W:(n + 1) * W],
                              start=True, stop=True).then_inc(turned, 1)

            pe.wait_ge(tables_in, 16)
            pe.wait_ge(xn_ready, 1)
            turn_rows("x1", lambda t, k: col(xn[:, t, :], k))
            pairs_freed("x1.3")
            block_loop("in0", 3)
            fill(0, "in7")
            pe.wait_ge(roped, 1)
            pe.wait_ge(evac["act"], BLOCKS["in7"][4])

            def turn_qk(h):
                turn_all(f"qk{h}", [qkv[:, t, c + h * P:c + (h + 1) * P] for c in (0, D) for t in range(NT)])

            turn_qk(0)
            turn_qk(1)
            pe.wait_ge(lat_ready, 2 * NT)
            turn_rows("cl", lambda t, k: col(lat[:, t, :], k), 5)
            for i in range(HEADS + 2):
                if i + 2 < HEADS:
                    turn_qk(i + 2)
                fill(DA_FILL[i][0])
                if i < HEADS:
                    pe.wait_ge(freed["act"], TURNS[f"qk{i}"][2])
                    if i >= 1:
                        pe.wait_ge(expd, i)
                    for j in range(2):
                        rows_j = slice(DA_HD * j, DA_HD * (j + 1))
                        m = scores(sco[:, j, :], qk_t[rows_j, i, 0:S], qk_t[rows_j, i, S:2 * S])
                    m.then_inc(scored, 1)
                if i == 3:
                    pairs_freed("cl.2")
                fill(DA_FILL[i][1])
                if 1 <= i <= HEADS:
                    pe.wait_ge(mixed, i)
                    turn_probs(f"dap{i - 1}", mix)
                if i >= 2:
                    h = i - 2
                    pe.wait_ge(freed["act"], TURNS[f"dap{h}"][2])
                    weigh(f"dao{h}", probs_t[:, h % 2, :], [va[t][:, h * P:(h + 1) * P] for t in range(NT)], P)
                fill(DA_FILL[i][2])
            pe.wait_ge(freed["dve"], TURNS["dao7"][2])
            turn_rows("oa", lambda t, k: head_out[:, t, k, :])
            pe.wait_ge(roped, 2)
            pe.wait_ge(evac["dve"], BLOCKS["ukv3"][4])
            qh = [qb[:, t, :].rearrange("p (h n) -> p h n", h=HEADS) for t in range(NT)]
            for g in range(4):
                turn_all(f"mr{g}", [qh[t][:, 2 * g + a, NOPE:MLA_QK] for a in range(2) for t in range(NT)])
            turn_all("kr", [lat[:, t, QR + KVR:C_W] for t in range(NT)])
            pairs_freed("oa.3")

            def turn_mq(h):
                turn_all(f"mq{h}", [qh[t][:, h, 0:NOPE] for t in range(NT)]
                         + [kvb[t][:, 2 * P * h:2 * P * h + P] for t in range(NT)])

            turn_mq(0)
            turn_mq(1)
            for i in range(HEADS + 2):
                if i + 2 < HEADS:
                    turn_mq(i + 2)
                if i < HEADS:
                    n = HEADS + i
                    pe.wait_ge(freed["act"], TURNS[f"mq{i}"][2])
                    pe.wait_ge(expd, HEADS if i < 2 else n - 1)
                    b = sco[:, n % 2, :]
                    q, k = qk_t[:, i, 0:S], qk_t[:, i, S:2 * S]
                    for t, c, keys in ((0, slice(0, P), slice(0, P)), (1, slice(P, SC_W), slice(0, S))):
                        qt = slice(t * P, (t + 1) * P)
                        pe.matmul(b[:, c], q[:, qt], k[:, keys], start=True, stop=False)
                        m = pe.matmul(b[:, c], qr_t[i][:, qt], kr_t[:, keys], start=False, stop=True)
                    m.then_inc(scored, 1)
                fill(MLA_FILL[i])
                if 1 <= i <= HEADS:
                    pe.wait_ge(expd, HEADS + i)
                    turn_probs(f"mp{i - 1}", probs[:, (i - 1) % 2, 0, :])
                if i >= 2:
                    h = i - 2
                    pe.wait_ge(freed["act"], TURNS[f"mp{h}"][2])
                    weigh(f"mo{h}", probs_t[:, h % 2, :], [kvb[t][:, 2 * P * h + P:2 * P * (h + 1)] for t in range(NT)],
                          P)
            pe.wait_ge(freed["dve"], TURNS["mo7"][2])
            turn_rows("ob", lambda t, k: head_out[:, t, k, :])
            pairs_freed("ob.3")
            fill(0, "pb1")
            pe.wait_ge(merged, 2 * NT)
            turn_rows("mg", lambda t, k: col(gate1[:, t, :], k))
            pairs_freed("mg.3")
            fill(0, "wo1")
            ada_sums(0, 4)
            pe.wait_ge(xn_ready, 2)
            turn_rows("x2", lambda t, k: col(xn[:, t, :], k))
            pairs_freed("x2.3")

            def mlp(name, label, n, hid0):
                u = BLOCKS[name][1]
                turn0, _, freed0 = TURNS[f"{label}0"]
                assert turn_at[0] == turn0

                def gate_up(u, shift=0):
                    for half in range(2):
                        pe.wait_ge(lo_ready, u + 2 * half + 2 + shift)
                        s = (u + 2 * half) % NSLOT
                        for k in range(4):
                            kt = 4 * half + k
                            rh, rl = (v[:, s:s + 2, k * EW:(k + 1) * EW] for v in (w_hi, w_lo))
                            for t in range(NT):
                                c = slice(t * P, (t + 1) * P)
                                i = three(lin[:, t, :].rearrange("p (a n) -> p a n", a=2), a_hi[:, kt, c],
                                          a_lo[:, kt, c], rh, rl, kt == 0, kt == DK - 1)
                        i.then_inc(used, 2)

                def turn_hidden(e, shift_e=0):
                    pe.wait_ge(hid_ready, hid0 + e + 1 + shift_e)
                    for k in range(2):
                        for t in range(NT):
                            at = k * S + t * P
                            i = pe.transpose(turn[:, 0, at:at + P], hid[:, t, k * P:(k + 1) * P], ident)
                    i.then_inc(turned, 1)

                def down(e, u, first=False, last=False, shift=0, shift_e=0):
                    pe.wait_ge(freed["dve"], freed0 + e + shift_e)
                    for k in range(2):
                        pe.wait_ge(lo_ready, u + k + 1 + shift)
                        s = (u + k) % NSLOT
                        for n_ in range(2):
                            wc = slice(n_ * W, (n_ + 1) * W)
                            for t in range(NT):
                                c = slice(t * P, (t + 1) * P)
                                i = three(y_bank[t][n_], b_hi[:, k, c], b_lo[:, k, c], w_hi[:, s, wc], w_lo[:, s, wc],
                                          first and k == 0, last and k == 1)
                        i.then_inc(used, 1)

                gate_up(u)
                u += 4
                turn_hidden(0)
                gate_up(u)
                down(0, u + 4, first=True)
                u += 6
                pairs = (n - 3) // 2
                with pe.Fori(0, pairs) as i:
                    for j in range(2):
                        turn_hidden(1 + j, i * 2)
                        gate_up(u + 6 * j, i * 12)
                        down(1 + j, u + 6 * j + 4, shift=i * 12, shift_e=i * 2)
                u += 12 * pairs
                for e in range(1 + 2 * pairs, n):
                    turn_hidden(e)
                    if e + 1 < n:
                        gate_up(u)
                        u += 4
                    down(e, u, last=e == n - 1)
                    u += 2
                turn_at[0] += n
                unit_at[0] = u

            def all_banks_free():
                for engine in ("act", "dve"):
                    done = [BLOCKS[n][4] for n in BLOCK_NAMES if BLOCKS[n][3] == engine and BLOCKS[n][1] < unit_at[0]]
                    pe.wait_ge(evac[engine], max(done))
                    pe.wait_ge(freed[engine], max(TURNS[n][2] for n in TURN_NAMES[:turn_at[0]]
                                                  if TURNS[n][1] == engine))

            all_banks_free()
            mlp("FFN", "ffn", N_FFN, 0)
            ada_sums(4, 10)
            pe.wait_ge(xn_ready, 3)
            turn_rows("u", lambda t, k: col(xn[:, t, :], k))
            pe.wait_ge(one_hot_in, 16)
            b = turn_bank("bv")
            pe.matmul(b[0:HEADS, 0:SC_W], rel_bias[:, :], mix[0:BUCKETS, :], start=True, stop=True).then_inc(turned, 1)
            pairs_freed("u.3")
            block_loop("jn0", 4)
            fill(0, "jn8")
            pe.wait_ge(lat_ready, 3 * NT)
            turn_all("lt", [zz[:, t, DKV:DKV + P] for t in range(NT)])
            pe.wait_ge(freed["act"], TURNS["lt"][2])
            b = turn_bank("lat")
            for t in range(NT):
                m = pe.matmul(b[:, t * P:(t + 1) * P], idk_t[:, t * P:(t + 1) * P], kv_up[:, :], start=True, stop=True)
            m.then_inc(turned, 1)
            pe.wait_ge(roped, 3)
            for g in range(4):
                turn_all(f"rt{g}", [col(zz[:, t, c:c + W], g) for c in (RQ, RK) for t in range(NT)])
            for g in range(4):
                c = IQ if g < 2 else DQ
                turn_all(f"dt{g}", [col(zz[:, t, c:c + W], 2 * (g % 2) + a) for a in range(2) for t in range(NT)])
            pe.wait_ge(freed["act"], TURNS["lat"][2])
            turn_all("dt4", [probs_t[:, t, 0:P] for t in range(NT)] + [zz[:, t, DKV:DKV + P] for t in range(NT)])
            for i in range(HEADS + 1):
                if i < HEADS:
                    pe.wait_ge(freed["act"], TURNS[f"rt{i // 2}"][2])
                    if i >= 2:
                        pe.wait_ge(decayed, i - 1)
                    r = slice(64 * (i % 2), 64 * (i % 2) + 64)
                    q, k = rt_t[r, i // 2, 0:S], rt_t[r, i // 2, S:2 * S]
                    b = sco[:, i % 2, :]
                    pe.matmul(b[:, 0:S], k[:, 0:P], q[:, 0:S], start=True, stop=True)
                    pe.matmul(b[:, S:SC_W], k[:, P:S], q[:, P:S], start=True, stop=True).then_inc(ret_scored, 1)
                fill(RET_FILL[i])
                if i >= 1:
                    h = i - 1
                    pe.wait_ge(decayed, i)
                    weigh(f"rto{h}", probs_t[:, h % 2, :], [zz[:, t, RV + h * P:RV + (h + 1) * P] for t in range(NT)],
                          P)
            pe.wait_ge(freed["act"], TURNS["dt4"][2])
            for i in range(HEADS):
                if i >= 2:
                    pe.wait_ge(relud, i - 1)
                r = slice(64 * (i % 2), 64 * (i % 2) + 64)
                scores(sco[:, i % 2, :], idq_t[r, i // 2, :], idk_t[r, 0:S]).then_inc(idx_scored, 1)
                fill(IDX_FILL[i])
            pe.wait_ge(dve_ret, 1)
            turn_rows("re", lambda t, k: col(zz[:, t, RV:RV + D], k))
            pairs_freed("re.3")
            for i in range(HEADS + 2):
                if i == 0:
                    fill(TOPK_FILL)
                fill(DSA_FILL[i])
                if i < HEADS:
                    pe.wait_ge(relud, HEADS)
                    if i >= 2:
                        pe.wait_ge(copied, i - 1)
                    r = slice(64 * (i % 2), 64 * (i % 2) + 64)
                    scores(sco[:, i % 2, :], idq_t[r, 4 + i // 2, :], idk_t[r, S:2 * S]).then_inc(scored, 1)
                if 1 <= i <= HEADS:
                    pe.wait_ge(expd, 2 * HEADS + i)
                    turn_probs(f"dsp{i - 1}", probs[:, (i - 1) % 2, 0, :])
                if i >= 2:
                    h = i - 2
                    pe.wait_ge(freed["act"], TURNS[f"dsp{h}"][2])
                    weigh(f"dso{h}", probs_t[:, h % 2, :], [dv[:, t, :] for t in range(NT)], 64)
            pe.wait_ge(freed["dve"], TURNS["dso7"][2])
            turn_rows("de", lambda t, k: col(zz[:, t, DQ:DQ + W], k), 4)
            pairs_freed("de.1")
            fill(0, "do1")
            pe.wait_ge(merged, 4 * NT)
            turn_rows("mh", lambda t, k: col(gate2[:, t, :], k))
            pairs_freed("mh.3")
            fill(0, "xo1")
            ada_sums(10, 12)
            pe.wait_ge(xn_ready, 4)
            turn_rows("v", lambda t, k: col(xn[:, t, :], k))
            pairs_freed("v.3")
            b = turn_bank("lg")
            pe.wait_ge(route_lo, 1)
            for t in range(NT):
                for k in range(DK):
                    c = slice(t * P, (t + 1) * P)
                    m = three(b[:, t * 20:t * 20 + 20], a_hi[:, k, c], a_lo[:, k, c], router_hi[:, k, :],
                              router_lo[:, k, :], k == 0, k == DK - 1)
            m.then_inc(turned, 1)
            all_banks_free()
            mlp("MOE", "moe", N_EXP, N_FFN)


_WEIGHTS = ["x", "positions", "w_in", "w_uq", "w_ukv", "w_proj_a", "w_proj_b", "w_o", "w_ffn_gate", "w_ffn_up",
            "w_ffn_down", "ln_mix_pre", "ln_mix_post", "ln_ffn_pre", "ln_ffn_post", "c_2", "w_ada_2", "b_ada_2",
            "norm_mix_g_2", "w_in_2", "ret_gn_g_2", "w_dsa_kv_up_2", "rel_bias_2", "w_ret_out_2", "w_dsa_out_2",
            "w_gate_2", "b_gate_2", "w_o_2", "norm_ffn_g_2", "w_exp_gate_2", "w_exp_up_2", "w_exp_down_2",
            "norm_final_g_2"]


def kernel(**inputs):
    import concourse.bacc as _bacc
    from concourse.bass_utils import run_bass_kernel_spmd as _run

    nc = _bacc.Bacc("TRN2", target_bir_lowering=False, num_devices=1)
    a = {name: np.ascontiguousarray(value) for name, value in inputs.items()}
    consts, one_hot = shape_constants()
    packed = {
        "constants": consts,
        "bucket_choice": one_hot,
        "small_gains": np.concatenate([a[n].reshape(1, -1) for n in (
            "da_subln", "q_a_norm", "kv_a_norm", "dsa_kv_norm_g_2", "b_group_router_2", "b_expert_router_2")], axis=1),
        "lambdas": np.concatenate([a[n].reshape(1, -1) for n in (
            "lambda_q1", "lambda_k1", "lambda_q2", "lambda_k2")], axis=1),
        "router": np.concatenate([a["w_group_router_2"][0], a["w_expert_router_2"][0]], axis=1),
    }
    arrays, aps = {}, {}
    for name, value in [(n, a[n]) for n in _WEIGHTS] + list(packed.items()):
        arrays[f"in_{name}_dram"] = value
        aps[name] = nc.dram_tensor(f"in_{name}_dram", value.shape, mybir.dt.from_np(value.dtype),
                                   kind="ExternalInput").ap()
    rel_rows = nc.dram_tensor("relative_rows", (HEADS, P, REL_W), F32).ap()
    out = nc.dram_tensor("out_0_dram", (1, S, D), F32, kind="ExternalOutput").ap()
    two_blocks(nc, aps, aps["constants"], aps["bucket_choice"], aps["small_gains"], aps["lambdas"], aps["router"],
               rel_rows, out)
    r = _run(nc, [arrays], core_ids=[0])
    return r.results[0]["out_0_dram"]
```

```python
from contextlib import ExitStack

import numpy as np

import concourse.bass as bass
from concourse import mybir

F32 = mybir.dt.float32
F32R = mybir.dt.float32r
I32 = mybir.dt.int32
ALU = mybir.AluOpType
ACT = mybir.ActivationFunctionType
AX = mybir.AxisListType

P = 128
D = 1024
S = 256
NT = S // P
DK = D // P
CHUNK = 64
HEADS = 8
W = 512
UK = 2
UW = UK * W
NSLOT = 4
LEAD = 3
NEG = -1e30
TAKEN = -3e38
EPS = 1e-6
GN_EPS = 1e-5
LAMBDA_INIT = 0.8 - 0.6
DA_HD = 64
QR, KVR, ROPE, NOPE = 384, 256, 64, 128
MLA_QK = NOPE + ROPE
C_W = QR + KVR + ROPE
QKV_W = 3 * D
DFF = 2816
EW = 256
N_FFN = DFF // EW
N_EXP = 16
GROUPS, PER_GROUP = 4, 4
IN2_W = 4296
RQ, RK, RV, RG, DQ, DKV, IQ, IK, IW = 0, 512, 1024, 2048, 3072, 3584, 3712, 4224, 4288
TOPK = 64
N_ARENA = 14736
N_STAT = 300
BUCKETS = 32
REL_W = 384
SC_W = P + S
TWO_PI_PARTS = (6.28125, 0.0019350051879882812, 3.01991598819e-07)
ROUND = 12582912.0
SM_DA, SM_CQ, SM_CKV, SM_LT, SM_B, SM_END = 0, 128, 512, 768, 896, 916
JOBS = [("x1", D, EPS, 2, 2), ("cq", QR, EPS, 2, 2), ("ckv", KVR, EPS, 2, 2)]
JOBS += [(f"da{n}", 2 * DA_HD, EPS, 2, 2) for n in range(HEADS)]
JOBS += [("wo.0", D, EPS, 2, 1), ("wo.1", D, EPS, 2, 1), ("x2", D, EPS, 2, 2)]
JOBS += [("ffn.0", D, EPS, 2, 1), ("ffn.1", D, EPS, 2, 1), ("u.0", D, EPS, 1, 1), ("u.1", D, EPS, 1, 1)]
JOBS += [("lt", P, EPS, 2, 2)]
JOBS += [(f"ret{n}", 1, GN_EPS, 4, 2) for n in range(HEADS)]
JOBS += [("v.0", D, EPS, 1, 1), ("v.1", D, EPS, 1, 1), ("fin.0", D, EPS, 1, 1), ("fin.1", D, EPS, 1, 1)]
JOB_NAMES = [j[0] for j in JOBS]
DA_FILL = [(1, 1, 1)] * 6 + [(0, 1, 1)] * 4
MLA_FILL = [1] * 8 + [0, 0]
RET_FILL = [1] * 8 + [0]
IDX_FILL = [1] * 8
TOPK_FILL = 4
DSA_FILL = [1] * 4 + [0] * 6

C_ID, C_DIST, C_COS2, C_SIN2, C_FREQ, C_W4, C_W16, C_END = 0, 128, 512, 576, 640, 672, 676, 692


def shape_constants():
    c = np.zeros((P, C_END), np.float32)
    c[:, C_ID:C_ID + P] = np.eye(P, dtype=np.float32)
    k = np.arange(P)[:, None]
    q = np.arange(S)[None, :]
    d0 = np.abs(q - k).astype(np.float32)
    d0[(k // CHUNK) > (q // CHUNK)] = 1e30
    c[:, C_DIST:C_DIST + S] = d0
    d1 = np.abs(q[:, :P] - k).astype(np.float32)
    d1[(k // CHUNK) > (q[:, :P] // CHUNK)] = 1e30
    c[:, C_DIST + S:C_DIST + SC_W] = d1
    half = np.arange(32, dtype=np.float32)
    f2 = np.power(np.float32(10000.0), -(half * np.float32(2.0)) / np.float32(64)).astype(np.float32)
    for t in range(NT):
        ang = (np.arange(P, dtype=np.float32) + np.float32(t * P))[:, None] * f2[None, :]
        c[:, C_COS2 + 32 * t:C_COS2 + 32 * t + 32] = np.cos(ang.astype(np.float64))
        c[:, C_SIN2 + 32 * t:C_SIN2 + 32 * t + 32] = np.sin(ang.astype(np.float64))
    inv = np.float32(1.0) / np.power(np.float32(10000.0), half * np.float32(2.0 / 64)).astype(np.float32)
    c[:, C_FREQ:C_FREQ + 32] = inv
    c[:, C_W4:C_W4 + 4] = np.arange(4, 0, -1)
    c[:, C_W16:C_W16 + 16] = np.arange(16, 0, -1)
    rel = np.arange(REL_W) - (S - 1)
    nb = BUCKETS // 2
    n = np.abs(rel)
    ex = nb // 2
    nf = np.maximum(n, 1).astype(np.float32)
    large = ex + (np.log(nf / np.float32(ex)) / np.float32(np.log(128 / ex)) * np.float32(nb - ex)).astype(np.int32)
    bucket = (rel > 0) * nb + np.where(n < ex, n, np.minimum(large, nb - 1))
    one_hot = (bucket[None, :] == np.arange(BUCKETS)[:, None]).astype(np.float32)
    return c, one_hot


def plan_blocks():
    order = [(f"in{n}", DK, "act") for n in range(11)]
    order += [(f"uq{n}", QR // P, "act") for n in range(3)]
    order += [(f"ukv{n}", KVR // P, "dve") for n in range(4)]
    order += [("in11", DK, "act")]
    order += [(f"{n}", DK, "dve") for n in ("pa0", "pa1", "pb0", "pb1", "wo0", "wo1")]
    order += [("FFN", 6 * N_FFN, None)]
    order += [(f"jn{n}", DK, "act") for n in range(9)]
    order += [(f"gt{n}", DK, "dve") for n in range(4)]
    order += [("ro0", DK, "dve"), ("ro1", DK, "dve"), ("do0", DK // 2, "dve"), ("do1", DK // 2, "dve")]
    order += [("xo0", DK, "dve"), ("xo1", DK, "dve")]
    order += [("MOE", 6 * N_EXP, None)]
    blocks, number, unit, count = {}, 0, 0, {"act": 0, "dve": 0}
    names = []
    for name, nk, engine in order:
        if engine is None:
            blocks[name] = (None, unit, nk, None, None)
            unit += nk
            continue
        units = -(-nk // UK)
        count[engine] += 1
        blocks[name] = (number, unit, units, engine, count[engine])
        names.append(name)
        number += 1
        unit += units
    return blocks, names, unit


def plan_turns():
    order = [(f"x1.{g}", "dve") for g in range(4)]
    order += [(f"qk{h}", "act") for h in range(2)]
    order += [(f"cl.{g}", "dve") for g in range(3)]
    for h in range(HEADS + 2):
        if h + 2 < HEADS:
            order.append((f"qk{h + 2}", "act"))
        if 1 <= h <= HEADS:
            order.append((f"dap{h - 1}", "act"))
        if 2 <= h:
            order.append((f"dao{h - 2}", "dve"))
    order += [(f"ad{n}", "act") for n in range(4)]
    order += [(f"oa.{g}", "dve") for g in range(4)]
    order += [(f"mr{g}", "act") for g in range(4)]
    order += [("kr", "act")]
    order += [(f"mq{h}", "act") for h in range(2)]
    for h in range(HEADS + 2):
        if h + 2 < HEADS:
            order.append((f"mq{h + 2}", "act"))
        if 1 <= h <= HEADS:
            order.append((f"mp{h - 1}", "act"))
        if 2 <= h:
            order.append((f"mo{h - 2}", "dve"))
    order += [(f"ob.{g}", "dve") for g in range(4)]
    order += [(f"mg.{g}", "dve") for g in range(4)]
    order += [(f"x2.{g}", "dve") for g in range(4)]
    order += [(f"ffn{e}", "dve") for e in range(N_FFN)]
    order += [("bv", "act")]
    order += [(f"u.{g}", "dve") for g in range(4)]
    order += [(f"ad{n}", "act") for n in range(4, 12)]
    order += [("lt", "act"), ("lat", "act")]
    order += [(f"rt{g}", "act") for g in range(4)]
    order += [(f"dt{g}", "act") for g in range(5)]
    order += [(f"rto{h}", "dve") for h in range(HEADS)]
    order += [(f"re.{g}", "dve") for g in range(4)]
    for h in range(HEADS + 2):
        if 1 <= h <= HEADS:
            order.append((f"dsp{h - 1}", "act"))
        if 2 <= h:
            order.append((f"dso{h - 2}", "dve"))
    order += [(f"de.{g}", "dve") for g in range(2)]
    order += [(f"mh.{g}", "dve") for g in range(4)]
    order += [(f"v.{g}", "dve") for g in range(4)]
    order += [(f"moe{e}", "dve") for e in range(N_EXP)]
    turns, count, names = {}, {"act": 0, "dve": 0}, []
    for number, (name, engine) in enumerate(order):
        count[engine] += 1
        turns[name] = (number, engine, count[engine])
        names.append(name)
    return turns, names


BLOCKS, BLOCK_NAMES, N_UNITS = plan_blocks()
TURNS, TURN_NAMES = plan_turns()


class Counted:

    def __init__(self, engine, done):
        self.engine, self.done, self.n, self.shift = engine, done, 0, 0

    def __call__(self, instruction):
        self.mark(instruction)
        self.wait()

    def mark(self, instruction):
        self.n += 1
        instruction.then_inc(self.done, 1)

    def wait(self):
        self.engine.wait_ge(self.done, self.n + self.shift)


def two_blocks(nc, ins, consts, one_hot_d, small_d, lambda_d, router_d, rel_rows, out):
    ctx = ExitStack()
    with ctx:
        def sb(name, shape, dt=F32):
            return ctx.enter_context(nc.sbuf_tensor(name, shape, dt))

        def psum(name, shape):
            return ctx.enter_context(nc.psum_tensor(name, shape, F32))

        def sem(name):
            return ctx.enter_context(nc.semaphore(name))

        raw = sb("raw", [P, NSLOT, UW])
        w_hi = sb("w_hi", [P, NSLOT, UW], F32R)
        w_lo = sb("w_lo", [P, NSLOT, UW], F32R)
        x = sb("x", [P, NT, D])
        a_hi = sb("a_hi", [P, DK, S], F32R)
        a_lo = sb("a_lo", [P, DK, S], F32R)
        b_hi = sb("b_hi", [P, 5, S], F32R)
        b_lo = sb("b_lo", [P, 5, S], F32R)
        c_col = sb("c_col", [P, DK])
        ones = sb("ones", [P, 1])
        mod = sb("mod", [P, 6 * D])
        rows = sb("rows", [P, 4, D])
        cst = sb("cst", [P, C_END])
        small = sb("small", [P, SM_END])
        probs = sb("probs", [P, 2, 2, SC_W])
        mix = sb("mix", [P, SC_W])
        probs_t = sb("probs_t", [P, 2, SC_W])
        dv = sb("dv", [P, NT, 64])
        router = sb("router", [P, DK, 20])
        router_hi = sb("router_hi", [P, DK, 20], F32R)
        router_lo = sb("router_lo", [P, DK, 20], F32R)
        trig = sb("trig", [P, 4, NT, 32])
        stat = sb("stat", [P, N_STAT])
        rel_bias = sb("rel_bias", [BUCKETS, HEADS])
        kv_up = sb("kv_up", [P, P])
        idk_t = sb("idk_t", [P, 2 * S])
        act_junk = idk_t[:, :].bitcast(mybir.dt.bfloat16)
        pos_i = sb("pos_i", [P, NT], I32)
        tmp = sb("tmp", [P, 2, W])
        arena = sb("arena", [P, N_ARENA])

        lin = psum("lin", [P, 4, W])
        turn = psum("turn", [P, 2, W])
        sco = psum("sco", [P, 2, W])

        ident = cst[:, C_ID:C_ID + P]

        def carve(at, *dims):
            n = int(np.prod(dims))
            v = arena[:, at:at + n]
            if len(dims) == 2:
                v = v.rearrange("p (a b) -> p a b", b=dims[1])
            return v, at + n

        xn, _ = carve(0, NT, D)

        qkv, at1 = carve(0, NT, QKV_W)
        qk_t, at2 = carve(at1, HEADS, 2 * S)
        lat, at3 = carve(at2, NT, C_W)
        qb, at4 = carve(at3, NT, HEADS * MLA_QK)
        head_out = qk_t[:, :, 0:S].rearrange("p h (t d) -> p t h d", t=NT)
        kvb = [qkv[:, t, 0:2 * D] for t in range(NT)]
        va = [qkv[:, t, 2 * D:3 * D] for t in range(NT)]
        kr_t = mix[0:ROPE, 0:S]
        qr_t = [va[h // 4][0:ROPE, (h % 4) * S:(h % 4 + 1) * S] for h in range(HEADS)]
        gate1 = mod[:, 2 * D:6 * D].rearrange("p (t n) -> p t n", t=NT)

        zz, bt1 = carve(0, NT, IN2_W)
        rt_t, bt2 = carve(bt1, 4, 2 * S)
        gate2, bt3 = carve(bt2, NT, 2 * D)
        idq_t = mod[:, 0:2 * D].rearrange("p (g n) -> p g n", g=8)
        assert max(at4, bt3) <= N_ARENA
        sel_mask, _ = carve(bt1, SC_W)
        rel_b = [arena[:, bt1 + 512 * (1 + n):bt1 + 512 * (1 + n) + SC_W] for n in range(2)]

        act_s, _ = carve(4096, NT, EW)
        hid, _ = carve(4608, NT, EW)
        y_bank = [[lin[:, 2, :], lin[:, 3, :]], [sco[:, 0, :], sco[:, 1, :]]]

        cols = {}
        for name, n in (("neg_half", 4), ("ms", 4), ("lam", 12), ("pos", 2), ("nmax", 8), ("rsum", 8), ("rinv", 8),
                        ("best", 8), ("bn", 12), ("route", 32), ("gates", 32), ("half_r", 2)):
            at = sum(cols[c][1] for c in cols)
            cols[name] = (at, n)
        ss_at = sum(n for _, n in cols.values())

        def st(name, a=0, n=None):
            at, size = cols[name]
            return stat[:, at + a:at + (size if n is None else a + n)]

        jobs = {}
        at, n_act, n_dve = ss_at, 0, 0
        for name, width, eps, n, tokens in JOBS:
            if name.startswith("ret"):
                n_dve += 1
            else:
                n_act += n
            jobs[name] = (len(jobs), at, width, eps, n, n_act, n_dve, tokens)
            at += n + tokens
        assert at <= N_STAT, at

        logit = arena[:, 5120:5160].rearrange("p (t n) -> p t n", t=NT)
        r_em, r_oh = arena[:, 5160:5192], arena[:, 5192:5224]
        route_y, route_x, r_eq4 = st("route", 8, 2), st("route", 14, 8), st("route", 22, 8)

        def ss(name, a):
            return stat[:, jobs[name][1] + a:jobs[name][1] + a + 1]

        def rstd(name, t):
            if name not in jobs:
                name, t = f"{name}.{t}", 0
            at = jobs[name][1] + jobs[name][4] + t
            return stat[:, at:at + 1]

        landed = [sem(f"unit_landed{s}") for s in range(NSLOT)]
        hi_ready = sem("unit_hi_ready")
        lo_ready = sem("unit_lo_ready")
        used = sem("units_used")
        evac = {"act": sem("blocks_evacuated_by_act"), "dve": sem("blocks_evacuated_by_dve")}
        turned = sem("turn_bank_filled")
        freed = {"act": sem("turn_bank_freed_by_act"), "dve": sem("turn_bank_freed_by_dve")}
        turn_hi = sem("turned_hi_ready")
        consts_in = sem("constants_landed")
        x_in = sem("x_landed")
        rows_in = [sem(f"rows{r}_landed") for r in range(3)]
        mod_clear = sem("modulation_rows_cleared")
        pool_rows_in = [sem(f"second_rows{r}_landed") for r in range(2)]
        bias_in = sem("b_ada_landed")
        ada_in = [sem(f"ada_weights{n}_landed") for n in range(8)]
        ada_done = sem("ada_products_accumulated")
        tables_in = sem("tables_landed")
        one_hot_in = sem("bucket_choice_landed")
        rows_used = sem("gain_rows_used")
        merged = sem("merged_rows_ready")
        dve_ret = sem("retention_rows_ready")
        tanh_ready = sem("gates_tanh_ready")
        sq_act = sem("squares_by_act")
        var_dve = sem("variances_by_dve")
        rstd_ready = sem("rstd_ready")
        silu_c = sem("silu_c_ready")
        half_ready = sem("half_rstd_ready")
        tables_ready = sem("rotation_tables_ready")
        angles = sem("angles_ready")
        sines = sem("sines_ready")
        lam_in = sem("lambda_products_ready")
        lam_exp = sem("lambda_exponentials_ready")
        x_ready = sem("residual_updated")
        xn_ready = sem("normalised_rows_ready")
        lat_ready = sem("normalised_latents_ready")
        roped_qk = sem("rotations_by_pool_ready")
        roped = sem("rotations_ready")
        scored = sem("attention_scores_ready")
        masked = sem("row_maxima_ready")
        expd = sem("exponentials_ready")
        mixed = sem("row_normalisers_ready")
        copied = sem("biased_scores_ready")
        ret_scored = sem("retention_scores_ready")
        decay = sem("retention_decays_ready")
        decayed = sem("decayed_scores_ready")
        idx_scored = sem("index_scores_ready")
        relud = sem("index_scores_rectified")
        idx_acc = sem("index_scores_summed")
        pairs_ready = sem("doubled_keys_ready")
        bv_in = sem("relative_rows_stored")
        rel_in = [sem(f"relative_tile{n}_landed") for n in range(2)]
        bm_ready = sem("biased_mask_ready")
        mask_ready = sem("selection_ready")
        silud = sem("silu_ready")
        hid_ready = sem("hidden_ready")
        route_hi = sem("router_hi_ready")
        route_lo = sem("router_lo_ready")
        route_in = sem("router_exponents_wanted")
        route_e = sem("router_exponentials_ready")
        first_rows = sem("sums_of_first_token_block")
        routed = sem("router_logits_ready")
        dve_step = sem("dve_step")
        act_step = sem("act_step")
        pool_step = sem("pool_step")
        stored = sem("output_stored")

        block = ctx.enter_context(nc.Block())

        def row_source(name):
            v = ins[name]
            return bass.AP(v.tensor, 0, [[0, P], [1, D]])

        def k_tiles(name):
            return ins[name][0].rearrange("(k p) n -> p k n", p=P)

        IN1 = [(n * W, W) for n in range(6)] + [(QKV_W, W), (QKV_W + W, C_W - W)] \
            + [(QKV_W + C_W + n * W, W) for n in range(4)]
        LOADS = {}
        for n in range(12):
            LOADS[f"in{n}"] = ("w_in", *IN1[n], DK)
        for n in range(3):
            LOADS[f"uq{n}"] = ("w_uq", n * W, W, QR // P)
        for n in range(4):
            LOADS[f"ukv{n}"] = ("w_ukv", n * W, W, KVR // P)
            LOADS[f"gt{n}"] = ("w_gate_2", n * W, W, DK)
        for n in range(9):
            LOADS[f"jn{n}"] = ("w_in_2", n * W, min(W, IN2_W - n * W), DK)
        for n in range(2):
            LOADS[f"pa{n}"] = ("w_proj_a", n * W, W, DK)
            LOADS[f"pb{n}"] = ("w_proj_b", n * W, W, DK)
            LOADS[f"wo{n}"] = ("w_o", n * W, W, DK)
            LOADS[f"ro{n}"] = ("w_ret_out_2", n * W, W, DK)
            LOADS[f"do{n}"] = ("w_dsa_out_2", n * W, W, DK // 2)
            LOADS[f"xo{n}"] = ("w_o_2", n * W, W, DK)

        @block.sync
        def _(sp):
            def free_slot(u, shift=0, looped=False):
                if u >= NSLOT or looped:
                    sp.wait_ge(lo_ready, u - NSLOT + 1 + shift)

            def load(name, col=None, shift=0, first=None, looped=False):
                weight, c0, width, nk = LOADS[name]
                u = BLOCKS[name][1] if first is None else first
                src = k_tiles(weight)
                for part in range(-(-nk // UK)):
                    n = min(UK, nk - part * UK)
                    free_slot(u, shift, looped)
                    where = slice(c0, c0 + width) if col is None else bass.ds(col, width)
                    dst = raw[:, u % NSLOT, :].rearrange("p (k n) -> p k n", k=UK)[:, 0:n, 0:width]
                    sp.dma_start(dst, src[:, part * UK:part * UK + n, where]).then_inc(landed[u % NSLOT], 16)
                    u += 1

            def load_slice(u, e, moe, down, shift=0):
                if not down:
                    for half in range(2):
                        for w in ("w_exp_gate_2", "w_exp_up_2") if moe else ("w_ffn_gate", "w_ffn_up"):
                            free_slot(u, shift)
                            if moe:
                                src = ins[w][0, bass.ds(e, 1)].rearrange("e (k p) n -> p (e k) n", p=P)
                                src = src[:, 4 * half:4 * half + 4, :]
                            else:
                                src = k_tiles(w)[:, 4 * half:4 * half + 4, bass.ds(e * EW, EW)]
                            sp.dma_start(raw[:, u % NSLOT, :].rearrange("p (k n) -> p k n", k=4), src)\
                              .then_inc(landed[u % NSLOT], 16)
                            u += 1
                else:
                    for k in range(2):
                        free_slot(u, shift)
                        if moe:
                            src = ins["w_exp_down_2"][0, bass.ds(e, 1)].rearrange("e f n -> (e f) n")
                            src = src[k * P:(k + 1) * P, :]
                        else:
                            src = ins["w_ffn_down"][0, bass.ds(e * EW + k * P, P), :]
                        sp.dma_start(raw[:, u % NSLOT, :], src).then_inc(landed[u % NSLOT], 16)
                        u += 1
                return u

            def load_mlp(name, n, moe):
                u = load_slice(BLOCKS[name][1], 0, moe, False)
                u = load_slice(u, 1, moe, False)
                u = load_slice(u, 0, moe, True)
                pairs = (n - 3) // 2
                with sp.Fori(0, pairs) as i:
                    for j in range(2):
                        load_slice(u + 6 * j, i * 2 + (2 + j), moe, False, i * 12)
                        load_slice(u + 6 * j + 4, i * 2 + (1 + j), moe, True, i * 12)
                u += 12 * pairs
                for e in range(1 + 2 * pairs, n):
                    if e + 1 < n:
                        u = load_slice(u, e + 1, moe, False)
                    u = load_slice(u, e, moe, True)

            sp.dma_start(x[:, 0, :], ins["x"][0, 0:P, :]).then_inc(x_in, 16)
            sp.dma_start(rows[:, 0, :], row_source("ln_mix_pre")).then_inc(rows_in[0], 16)
            sp.dma_start(x[:, 1, :], ins["x"][0, P:S, :]).then_inc(x_in, 16)
            load("in0")
            load("in1")
            with sp.Fori(1, 3) as i:
                for j in range(2):
                    load("in0", i * (2 * W) + j * W, i * 8, BLOCKS["in0"][1] + 4 * j, True)
            for name in BLOCK_NAMES[BLOCK_NAMES.index("in6"):BLOCK_NAMES.index("pb1") + 1]:
                load(name)
            sp.dma_start(rows[:, 1, :], row_source("ln_mix_post")).then_inc(rows_in[1], 16)
            sp.wait_ge(roped_qk, 1)
            sp.dma_start(rows[:, 2, :], row_source("ln_ffn_pre")).then_inc(rows_in[2], 16)
            sp.dma_start(rows[:, 3, :], row_source("ln_ffn_post")).then_inc(rows_in[2], 16)
            load("wo0")
            load("wo1")
            load_mlp("FFN", N_FFN, False)
            with sp.Fori(0, 4) as i:
                for j in range(2):
                    load("jn0", i * (2 * W) + j * W, i * 8, BLOCKS["jn0"][1] + 4 * j)
            load("jn8")
            sp.wait_ge(rows_used, 4)
            gate_src = bass.AP(ins["b_gate_2"].tensor, 0, [[0, P], [1, 2 * D]])
            sp.dma_start(rows[:, 2:4, :].rearrange("p a n -> p (a n)"), gate_src).then_inc(rows_in[2], 16)
            for n in range(4):
                load(f"gt{n}")
            sp.wait_ge(rows_used, 6)
            sp.dma_start(rows[:, 0, :], row_source("norm_ffn_g_2")).then_inc(rows_in[0], 16)
            sp.dma_start(rows[:, 1, :], row_source("norm_final_g_2")).then_inc(rows_in[1], 16)
            for name in ("ro0", "ro1", "do0", "do1", "xo0", "xo1"):
                load(name)
            load_mlp("MOE", N_EXP, True)
            out_d = out[0].rearrange("(t p) n -> p t n", p=P)
            for t in range(NT):
                sp.wait_ge(xn_ready, 4 * NT + t + 1)
                sp.dma_start(out_d[:, t, :], xn[:, t, :]).then_inc(stored, 16)
            sp.wait_ge(stored, 16 * NT)

        def rotate(engine, step, temp, v, cos, sin, nsin, groups):
            def over(table, *dims):
                return bass.AP(table.tensor, table.offset, [table.ap[0]] + [[0, n] for n in dims] + [[1, 32]])
            n = groups * 64
            by_cos = temp[:, 0, 0:n].rearrange("p (g a n) -> p g a n", g=groups, a=2)
            by_sin = temp[:, 1, 0:n].rearrange("p (g a n) -> p g a n", g=groups, a=2)
            step.mark(engine.tensor_tensor(by_cos, v, over(cos, groups, 2), ALU.mult))
            step.mark(engine.tensor_tensor(by_sin[:, :, 0, :], v[:, :, 1, :], over(nsin, groups), ALU.mult))
            step(engine.tensor_tensor(by_sin[:, :, 1, :], v[:, :, 0, :], over(sin, groups), ALU.mult))
            step(engine.tensor_tensor(v, by_cos, by_sin, ALU.add))

        def ada_slots(g):
            return [carve(at1 + n * D, D)[0] for n in range(8)] if g < 2 else [carve(5632 + n * D, D)[0] for n in range(4)]

        @block.gpsimd
        def _(pool):
            pool.dma_start(cst[:, :], consts).then_inc(tables_in, 16)
            with nc.allow_non_contiguous_dma(reason="a column a K tile, a position a partition"):
                pool.dma_start(probs[:, 0, 0, 0:DK], ins["c_2"].rearrange("a (k p) -> p (a k)", p=P))\
                    .then_inc(consts_in, 16)
                pool.dma_start(pos_i[:, :], ins["positions"].rearrange("a (t p) -> p (a t)", p=P))\
                    .then_inc(consts_in, 16)
            pool.dma_start(small[:, :], bass.AP(small_d.tensor, 0, [[0, P], [1, SM_END]])).then_inc(consts_in, 16)
            pool.dma_start(probs[:, 1, 0, 0:S], bass.AP(lambda_d.tensor, 0, [[0, P], [1, S]])).then_inc(consts_in, 16)
            pool.dma_start(router[:, :, :], router_d.rearrange("(k p) n -> p k n", p=P)).then_inc(consts_in, 16)
            pool.dma_start(rel_bias[:, :], ins["rel_bias_2"]).then_inc(consts_in, 16)
            pool.dma_start(kv_up[:, :], ins["w_dsa_kv_up_2"][0]).then_inc(consts_in, 16)
            step = Counted(pool, pool_step)
            step(pool.memset(st("neg_half"), -0.5))
            pool.memset(ones[:, :], 1.0).then_inc(mod_clear, 1)

            def clear_rows(n, c):
                pool.memset(mod[:, c], 0.0).then_inc(mod_clear, 1)
                pool.wait_ge(mod_clear, n)
                pool.dma_start(mod[0:1, c], ins["b_ada_2"][:, c]).then_inc(bias_in, 16)
                pool.wait_ge(bias_in, 16 * (n - 1))

            def ada_source(k, c):
                return ins["w_ada_2"][0, k * P:(k + 1) * P, c]

            def norm_job(name):
                number, at, width, eps, n, n_act, n_dve, tokens = jobs[name]
                source = stat[:, at:at + tokens]
                if name.startswith("ret"):
                    pool.wait_ge(var_dve, n_dve)
                    source = stat[:, at + 1:at + 4:2]
                else:
                    pool.wait_ge(sq_act, n_act)
                    if n > tokens:
                        step(pool.tensor_tensor(st("ms", 2, 1), stat[:, at:at + 1], stat[:, at + 1:at + 2], ALU.add))
                        source = st("ms", 2, 1)
                ms = st("ms", 0, tokens)
                step(pool.tensor_scalar(ms, source, 1.0 / width, eps, ALU.mult, ALU.add))
                pool.tensor_tensor(stat[:, at + n:at + n + tokens], ms, st("neg_half", 0, tokens), ALU.pow)\
                    .then_inc(rstd_ready, 1)
                pool.wait_ge(rstd_ready, number + 1)

            def norm_jobs(first, last):
                for name in JOB_NAMES[JOB_NAMES.index(first):JOB_NAMES.index(last) + 1]:
                    norm_job(name)

            norm_jobs("x1", "x1")
            pool.tensor_scalar(st("half_r"), stat[:, jobs["x1"][1] + 2:jobs["x1"][1] + 4], 0.5, None, ALU.mult)\
                .then_inc(half_ready, 1)
            clear_rows(2, slice(0, 2 * D))
            for n in range(2 * DK):
                if n >= 8:
                    pool.wait_ge(ada_done, n - 7)
                pool.dma_start(ada_slots(0)[n % 8], ada_source(n % DK, slice(n // DK * D, (n // DK + 1) * D)))\
                    .then_inc(ada_in[n % 8], 16)
            pool.wait_ge(tables_ready, 1)
            in_rows = rows[:, 2, :].rearrange("p (a n) -> p a n", a=2)
            for n in range(4):
                pool.wait_ge(evac["act"], n + 1)
                for t in range(NT):
                    rotate(pool, step, in_rows, qkv[:, t, n * W:(n + 1) * W].rearrange("p (g a n) -> p g a n", g=8, a=2),
                           trig[:, 0, t, :], trig[:, 1, t, :], trig[:, 2, t, :], 8)
            pool.nop().then_inc(roped_qk, 1)
            norm_jobs("cq", "x2")
            pool.wait_ge(rows_used, 3)
            pool.dma_start(rows[:, 0, :], row_source("norm_mix_g_2")).then_inc(pool_rows_in[0], 16)
            pool.dma_start(rows[:, 1, :], row_source("ret_gn_g_2")).then_inc(pool_rows_in[1], 16)
            pool.wait_ge(turned, TURNS["mg.3"][0] + 1)
            clear_rows(3, slice(2 * D, 6 * D))
            with pool.Fori(0, 4) as i:
                for k in range(DK):
                    pool.wait_ge(ada_done, i * DK + (2 * DK + k - 3))
                    pool.dma_start(ada_slots(2)[k % 4], ada_source(k, bass.ds(i * D + 2 * D, D)))\
                        .then_inc(ada_in[k % 4], 16)
            pool.dma_start(mix[0:BUCKETS, :], one_hot_d).then_inc(one_hot_in, 16)
            norm_jobs("ffn.0", "u.1")
            pool.wait_ge(freed["act"], TURNS["bv"][2])
            row = probs[0:HEADS, 1, 0, :]
            pool.dma_start(rel_rows, bass.AP(row.tensor, row.offset, [row.ap[0], [0, P], row.ap[1]])).then_inc(bv_in, 16)
            pool.wait_ge(x_ready, 2 * NT)
            for n in range(2):
                pool.wait_ge(evac["act"], BLOCKS["jn0"][4] + n)
                for t in range(NT):
                    rotate(pool, step, tmp, zz[:, t, n * W:(n + 1) * W].rearrange("p (g a n) -> p g a n", g=8, a=2),
                           cst[:, C_COS2 + 32 * t:C_COS2 + 32 * t + 32], cst[:, C_SIN2 + 32 * t:C_SIN2 + 32 * t + 32],
                           trig[:, 3, t, :], 8)
            pool.nop().then_inc(roped_qk, 1)
            norm_jobs("lt", "ret7")
            pool.wait_ge(bv_in, 16)

            def load_rel(h):
                n = h % 2
                b0 = bass.AP(rel_rows.tensor, h * P * REL_W + S - 1, [[REL_W - 1, P], [1, P]])
                b1 = bass.AP(rel_rows.tensor, h * P * REL_W + P - 1, [[REL_W - 1, P], [1, S]])
                pool.dma_start(rel_b[n][:, 0:P], b0).then_inc(rel_in[n], 16)
                pool.dma_start(rel_b[n][:, P:SC_W], b1).then_inc(rel_in[n], 16)

            load_rel(0)
            load_rel(1)
            pool.wait_ge(mask_ready, 1)
            for h in range(HEADS):
                pool.wait_ge(rel_in[h % 2], 32 * (h // 2 + 1))
                if h >= 2:
                    pool.wait_ge(copied, h - 1)
                pool.tensor_tensor(probs[:, h % 2, 1, :], rel_b[h % 2], sel_mask, ALU.add).then_inc(bm_ready, 1)
                if h + 2 < HEADS:
                    pool.wait_ge(bm_ready, h + 1)
                    load_rel(h + 2)
            norm_jobs("v.0", "fin.1")

        @block.scalar
        def _(act):
            split_at = [0]
            unit_at = [0]
            sq_at = [0]

            def split(u, shift=0, looped=False):
                s = u % NSLOT
                act.wait_ge(landed[s], 16 * (u // NSLOT + 1) + shift * 4)
                if u >= NSLOT or looped:
                    act.wait_ge(used, u - NSLOT + 1 + shift)
                act.activation(w_hi[:, s, :], raw[:, s, :], ACT.Copy).then_inc(hi_ready, 1)

            def split_to(n):
                while split_at[0] < min(n, N_UNITS):
                    split(split_at[0])
                    split_at[0] += 1

            def fill(n, until=None):
                end = unit_at[0] + n if until is None else BLOCKS[until][1] + BLOCKS[until][2]
                while unit_at[0] < end:
                    split_to(unit_at[0] + LEAD + 1)
                    unit_at[0] += 1
                    for name in BLOCK_NAMES:
                        if BLOCKS[name][1] + BLOCKS[name][2] == unit_at[0]:
                            if BLOCKS[name][3] == "act":
                                evacuate(name)
                            elif name[:2] == "gt":
                                gate_tanh(name)

            def evacuate(name):
                number, u0, units, _, _ = BLOCKS[name]
                act.wait_ge(used, u0 + units)
                bank = 2 * (number % 2)
                kind, n = name[:2], int(name[2:])
                for t in range(NT):
                    if kind == "in" and n >= 8:
                        c = (n - 8) * W
                        i = act.activation(gate1[:, t, c:c + W], lin[:, bank + t, :], ACT.Tanh,
                                           scale=st("half_r", t, 1))
                    elif kind == "in":
                        c, w = (n - 6) * W, IN1[n][1]
                        i = act.activation(lat[:, t, c:c + w], lin[:, bank + t, 0:w], ACT.Copy, scale=rstd("x1", t))
                    elif kind == "uq":
                        i = act.activation(qb[:, t, n * W:(n + 1) * W], lin[:, bank + t, :], ACT.Copy)
                    else:
                        w = LOADS[name][2]
                        i = act.activation(zz[:, t, n * W:n * W + w], lin[:, bank + t, 0:w], ACT.Copy)
                i.then_inc(evac["act"], 1)

            def gate_tanh(name):
                n = int(name[2:])
                act.wait_ge(evac["dve"], BLOCKS[name][4])
                g = gate2[:, :, n * W:(n + 1) * W]
                act.activation(g, g, ACT.Tanh, scale=0.5).then_inc(tanh_ready, 1)

            def block_loop(first, pairs, target, scale=lambda t: 1.0):
                number, u0, units, _, _ = BLOCKS[first]
                assert u0 + LEAD <= split_at[0] <= u0 + 4 and unit_at[0] == u0

                def pair(i, looped):
                    for j in range(2):
                        for k in range(4):
                            u = u0 + LEAD + 4 * j + k
                            if looped or u >= split_at[0]:
                                split(u, i * 8, looped)
                        act.wait_ge(used, i * 8 + (u0 + 4 * j + 4))
                        act.nop()
                        bank = 2 * ((number + j) % 2)
                        for t in range(NT):
                            e = act.activation(target[:, t, bass.ds(i * (2 * W) + j * W, W)],
                                               lin[:, bank + t, :], ACT.Copy, scale=scale(t))
                        e.then_inc(evac["act"], 1)

                pair(0, False)
                with act.Fori(1, pairs) as i:
                    pair(i, True)
                split_at[0] = u0 + LEAD + 8 * pairs
                unit_at[0] += 8 * pairs

            def bank_of(name):
                return turn[:, TURNS[name][0] % 2, :]

            def turned_hi(name, hi, k0, nk, scale=1.0):
                act.wait_ge(turned, TURNS[name][0] + 1)
                src = bank_of(name)[:, 0:nk * S].rearrange("p (k n) -> p k n", k=nk)
                act.activation(hi[:, k0:k0 + nk, :], src, ACT.Copy, scale=scale).then_inc(turn_hi, 1)

            def rows_hi(label, t):
                for g in (2 * t, 2 * t + 1):
                    act.wait_ge(turned, TURNS[f"{label}.{g}"][0] + 1)
                    act.activation(a_hi[:, 4 * (g % 2):4 * (g % 2) + 4, t * P:(t + 1) * P],
                                   bank_of(f"{label}.{g}").rearrange("p (k n) -> p k n", k=4), ACT.Copy)\
                        .then_inc(turn_hi, 1)

            def turned_copy(name, targets):
                act.wait_ge(turned, TURNS[name][0] + 1)
                for dst, src, scale in targets:
                    i = act.activation(dst, src, ACT.Copy, scale=scale)
                i.then_inc(freed["act"], 1)

            def squares(name, sources):
                for a, src in enumerate(sources):
                    n = src.shape[-1]
                    if sq_at[0]:
                        act.wait_ge(sq_act, sq_at[0])
                    sq_at[0] += 1
                    act.activation(act_junk[:, 0:n], src, ACT.Square, accum_out=ss(name, a)).then_inc(sq_act, 1)

            def exps(n, comps):
                act.wait_ge(masked, n + 1)
                if n >= 2:
                    act.wait_ge(mixed, n - 1)
                for j in range(comps):
                    for t in range(NT):
                        c = slice(0, P) if t == 0 else slice(P, SC_W)
                        k = 4 * (n % 2) + 2 * t + j
                        dst = probs[:, n % 2, j, c]
                        if comps == 2:
                            src = sco[:, j, c]
                        elif n < 2 * HEADS:
                            src = sco[:, n % 2, c]
                        else:
                            src = dst
                        i = act.activation(dst, src, ACT.Exp, bias=st("nmax", k, 1), accum_out=st("rsum", k, 1))
                i.then_inc(expd, 1)

            def probs_out(name, i, before):
                if i >= 2:
                    act.wait_ge(turned, TURNS[f"{before}{i - 2}"][0] + 1)
                turned_copy(name, [(probs_t[:, i % 2, :], bank_of(name)[:, 0:SC_W], 1.0)])

            split_to(1)
            rows_hi("x1", 0)
            split_to(4)
            rows_hi("x1", 1)
            act.wait_ge(x_in, 16 * NT)
            squares("x1", [x[:, t, :] for t in range(NT)])
            act.wait_ge(consts_in, 112)
            act.activation(c_col[:, :], probs[:, 0, 0, 0:DK], ACT.Silu).then_inc(silu_c, 1)
            act.activation(router_hi[:, :, :], router[:, :, :], ACT.Copy).then_inc(route_hi, 1)
            act.wait_ge(angles, 1)
            act.activation(trig[:, 0:2, :, :].rearrange("p a t n -> p (a t n)"), mix[:, 0:P], ACT.Sin)\
                .then_inc(sines, 1)
            act.wait_ge(lam_in, 1)
            act.activation(st("lam", 2, 2), st("lam", 0, 2), ACT.Exp).then_inc(lam_exp, 1)
            act.wait_ge(rstd_ready, 1)
            act.wait_ge(half_ready, 1)
            block_loop("in0", 3, qkv, lambda t: rstd("x1", t))
            act.wait_ge(ada_done, 2 * DK)
            fill(0, "in7")
            squares("cq", [lat[:, t, 0:QR] for t in range(NT)])
            squares("ckv", [lat[:, t, QR:QR + KVR] for t in range(NT)])

            def ada_out(n0, n1):
                for n in range(n0, n1):
                    turned_copy(f"ad{n}", [(mod[:, n * W:(n + 1) * W], bank_of(f"ad{n}"), 1.0)])

            def q_and_k_out(name, h, scale):
                b = bank_of(name)
                turned_copy(name, [(qk_t[:, h, 0:S], b[:, 0:S], scale), (qk_t[:, h, S:2 * S], b[:, S:2 * S], 1.0)])

            q_and_k_out("qk0", 0, DA_HD ** -0.5)
            q_and_k_out("qk1", 1, DA_HD ** -0.5)
            turned_hi("cl.0", b_hi, 0, 2)
            turned_hi("cl.1", b_hi, 2, 2)
            turned_hi("cl.2", b_hi, 4, 1)
            for i in range(HEADS + 2):
                if i + 2 < HEADS:
                    q_and_k_out(f"qk{i + 2}", i + 2, DA_HD ** -0.5)
                fill(DA_FILL[i][0])
                if i < HEADS:
                    exps(i, 2)
                fill(DA_FILL[i][1])
                if 1 <= i <= HEADS:
                    probs_out(f"dap{i - 1}", i - 1, "dao")
                if i >= 2:
                    act.wait_ge(turned, TURNS[f"dao{i - 2}"][0] + 1)
                    squares(f"da{i - 2}", [bank_of(f"dao{i - 2}")[:, P * t:P * t + P] for t in range(NT)])
                fill(DA_FILL[i][2])
            ada_out(0, 4)
            for g in range(4):
                turned_hi(f"oa.{g}", a_hi, 2 * g, 2)

            scale = MLA_QK ** -0.5
            for g in range(4):
                b = bank_of(f"mr{g}")
                turned_copy(f"mr{g}", [(qr_t[2 * g + a], b[0:ROPE, a * S:(a + 1) * S], scale) for a in range(2)])
            turned_copy("kr", [(kr_t, bank_of("kr")[0:ROPE, 0:S], 1.0)])
            q_and_k_out("mq0", 0, scale)
            q_and_k_out("mq1", 1, scale)
            for i in range(HEADS + 2):
                if i + 2 < HEADS:
                    q_and_k_out(f"mq{i + 2}", i + 2, scale)
                if i < HEADS:
                    exps(HEADS + i, 1)
                fill(MLA_FILL[i])
                if 1 <= i <= HEADS:
                    probs_out(f"mp{i - 1}", i - 1, "mo")
            for g in range(4):
                turned_hi(f"ob.{g}", a_hi, 2 * g, 2)
            fill(0, "pb1")
            for g in range(4):
                turned_hi(f"mg.{g}", a_hi, 2 * g, 2, 0.5)
            fill(0, "wo0")
            u_next = BLOCKS["FFN"][1]
            split_to(u_next)
            banks = [2 * (BLOCKS[f"wo{n}"][0] % 2) for n in range(2)]
            act.wait_ge(first_rows, 1)
            squares("wo.0", [lin[:, b, :] for b in banks])
            split_to(u_next + LEAD)
            act.wait_ge(used, u_next)
            squares("wo.1", [lin[:, b + 1, :] for b in banks])
            unit_at[0] = u_next
            split_to(u_next + 4)
            rows_hi("x2", 0)
            rows_hi("x2", 1)
            act.wait_ge(x_ready, NT)
            squares("x2", [x[:, t, :] for t in range(NT)])

            def silu_step(scale, u_end, shift=0):
                act.wait_ge(used, u_end + shift)
                for t in range(NT):
                    act.activation(act_s[:, t, :], lin[:, t, 0:EW], ACT.Silu, scale=scale(t)).then_inc(silud, 1)

            def mlp(name, label, n, scale=lambda t: 1.0):
                u = BLOCKS[name][1]
                turn0 = TURNS[f"{label}0"][0]
                assert split_at[0] in (u + LEAD, u + 4)
                split_to(u + 6)
                silu_step(scale, u + 4)
                split_to(u + 4 + LEAD)
                u += 4

                def one(e, u, last=False, shift=0, shift_e=0):
                    act.wait_ge(turned, turn0 + e + 1 + shift_e)
                    act.activation(b_hi[:, 0:2, :], turn[:, 0, :].rearrange("p (k n) -> p k n", k=2), ACT.Copy)\
                        .then_inc(turn_hi, 1)
                    for j in range(1 if last else 6):
                        if j == 3:
                            silu_step(scale, u + 4, shift)
                        if u + LEAD + j < N_UNITS:
                            split(u + LEAD + j, shift)

                one(0, u)
                u += 6
                pairs = (n - 3) // 2
                with act.Fori(0, pairs) as i:
                    for j in range(2):
                        one(1 + j, u + 6 * j, False, i * 12, i * 2)
                u += 12 * pairs
                for e in range(1 + 2 * pairs, n):
                    one(e, u, e == n - 1)
                    u += 2 if e == n - 1 else 6
                split_at[0] = min(u + LEAD - 1, N_UNITS)
                unit_at[0] = u

            act.wait_ge(rstd_ready, jobs["x2"][0] + 1)
            mlp("FFN", "ffn", N_FFN, lambda t: rstd("x2", t))
            act.wait_ge(first_rows, 2)
            squares("ffn.0", y_bank[0])
            u_next = BLOCKS["jn0"][1]
            split_to(u_next + LEAD)
            act.wait_ge(used, u_next)
            squares("ffn.1", y_bank[1])
            split_to(u_next + 4)
            for t in range(NT):
                act.wait_ge(x_ready, NT + t + 1)
                squares(f"u.{t}", [x[:, t, :]])
            turned_copy("bv", [(probs[0:HEADS, 1, 0, :], bank_of("bv")[0:HEADS, 0:SC_W], 1.0)])
            rows_hi("u", 0)
            rows_hi("u", 1)

            block_loop("jn0", 4, zz)
            act.wait_ge(evac["act"], BLOCKS["jn7"][4])
            squares("lt", [zz[:, t, DKV:DKV + P] for t in range(NT)])
            ada_out(4, 8)
            fill(0, "jn8")
            ada_out(8, 12)
            for t in range(NT):
                act.activation(gate2[:, t, 0:D], zz[:, t, RG:RG + D], ACT.Tanh, scale=0.5).then_inc(tanh_ready, 1)
            turned_copy("lt", [(idk_t[:, 0:S], bank_of("lt")[:, 0:S], 1.0)])
            b = bank_of("lat")[:, 0:S].rearrange("p (t n) -> p t n", t=NT)
            turned_copy("lat", [(zz[:, :, DKV:DKV + 64], b[:, :, 0:64], 1.0),
                                (zz[:, :, DKV + 64:DKV + 128], b[:, :, 0:64], 1.0),
                                (probs_t[:, :, 0:64], zz[:, :, IK:IK + 64], 1.0),
                                (probs_t[:, :, 64:128], zz[:, :, IK:IK + 64], 1.0),
                                (dv[:, :, :], b[:, :, 64:128], 1.0)])
            for g in range(4):
                turned_copy(f"rt{g}", [(rt_t[:, g, :], bank_of(f"rt{g}"), 1.0)])
            for g in range(5):
                name = f"dt{g}"
                dst = idk_t[:, :] if g == 4 else idq_t[:, 2 * g:2 * g + 2, :].rearrange("p a n -> p (a n)")
                turned_copy(name, [(dst, bank_of(name), 1.0)])

            pool_rows = 16
            act.wait_ge(bv_in, pool_rows)
            for i in range(HEADS + 1):
                if i < HEADS:
                    if i >= 2:
                        act.wait_ge(decayed, i - 1)
                    g = float(np.log(np.float32(1.0 - 2.0 ** (-5.0 - i))))
                    act.activation(probs[:, i % 2, 0, :], cst[:, C_DIST:C_DIST + SC_W], ACT.Exp, scale=g)\
                        .then_inc(decay, 1)
                fill(RET_FILL[i])
            act.wait_ge(decayed, HEADS)
            for i in range(HEADS):
                act.wait_ge(idx_scored, i + 1)
                if i >= 2:
                    act.wait_ge(idx_acc, i - 1)
                act.activation(probs[:, i % 2, 0, :], sco[:, i % 2, 0:SC_W], ACT.Relu).then_inc(relud, 1)
                fill(IDX_FILL[i])
            for g in range(4):
                turned_hi(f"re.{g}", a_hi, 2 * g, 2)
            fill(TOPK_FILL)
            for i in range(HEADS + 2):
                fill(DSA_FILL[i])
                if i < HEADS:
                    exps(2 * HEADS + i, 1)
                if 1 <= i <= HEADS:
                    probs_out(f"dsp{i - 1}", i - 1, "dso")
            turned_hi("de.0", b_hi, 0, 2)
            turned_hi("de.1", b_hi, 2, 2)
            fill(0, "do1")
            for g in range(4):
                turned_hi(f"mh.{g}", a_hi, 2 * g, 2, 0.5)
            fill(0, "xo0")
            u_next = BLOCKS["MOE"][1]
            split_to(u_next)
            act.wait_ge(x_ready, 2 * NT + 1)
            squares("v.0", [x[:, 0, :]])
            split_to(u_next + LEAD)
            act.wait_ge(x_ready, 2 * NT + 2)
            squares("v.1", [x[:, 1, :]])
            unit_at[0] = u_next
            split_to(u_next + 4)
            rows_hi("v", 0)
            rows_hi("v", 1)
            act.wait_ge(route_in, 1)
            act.activation(route_x, route_x, ACT.Exp).then_inc(route_e, 1)
            act.wait_ge(route_in, 2)
            act.activation(route_y, route_y, ACT.Exp).then_inc(route_e, 1)
            mlp("MOE", "moe", N_EXP)
            for t in range(NT):
                act.wait_ge(x_ready, 3 * NT + t + 1)
                squares(f"fin.{t}", [x[:, t, :]])

        @block.vector
        def _(dve):
            split_at = [0]
            unit_at = [0]
            step = Counted(dve, dve_step)

            def split(u, shift=0):
                s = u % NSLOT
                dve.wait_ge(hi_ready, u + 1 + shift)
                dve.tensor_tensor(w_lo[:, s, :], raw[:, s, :], w_hi[:, s, :].bitcast(F32), ALU.subtract)\
                   .then_inc(lo_ready, 1)

            def split_to(n):
                while split_at[0] < min(n, N_UNITS):
                    split(split_at[0])
                    split_at[0] += 1

            def fill(n, until=None):
                end = unit_at[0] + n if until is None else BLOCKS[until][1] + BLOCKS[until][2]
                while unit_at[0] < end:
                    split_to(unit_at[0] + LEAD + 1)
                    unit_at[0] += 1
                    for name in BLOCK_NAMES:
                        if BLOCKS[name][1] + BLOCKS[name][2] == unit_at[0] and BLOCKS[name][3] == "dve":
                            evacuate(name)

            def evacuate(name):
                number, u0, units, _, _ = BLOCKS[name]
                dve.wait_ge(used, u0 + units)
                bank = 2 * (number % 2)
                kind = name.rstrip("0123456789")
                n = int(name[len(kind):])
                c = slice(n * W, (n + 1) * W)
                done = evac["dve"]
                if kind == "ukv":
                    for t in range(NT):
                        i = dve.tensor_copy(kvb[t][:, c], lin[:, bank + t, :])
                    i.then_inc(done, 1)
                elif kind == "gt":
                    dve.wait_ge(rows_in[2], 48)
                    bias = rows[:, 2 + n // 2, (n % 2) * W:(n % 2) * W + W]
                    for t in range(NT):
                        i = dve.tensor_tensor(gate2[:, t, c], lin[:, bank + t, :], bias, ALU.add)
                    i.then_inc(done, 1)
                elif kind in ("pa", "ro"):
                    gate = gate1 if kind == "pa" else gate2
                    if kind == "ro":
                        dve.wait_ge(tanh_ready, NT + 4)
                    for t in range(NT):
                        i = dve.scalar_tensor_tensor(out=gate[:, t, c], in0=gate[:, t, c], scalar=1.0,
                                                     in1=lin[:, bank + t, :], op0=ALU.add, op1=ALU.mult)
                    i.then_inc(done, 1)
                elif kind in ("pb", "do"):
                    gate = gate1 if kind == "pb" else gate2
                    cb = slice(D + n * W, D + (n + 1) * W)
                    for t in range(NT):
                        i = dve.scalar_tensor_tensor(out=gate[:, t, cb], in0=gate[:, t, cb], scalar=1.0,
                                                     in1=lin[:, bank + t, :], op0=ALU.add, op1=ALU.mult)
                    i.then_inc(done, 1)
                    dve.wait_ge(done, BLOCKS[name][4])
                    for t in range(NT):
                        dve.tensor_tensor(gate[:, t, c], gate[:, t, c], gate[:, t, cb], ALU.add).then_inc(merged, 1)
                elif kind == "wo":
                    pass
                else:
                    for t in range(NT):
                        gated_rows(n, t, done if t == NT - 1 else None)

            def gated_rows(n, t, done):
                c = slice(n * W, (n + 1) * W)
                bank = 2 * (BLOCKS[f"xo{n}"][0] % 2)
                dve.wait_ge(freed["act"], TURNS["ad5"][2])
                step(dve.tensor_tensor(tmp[:, 0, :], lin[:, bank + t, :], mod[:, 2 * D + n * W:2 * D + (n + 1) * W],
                                       ALU.mult))
                i = dve.tensor_tensor(x[:, t, c], x[:, t, c], tmp[:, 0, :], ALU.add)
                if done is None:
                    step(i)
                else:
                    i.then_inc(done, 1)

            def ada_part(g0, i, k):
                slots = ada_slots(g0)
                n_s = len(slots)
                before = 32 if g0 else 0
                dve.wait_ge(ada_in[k % n_s], i * (16 * DK // n_s) + (before + 16 * (k // n_s + 1)))
                if k:
                    dve.wait_ge(ada_done, i * DK + (g0 * DK + k))
                acc = mod[:, bass.ds(i * D + g0 * D, D)]
                dve.scalar_tensor_tensor(out=acc, in0=slots[k % n_s], scalar=c_col[:, k:k + 1], in1=acc,
                                         op0=ALU.mult, op1=ALU.add).then_inc(ada_done, 1)

            def block_loop(first, pairs, beside=None):
                u0 = BLOCKS[first][1]
                assert u0 + LEAD <= split_at[0] <= u0 + 4 and unit_at[0] == u0
                for k in range(8):
                    if u0 + LEAD + k >= split_at[0]:
                        split(u0 + LEAD + k)
                with dve.Fori(1, pairs) as i:
                    for k in range(8):
                        split(u0 + LEAD + k, i * 8)
                        if beside is not None:
                            beside(i - 1, k)
                split_at[0] = u0 + LEAD + 8 * pairs
                unit_at[0] += 8 * pairs

            def bank_of(name):
                return turn[:, TURNS[name][0] % 2, :]

            turn_pairs = [0]

            def turned_lo(name, hi, lo, k0, nk, scale=None):
                turn_pairs[0] += 1
                dve.wait_ge(turn_hi, turn_pairs[0])
                src = bank_of(name)[:, 0:nk * S].rearrange("p (k n) -> p k n", k=nk)
                up = hi[:, k0:k0 + nk, :].bitcast(F32)
                if scale is None:
                    i = dve.tensor_tensor(lo[:, k0:k0 + nk, :], src, up, ALU.subtract)
                else:
                    flat = "p k n -> p (k n)"
                    i = dve.scalar_tensor_tensor(out=lo[:, k0:k0 + nk, :].rearrange(flat), in0=src.rearrange(flat),
                                                 scalar=scale, in1=up.rearrange(flat), op0=ALU.mult,
                                                 op1=ALU.subtract)
                i.then_inc(freed["dve"], 1)

            def rows_lo(label, t):
                for g in (2 * t, 2 * t + 1):
                    turn_pairs[0] += 1
                    dve.wait_ge(turn_hi, turn_pairs[0])
                    part = (slice(None), slice(4 * (g % 2), 4 * (g % 2) + 4), slice(t * P, (t + 1) * P))
                    dve.tensor_tensor(a_lo[part], bank_of(f"{label}.{g}").rearrange("p (k n) -> p k n", k=4),
                                      a_hi[part].bitcast(F32), ALU.subtract).then_inc(freed["dve"], 1)

            def wait_norm(name):
                dve.wait_ge(rstd_ready, jobs[name][0] + 1)

            def rotate1(v, t, groups):
                rotate(dve, step, tmp, v, trig[:, 0, t, :], trig[:, 1, t, :], trig[:, 2, t, :], groups)

            def row_maxima(n, comps):
                dve.wait_ge(scored, n + 1)
                b = slice(0, 2) if comps == 2 else slice(n % 2, n % 2 + 1)
                late = sco[0:CHUNK, b, :].rearrange("p j (b c) -> p j b c", c=S)[:, :, :, CHUNK:P]
                step(dve.memset(late, NEG))
                maxima(n, comps, sco[:, b, 0:SC_W])

            def maxima(n, comps, s):
                k = 4 * (n % 2)
                for t in range(NT):
                    c = slice(0, P) if t == 0 else slice(P, SC_W)
                    i = dve.tensor_reduce(st("nmax", k + 2 * t, comps), s[:, :, c], AX.X, ALU.max, negate=True)
                i.then_inc(masked, 1)

            def head_scaled(name, n, dst, width):
                dve.wait_ge(mixed, n + 1)
                dve.wait_ge(turned, TURNS[name][0] + 1)
                b = bank_of(name)
                for t in range(NT):
                    i = dve.tensor_scalar(dst(t), b[:, width * t:width * t + width],
                                          st("rinv", 4 * (n % 2) + 2 * t, 1), None, ALU.mult)
                i.then_inc(freed["dve"], 1)
                dve.wait_ge(freed["dve"], TURNS[name][2])

            def row_sums(n):
                dve.wait_ge(expd, n + 1)
                k = 4 * (n % 2)
                dve.reciprocal(st("rinv", k, 4)[:, 0:4:2], st("rsum", k, 4)[:, 0:4:2]).then_inc(mixed, 1)

            def gained(t, gain):
                return dve.tensor_tensor(xn[:, t, :], x[:, t, :], gain, ALU.mult)

            def modulated(name, t, shift):
                wait_norm(f"{name}.{t}")
                dve.scalar_tensor_tensor(out=xn[:, t, :], in0=xn[:, t, :], scalar=rstd(name, t), in1=shift,
                                         op0=ALU.mult, op1=ALU.add).then_inc(xn_ready, 1)

            def weighted(t, banks, gain, name=None):
                for n in range(2):
                    if name is not None:
                        dve.wait_ge(sq_act, jobs[f"{name}.{t}"][5] - 1 + n)
                    step.mark(dve.tensor_tensor(xn[:, t, n * W:(n + 1) * W], banks[n], gain[:, n * W:(n + 1) * W],
                                                ALU.mult))

            def add_normed(name, t):
                wait_norm(f"{name}.{t}")
                step.wait()
                dve.scalar_tensor_tensor(out=x[:, t, :], in0=xn[:, t, :], scalar=rstd(name, t), in1=x[:, t, :],
                                         op0=ALU.mult, op1=ALU.add).then_inc(x_ready, 1)

            dve.wait_ge(rows_in[0], 16)
            for t in range(NT):
                dve.wait_ge(x_in, 16 * NT)
                gained(t, rows[:, 0, :]).then_inc(xn_ready, 1)
            split_to(1)
            rows_lo("x1", 0)
            split_to(4)
            rows_lo("x1", 1)
            dve.wait_ge(xn_ready, NT)
            dve.nop().then_inc(rows_used, 1)
            dve.wait_ge(tables_in, 16)
            dve.wait_ge(consts_in, 112)
            step(dve.tensor_copy(st("pos"), pos_i[:, :]))
            half, two, whole = mix[:, 0:64], mix[:, 64:128], mix[:, 0:128]
            kmul = tmp[:, 0, 0:P]
            for t in range(NT):
                for a in range(2):
                    step.mark(dve.tensor_scalar(mix[:, 64 * a + 32 * t:64 * a + 32 * t + 32],
                                                cst[:, C_FREQ:C_FREQ + 32], st("pos", t, 1), None, ALU.mult))
            step.wait()
            step.mark(dve.tensor_scalar(kmul[:, 0:64], half, 1.0 / (2 * np.pi), 0.25, ALU.mult, ALU.add))
            step.mark(dve.tensor_scalar(kmul[:, 64:128], two, 1.0 / (2 * np.pi), None, ALU.mult))
            step.wait()
            step(dve.tensor_scalar(kmul, kmul, ROUND, None, ALU.add))
            step(dve.tensor_scalar(kmul, kmul, ROUND, None, ALU.subtract))
            for part in TWO_PI_PARTS:
                step(dve.scalar_tensor_tensor(out=whole, in0=kmul, scalar=-part, in1=whole, op0=ALU.mult,
                                              op1=ALU.add))
            step(dve.tensor_scalar(half, half, float(np.float32(np.pi / 2)), None, ALU.add))
            dve.tensor_scalar(whole, whole, 3.1415925, -3.1415925, ALU.min, ALU.max).then_inc(angles, 1)
            for a in range(2):
                lq, lk = (probs[:, 1, 0, 128 * a + 64 * b:128 * a + 64 * b + 64] for b in range(2))
                step(dve.tensor_tensor(tmp[:, 1, 0:64], lq, lk, ALU.mult))
                i = dve.tensor_reduce(st("lam", a, 1), tmp[:, 1, 0:64], AX.X, ALU.add)
                if a == 0:
                    step(i)
                else:
                    i.then_inc(lam_in, 1)
            dve.wait_ge(route_hi, 1)
            dve.tensor_tensor(router_lo[:, :, :], router[:, :, :], router_hi[:, :, :].bitcast(F32), ALU.subtract)\
               .then_inc(route_lo, 1)
            dve.wait_ge(sines, 1)
            step(dve.tensor_scalar(trig[:, 2, :, :], trig[:, 1, :, :], -1.0, None, ALU.mult))
            cst_sin2 = cst[:, C_SIN2:C_SIN2 + 64].rearrange("p (t n) -> p t n", t=NT)
            step(dve.tensor_scalar(trig[:, 3, :, :], cst_sin2, -1.0, None, ALU.mult))
            dve.nop().then_inc(tables_ready, 1)
            dve.wait_ge(lam_exp, 1)
            step(dve.tensor_tensor(st("lam", 4, 1), st("lam", 3, 1), st("lam", 2, 1), ALU.subtract))
            step(dve.tensor_scalar(st("lam", 5, 1), st("lam", 4, 1), -LAMBDA_INIT, None, ALU.add))
            step(dve.tensor_scalar(small[:, SM_DA:SM_DA + P], small[:, SM_DA:SM_DA + P], 1.0 - LAMBDA_INIT, None,
                                   ALU.mult))
            dve.wait_ge(silu_c, 1)
            dve.wait_ge(bias_in, 16)
            block_loop("in0", 3, lambda i, k: ada_part(0, i, k))

            fill(0, "in7")
            for name, at, n, gain in (("cq", 0, QR, SM_CQ), ("ckv", QR, KVR, SM_CKV)):
                wait_norm(name)
                for t in range(NT):
                    i = dve.scalar_tensor_tensor(out=lat[:, t, at:at + n], in0=lat[:, t, at:at + n],
                                                 scalar=rstd(name, t), in1=small[:, gain:gain + n], op0=ALU.mult,
                                                 op1=ALU.mult)
                    i.then_inc(lat_ready, 1)
            for t in range(NT):
                rotate1(lat[:, t, QR + KVR:C_W].rearrange("p (g a n) -> p g a n", g=1, a=2), t, 1)
            for g, nk in ((0, 2), (1, 2), (2, 1)):
                turned_lo(f"cl.{g}", b_hi, b_lo, 2 * g, nk)

            for i in range(HEADS + 2):
                fill(DA_FILL[i][0])
                if i < HEADS:
                    row_maxima(i, 2)
                fill(DA_FILL[i][1])
                if i < HEADS:
                    dve.wait_ge(expd, i + 1)
                    k, h = 4 * (i % 2), i % 2
                    step(dve.reciprocal(st("rinv", k, 4), st("rsum", k, 4)))
                    step(dve.tensor_scalar(st("rinv", k, 4)[:, 1:4:2], st("rinv", k, 4)[:, 1:4:2],
                                           st("lam", 5, 1), None, ALU.mult))
                    if i >= 1:
                        dve.wait_ge(turned, TURNS[f"dap{i - 1}"][0] + 1)
                    cs = (slice(0, P), slice(P, SC_W))
                    for t in range(NT):
                        step.mark(dve.tensor_scalar(mix[:, cs[t]], probs[:, h, 0, cs[t]],
                                                    st("rinv", k + 2 * t, 1), None, ALU.mult))
                    step.wait()
                    for t in range(NT):
                        j = dve.scalar_tensor_tensor(out=mix[:, cs[t]], in0=probs[:, h, 1, cs[t]],
                                                     scalar=st("rinv", k + 2 * t + 1, 1), in1=mix[:, cs[t]],
                                                     op0=ALU.mult, op1=ALU.add)
                    j.then_inc(mixed, 1)
                if i >= 2:
                    n = i - 2
                    wait_norm(f"da{n}")
                    b = bank_of(f"dao{n}")
                    for t in range(NT):
                        j = dve.scalar_tensor_tensor(out=head_out[:, t, n, :], in0=b[:, P * t:P * t + P],
                                                     scalar=rstd(f"da{n}", t), in1=small[:, SM_DA:SM_DA + P],
                                                     op0=ALU.mult, op1=ALU.mult)
                    j.then_inc(freed["dve"], 1)
                fill(DA_FILL[i][2])
                if i in (6, 7):
                    t = i - 6
                    dve.wait_ge(evac["act"], BLOCKS["uq2"][4])
                    v = qb[:, t, :].rearrange("p (h n) -> p h n", h=HEADS)[:, :, NOPE:MLA_QK]
                    rotate1(v.rearrange("p h (a n) -> p h a n", a=2), t, HEADS)
                    if t == 1:
                        dve.nop().then_inc(roped, 1)
            for g in range(4):
                turned_lo(f"oa.{g}", a_hi, a_lo, 2 * g, 2)

            for i in range(HEADS + 2):
                if i < HEADS:
                    row_maxima(HEADS + i, 1)
                fill(MLA_FILL[i])
                if i >= 2:
                    head_scaled(f"mo{i - 2}", HEADS + i - 2, lambda t: head_out[:, t, i - 2, :], P)
                if i < HEADS:
                    row_sums(HEADS + i)
            for g in range(4):
                turned_lo(f"ob.{g}", a_hi, a_lo, 2 * g, 2)
            fill(0, "pb1")
            for g in range(4):
                turned_lo(f"mg.{g}", a_hi, a_lo, 2 * g, 2, 0.5)
            fill(0, "wo0")
            u_next = BLOCKS["FFN"][1]
            split_to(u_next)
            dve.wait_ge(rows_in[1], 16)
            dve.wait_ge(rows_in[2], 32)
            banks = [2 * (BLOCKS[f"wo{n}"][0] % 2) for n in range(2)]

            def wo_rows(t):
                weighted(t, [lin[:, b + t, :] for b in banks], rows[:, 1, :], "wo")
                add_normed("wo", t)
                dve.wait_ge(x_ready, t + 1)
                gained(t, rows[:, 2, :]).then_inc(xn_ready, 1)

            dve.wait_ge(first_rows, 1)
            wo_rows(0)
            split_to(u_next + 4)
            dve.wait_ge(used, u_next)
            rows_lo("x2", 0)
            wo_rows(1)
            rows_lo("x2", 1)
            dve.wait_ge(xn_ready, 2 * NT)
            unit_at[0] = u_next
            for counted in (evac["dve"], evac["dve"], rows_used, rows_used):
                dve.nop().then_inc(counted, 1)

            def hidden(e, gate):
                dve.wait_ge(silud, 2 * e)
                for t in range(NT):
                    i = dve.scalar_tensor_tensor(out=hid[:, t, :], in0=act_s[:, t, :], scalar=gate(t),
                                                 in1=lin[:, t, EW:2 * EW], op0=ALU.mult, op1=ALU.mult)
                i.then_inc(hid_ready, 1)

            def mlp(name, n, e0, gated, beside=None, late=None):
                u = BLOCKS[name][1]
                pairs0 = turn_pairs[0]

                def gate_of(e):
                    if not gated:
                        return lambda t: rstd("x2", t)
                    if isinstance(e, int):
                        return lambda t: st("gates", N_EXP * t + e, 1)
                    return lambda t: stat[:, bass.ds(e + (cols["gates"][0] + N_EXP * t), 1)]

                assert split_at[0] in (u + LEAD, u + 4)
                split_to(u + 6)
                hidden(e0 + 1, gate_of(0))
                split_to(u + 4 + LEAD)
                u += 4

                def one(e, u, last=False, shift=0, shift_e=0, beside=None):
                    dve.wait_ge(turn_hi, pairs0 + e + 1 + shift_e)
                    dve.tensor_tensor(b_lo[:, 0:2, :], turn[:, 0, :].rearrange("p (k n) -> p k n", k=2),
                                      b_hi[:, 0:2, :].bitcast(F32), ALU.subtract).then_inc(freed["dve"], 1)
                    for j in range(1 if last else 6):
                        if j == 3:
                            hidden(e0 + e + 2 + shift_e, gate_of(shift_e + (e + 1)))
                        if u + LEAD + j < N_UNITS:
                            split(u + LEAD + j, shift)
                        if beside is not None and j in (0, 1, 3, 4):
                            beside((0, 1, None, 2, 3)[j])

                one(0, u)
                u += 6
                pairs = (n - 3) // 2
                with dve.Fori(0, pairs) as i:
                    for j in range(2):
                        one(1 + j, u + 6 * j, False, i * 12, i * 2,
                            None if beside is None else lambda k: beside(i, 4 * j + k))
                u += 12 * pairs
                if late is not None:
                    late()
                for e in range(1 + 2 * pairs, n):
                    one(e, u, e == n - 1)
                    u += 2 if e == n - 1 else 6
                turn_pairs[0] += n
                split_at[0] = min(u + LEAD - 1, N_UNITS)
                unit_at[0] = u

            wait_norm("x2")
            dve.wait_ge(bias_in, 32)

            def gain_u():
                dve.wait_ge(freed["act"], TURNS["ad3"][2])
                dve.wait_ge(pool_rows_in[0], 16)
                step(dve.scalar_tensor_tensor(out=mod[:, D:2 * D], in0=mod[:, D:2 * D], scalar=1.0, in1=rows[:, 0, :],
                                              op0=ALU.add, op1=ALU.mult))

            mlp("FFN", N_FFN, 0, False, lambda i, k: ada_part(2, i, k), gain_u)
            dve.wait_ge(first_rows, 2)
            weighted(0, y_bank[0], rows[:, 3, :], "ffn")
            u_next = BLOCKS["jn0"][1]
            split_to(u_next + 2)
            dve.wait_ge(used, u_next)
            weighted(1, y_bank[1], rows[:, 3, :], "ffn")
            for t in range(NT):
                add_normed("ffn", t)
                dve.wait_ge(x_ready, NT + t + 1)
                step(gained(t, mod[:, D:2 * D]))
            for t in range(NT):
                modulated("u", t, mod[:, 0:D])
            for counted in (rows_used, rows_used):
                dve.nop().then_inc(counted, 1)
            split_to(u_next + LEAD)
            rows_lo("u", 0)
            split_to(u_next + 4)
            rows_lo("u", 1)
            block_loop("jn0", 4)

            fill(0, "jn8")
            wait_norm("lt")
            for t in range(NT):
                dve.scalar_tensor_tensor(out=zz[:, t, DKV:DKV + P], in0=zz[:, t, DKV:DKV + P], scalar=rstd("lt", t),
                                         in1=small[:, SM_LT:SM_LT + P], op0=ALU.mult, op1=ALU.mult)\
                   .then_inc(lat_ready, 1)
            dve.wait_ge(tanh_ready, NT)
            dve.wait_ge(pool_rows_in[1], 16)
            for t in range(NT):
                g = zz[:, t, RG:RG + D]
                step(dve.scalar_tensor_tensor(out=g, in0=gate2[:, t, 0:D], scalar=1.0, in1=g, op0=ALU.add,
                                              op1=ALU.mult))
                step(dve.scalar_tensor_tensor(out=g, in0=g, scalar=0.5, in1=rows[:, 1, :], op0=ALU.mult,
                                              op1=ALU.mult))
            dve.nop().then_inc(rows_used, 1)

            def ret_out(n):
                wait_norm(f"ret{n}")
                b = bank_of(f"rto{n}")
                for t in range(NT):
                    i = dve.tensor_scalar(zz[:, t, RV + n * P:RV + (n + 1) * P], b[:, P * t:P * t + P],
                                          ss(f"ret{n}", 2 * t), rstd(f"ret{n}", t), ALU.subtract, ALU.mult)
                i.then_inc(freed["dve"], 1)
                dve.wait_ge(freed["dve"], TURNS[f"rto{n}"][2])
                for t in range(NT):
                    v = zz[:, t, RV + n * P:RV + (n + 1) * P]
                    step.mark(dve.tensor_tensor(v, v, zz[:, t, RG + n * P:RG + (n + 1) * P], ALU.mult))

            dve.wait_ge(turned, TURNS["dt4"][0] + 1)
            for i in range(HEADS + 1):
                if i < HEADS:
                    dve.wait_ge(ret_scored, i + 1)
                    dve.wait_ge(decay, i + 1)
                    dve.scalar_tensor_tensor(out=probs_t[:, i % 2, :], in0=sco[:, i % 2, 0:SC_W],
                                             scalar=64 ** -0.5, in1=probs[:, i % 2, 0, :], op0=ALU.mult,
                                             op1=ALU.mult).then_inc(decayed, 1)
                fill(RET_FILL[i])
                if i >= 1:
                    n = i - 1
                    dve.wait_ge(turned, TURNS[f"rto{n}"][0] + 1)
                    b = bank_of(f"rto{n}")
                    for t in range(NT):
                        step.mark(dve.bn_stats(st("bn", 6 * t, 6), b[:, P * t:P * t + P]))
                    step.wait()
                    at = jobs[f"ret{n}"][1]
                    for t in range(NT):
                        j = dve.bn_aggr(stat[:, at + 2 * t:at + 2 * t + 2], st("bn", 6 * t, 6))
                    j.then_inc(var_dve, 1)
                    ret_out(n)

            step.wait()
            dve.nop().then_inc(dve_ret, 1)

            for i in range(HEADS):
                dve.wait_ge(relud, i + 1)
                for t in range(NT):
                    c = slice(0, P) if t == 0 else slice(P, SC_W)
                    w = zz[:, t, IW + i:IW + i + 1]
                    if i == 0:
                        step.mark(dve.tensor_scalar(mix[:, c], probs[:, i % 2, 0, c], w, None, ALU.mult))
                    else:
                        step.mark(dve.scalar_tensor_tensor(out=mix[:, c], in0=probs[:, i % 2, 0, c], scalar=w,
                                                           in1=mix[:, c], op0=ALU.mult, op1=ALU.add))
                step.wait()
                dve.nop().then_inc(idx_acc, 1)
                fill(IDX_FILL[i])
            for g in range(4):
                turned_lo(f"re.{g}", a_hi, a_lo, 2 * g, 2)
            step(dve.tensor_scalar(mix[:, :], mix[:, :], (64 ** -0.5) * (HEADS ** -0.5), None, ALU.mult))
            for c in (CHUNK, P + P + CHUNK):
                step.mark(dve.memset(mix[0:CHUNK, c:c + CHUNK], NEG))
            step.wait()
            for t in range(NT):
                c = slice(0, P) if t == 0 else slice(P, SC_W)
                here, there = mix[:, c], probs[:, 0, 0, c]
                for r in range(TOPK // 8):
                    step(dve.max(st("best"), here))
                    step(dve.match_replace(there, st("best"), here, TAKEN))
                    here, there = there, here
                    if r % 4 == 3:
                        fill(TOPK_FILL // 4)
                i = dve.tensor_scalar(sel_mask[:, c], here, TAKEN / 2, NEG, ALU.is_gt, ALU.mult)
                if t == 0:
                    step(i)
                else:
                    i.then_inc(mask_ready, 1)

            for i in range(HEADS + 2):
                fill(DSA_FILL[i])
                if i < HEADS:
                    n, h = 2 * HEADS + i, i % 2
                    dve.wait_ge(scored, n + 1)
                    dve.wait_ge(bm_ready, i + 1)
                    if i >= 2:
                        dve.wait_ge(turned, TURNS[f"dsp{i - 2}"][0] + 1)
                    dve.scalar_tensor_tensor(out=probs[:, h, 0, :], in0=sco[:, h, 0:SC_W], scalar=64 ** -0.5,
                                             in1=probs[:, h, 1, :], op0=ALU.mult, op1=ALU.add).then_inc(copied, 1)
                    dve.wait_ge(copied, i + 1)
                    maxima(n, 1, probs[:, h, 0:1, :])
                if i >= 2:
                    head_scaled(f"dso{i - 2}", 2 * HEADS + i - 2,
                                lambda t: zz[:, t, DQ + 64 * (i - 2):DQ + 64 * (i - 1)], 64)
                if i < HEADS:
                    row_sums(2 * HEADS + i)
            turned_lo("de.0", b_hi, b_lo, 0, 2)
            turned_lo("de.1", b_hi, b_lo, 2, 2)
            fill(0, "do1")
            for g in range(4):
                turned_lo(f"mh.{g}", a_hi, a_lo, 2 * g, 2, 0.5)
            dve.wait_ge(rows_in[0], 32)
            dve.wait_ge(freed["act"], TURNS["ad9"][2])
            step(dve.scalar_tensor_tensor(out=mod[:, 4 * D:5 * D], in0=mod[:, 4 * D:5 * D], scalar=1.0,
                                          in1=rows[:, 0, :], op0=ALU.add, op1=ALU.mult))
            fill(0, "xo0")
            u_next = BLOCKS["MOE"][1]
            split_to(u_next)
            dve.wait_ge(evac["dve"], BLOCKS["xo0"][4])
            dve.wait_ge(first_rows, 3)
            for t in range(NT):
                if t == 1:
                    split_to(u_next + LEAD)
                    dve.wait_ge(used, u_next)
                gated_rows(1, t, x_ready)
                dve.wait_ge(x_ready, 2 * NT + t + 1)
                step(gained(t, mod[:, 4 * D:5 * D]))
                if t == 1:
                    rows_lo("v", 0)
                modulated("v", t, mod[:, 3 * D:4 * D])
            unit_at[0] = u_next
            dve.nop().then_inc(evac["dve"], 1)
            split_to(u_next + 4)
            rows_lo("v", 1)

            def per(v, n):
                return v.rearrange("p (t n) -> p t n", t=NT)

            def over(v, n):
                return bass.AP(v.tensor, v.offset, [v.ap[0], v.ap[1], [0, n]])

            def first_of(eq, weights, n, m):
                w = bass.AP(weights.tensor, weights.offset, [weights.ap[0], [0, NT], [1, n]])
                step(dve.tensor_tensor(eq, eq, w, ALU.mult))
                step(dve.tensor_reduce(m, eq, AX.X, ALU.max))
                step(dve.tensor_tensor(eq, eq, over(m, n), ALU.is_equal))

            dve.wait_ge(routed, 1)
            b = sco[:, 0, 0:40].rearrange("p (t n) -> p t n", t=NT)
            bias = small[:, SM_B:SM_B + 20]
            dve.tensor_tensor(logit, b, bass.AP(bias.tensor, bias.offset, [bias.ap[0], [0, NT], [1, 20]]), ALU.add)\
               .then_inc(dve_step, 1)
            step.n += 1
            step.wait()
            gl = logit[:, :, 0:4]
            top, m = st("route", 0, 2), st("route", 2, 2)
            step(dve.tensor_reduce(top, gl, AX.X, ALU.max))
            step(dve.tensor_tensor(per(r_eq4, 4), gl, over(top, 4), ALU.is_ge))
            dve.tensor_tensor(per(route_x, 4), gl, over(top, 4), ALU.subtract).then_inc(route_in, 1)
            first_of(per(r_eq4, 4), cst[:, C_W4:C_W4 + 4], 4, m)
            spread = bass.AP(r_eq4.tensor, r_eq4.offset, [r_eq4.ap[0], [4, NT], [1, GROUPS], [0, PER_GROUP]])
            four = "p t (g n) -> p t g n"
            e4 = per(r_em, 16).rearrange(four, g=GROUPS)
            o4 = per(r_oh, 16).rearrange(four, g=GROUPS)
            step.mark(dve.tensor_tensor(e4, logit[:, :, 4:20].rearrange(four, g=GROUPS), spread, ALU.mult))
            step.mark(dve.tensor_scalar(o4, spread, -1.0, -NEG, ALU.add, ALU.mult))
            step.wait()
            step(dve.tensor_tensor(r_em, r_em, r_oh, ALU.add))
            v1, v2 = st("route", 4, 2), st("route", 6, 2)
            step(dve.tensor_reduce(v1, per(r_em, 16), AX.X, ALU.max))
            step(dve.tensor_tensor(per(r_oh, 16), per(r_em, 16), over(v1, 16), ALU.is_equal))
            first_of(per(r_oh, 16), cst[:, C_W16:C_W16 + 16], 16, m)
            step(dve.scalar_tensor_tensor(out=r_em, in0=r_oh, scalar=2 * NEG, in1=r_em, op0=ALU.mult, op1=ALU.add))
            step(dve.tensor_reduce(v2, per(r_em, 16), AX.X, ALU.max))
            step(dve.tensor_tensor(per(r_em, 16), per(r_em, 16), over(v2, 16), ALU.is_equal))
            dve.tensor_tensor(route_y, v2, v1, ALU.subtract).then_inc(route_in, 1)
            first_of(per(r_em, 16), cst[:, C_W16:C_W16 + 16], 16, m)
            dve.wait_ge(route_e, 2)
            total, w1 = st("route", 10, 2), st("route", 12, 2)
            step.mark(dve.tensor_reduce(total, per(route_x, 4), AX.X, ALU.add))
            step.mark(dve.tensor_scalar(w1, route_y, 1.0, None, ALU.add))
            step.wait()
            step(dve.tensor_tensor(w1, w1, total, ALU.mult))
            step(dve.reciprocal(w1, w1))
            step(dve.tensor_tensor(route_y, route_y, w1, ALU.mult))
            step.mark(dve.tensor_tensor(per(r_oh, 16), per(r_oh, 16), over(w1, 16), ALU.mult))
            step.mark(dve.tensor_tensor(per(r_em, 16), per(r_em, 16), over(route_y, 16), ALU.mult))
            step.wait()
            step(dve.tensor_tensor(st("gates"), r_oh, r_em, ALU.add))
            mlp("MOE", N_EXP, N_FFN, True)

            dve.wait_ge(freed["act"], TURNS["ad11"][2])
            dve.wait_ge(first_rows, 4)
            for t in range(NT):
                if t == 1:
                    dve.wait_ge(used, N_UNITS)
                weighted(t, y_bank[t], mod[:, 5 * D:6 * D])
                step.wait()
                dve.tensor_tensor(x[:, t, :], x[:, t, :], xn[:, t, :], ALU.add).then_inc(x_ready, 1)
            dve.wait_ge(x_ready, 4 * NT)
            dve.wait_ge(rows_in[1], 32)
            for t in range(NT):
                wait_norm(f"fin.{t}")
                dve.scalar_tensor_tensor(out=xn[:, t, :], in0=x[:, t, :], scalar=rstd("fin", t), in1=rows[:, 1, :],
                                         op0=ALU.mult, op1=ALU.mult).then_inc(xn_ready, 1)

        @block.tensor
        def _(pe):
            turn_at = [0]
            unit_at = [0]

            def three(dst, l_hi, l_lo, r_hi, r_lo, start, stop):
                pe.matmul(dst, l_hi, r_hi, start=start, stop=False)
                pe.matmul(dst, l_hi, r_lo, start=False, stop=False)
                return pe.matmul(dst, l_lo, r_hi, start=False, stop=stop)

            def bank_free(name):
                number = BLOCKS[name][0]
                if number >= 2:
                    before = BLOCKS[BLOCK_NAMES[number - 2]]
                    pe.wait_ge(evac[before[3]], before[4])

            def left(name):
                kind = name.rstrip("0123456789")
                if kind in ("uq", "ukv", "do"):
                    return b_hi, b_lo, 3 if kind == "ukv" else 0
                return a_hi, a_lo, 0

            def product_unit(name, part, shift=0, first=None, tokens=(0, 1)):
                number, u0, units, _, _ = BLOCKS[name]
                if first is not None:
                    number, u0 = first
                nk_all, width = LOADS[name][3], LOADS[name][2]
                u = u0 + part
                pe.wait_ge(lo_ready, u + 1 + shift)
                hi, lo, k0 = left(name)
                wh = w_hi[:, u % NSLOT, :].rearrange("p (k n) -> p k n", k=UK)
                wl = w_lo[:, u % NSLOT, :].rearrange("p (k n) -> p k n", k=UK)
                for k in range(min(UK, nk_all - part * UK)):
                    kt = part * UK + k
                    start, stop = kt == 0, kt == nk_all - 1
                    for t in tokens:
                        c = slice(t * P, (t + 1) * P)
                        i = three(lin[:, 2 * (number % 2) + t, 0:width], hi[:, k0 + kt, c], lo[:, k0 + kt, c],
                                  wh[:, k, 0:width], wl[:, k, 0:width], start, stop)
                if 1 in tokens:
                    i.then_inc(used, 1)
                return i

            def block_by_rows(name, between=None):
                for part in range(4):
                    i = product_unit(name, part, tokens=(0,))
                if between is None:
                    i.then_inc(first_rows, 1)
                else:
                    between()
                for part in range(4):
                    product_unit(name, part, tokens=(1,))

            def fill(n, until=None):
                end = unit_at[0] + n if until is None else BLOCKS[until][1] + BLOCKS[until][2]
                while unit_at[0] < end:
                    for name in BLOCK_NAMES:
                        _, u0, units, _, _ = BLOCKS[name]
                        if u0 <= unit_at[0] < u0 + units:
                            if unit_at[0] == u0:
                                bank_free(name)
                            product_unit(name, unit_at[0] - u0)
                    unit_at[0] += 1

            def block_loop(first, pairs, between):
                number, u0, units, engine, count = BLOCKS[first]
                for before in BLOCK_NAMES[max(0, number - 2):number]:
                    pe.wait_ge(evac[BLOCKS[before][3]], BLOCKS[before][4])
                block_by_rows(first, between)
                for part in range(4):
                    product_unit(first, part, 0, (number + 1, u0 + 4))
                with pe.Fori(1, pairs) as i:
                    for j in range(2):
                        pe.wait_ge(evac[engine], i * 2 + (count - 2 + j))
                        for part in range(4):
                            product_unit(first, part, i * 8, (number + j, u0 + 4 * j))
                unit_at[0] += 8 * pairs

            def turn_bank(name):
                number = TURNS[name][0]
                assert number == turn_at[0], (name, number, turn_at[0])
                turn_at[0] += 1
                if number >= 2:
                    _, engine, count = TURNS[TURN_NAMES[number - 2]]
                    pe.wait_ge(freed[engine], count)
                return turn[:, number % 2, :]

            def turn_all(name, sources):
                b = turn_bank(name)
                at = 0
                for src in sources:
                    n, m = src.shape[-1], src.shape[0]
                    i = pe.transpose(b[0:n, at:at + m], src, ident[0:m, 0:m])
                    at += m
                i.then_inc(turned, 1)

            def turn_rows(label, source, n_k=DK):
                for g in range(-(-n_k // 2)):
                    turn_all(f"{label}.{g}", [source(t, k) for k in range(2 * g, min(n_k, 2 * g + 2))
                                              for t in range(NT)])

            def turn_first(label, t):
                for g in (2 * t, 2 * t + 1):
                    turn_all(f"{label}.{g}", [col(xn[:, t, :], k) for k in range(4 * (g % 2), 4 * (g % 2) + 4)])
                pairs_freed(f"{label}.{2 * t + 1}")

            def turn_second(label, ready):
                pe.wait_ge(xn_ready, ready)
                turn_first(label, 1)

            def pairs_freed(name):
                _, engine, count = TURNS[name]
                pe.wait_ge(freed[engine], count)

            def col(v, k, n=P):
                return v[:, k * n:(k + 1) * n]

            def scores(bank, q, k):
                pe.matmul(bank[:, 0:P], q[:, 0:P], k[:, 0:P], start=True, stop=True)
                return pe.matmul(bank[:, P:SC_W], q[:, P:S], k[:, 0:S], start=True, stop=True)

            def turn_probs(name, p):
                turn_all(name, [p[:, 0:P], p[:, P:2 * P], p[:, 2 * P:3 * P]])

            def weigh(name, p, v, width):
                b = turn_bank(name)
                pe.matmul(b[:, 0:width], p[:, 0:P], v[0], start=True, stop=True)
                pe.matmul(b[:, width:2 * width], p[:, P:2 * P], v[0], start=True, stop=False)
                pe.matmul(b[:, width:2 * width], p[:, 2 * P:3 * P], v[1], start=False, stop=True).then_inc(turned, 1)

            def ada_sums(n0, n1):
                pe.wait_ge(ada_done, DK * ((n1 + 1) // 2))
                for n in range(n0, n1):
                    pe.matmul(turn_bank(f"ad{n}"), ones[:, :].broadcast_to([P, P]), mod[:, n * W:(n + 1) * W],
                              start=True, stop=True).then_inc(turned, 1)

            pe.wait_ge(tables_in, 16)
            pe.wait_ge(xn_ready, 1)
            turn_first("x1", 0)
            block_loop("in0", 3, lambda: turn_second("x1", 2))
            fill(0, "in7")
            pe.wait_ge(roped_qk, 1)
            pe.wait_ge(evac["act"], BLOCKS["in7"][4])

            def turn_qk(h):
                turn_all(f"qk{h}", [qkv[:, t, c + h * P:c + (h + 1) * P] for c in (0, D) for t in range(NT)])

            turn_qk(0)
            turn_qk(1)
            pe.wait_ge(lat_ready, 2 * NT)
            turn_rows("cl", lambda t, k: col(lat[:, t, :], k), 5)
            for i in range(HEADS + 2):
                if i + 2 < HEADS:
                    turn_qk(i + 2)
                fill(DA_FILL[i][0])
                if i < HEADS:
                    pe.wait_ge(freed["act"], TURNS[f"qk{i}"][2])
                    if i >= 1:
                        pe.wait_ge(expd, i)
                    for j in range(2):
                        rows_j = slice(DA_HD * j, DA_HD * (j + 1))
                        m = scores(sco[:, j, :], qk_t[rows_j, i, 0:S], qk_t[rows_j, i, S:2 * S])
                    m.then_inc(scored, 1)
                if i == 3:
                    pairs_freed("cl.2")
                fill(DA_FILL[i][1])
                if 1 <= i <= HEADS:
                    pe.wait_ge(mixed, i)
                    turn_probs(f"dap{i - 1}", mix)
                if i >= 2:
                    h = i - 2
                    pe.wait_ge(freed["act"], TURNS[f"dap{h}"][2])
                    weigh(f"dao{h}", probs_t[:, h % 2, :], [va[t][:, h * P:(h + 1) * P] for t in range(NT)], P)
                fill(DA_FILL[i][2])
            ada_sums(0, 4)
            pe.wait_ge(freed["dve"], TURNS["dao7"][2])
            turn_rows("oa", lambda t, k: head_out[:, t, k, :])
            pe.wait_ge(roped, 1)
            pe.wait_ge(evac["dve"], BLOCKS["ukv3"][4])
            qh = [qb[:, t, :].rearrange("p (h n) -> p h n", h=HEADS) for t in range(NT)]
            for g in range(4):
                turn_all(f"mr{g}", [qh[t][:, 2 * g + a, NOPE:MLA_QK] for a in range(2) for t in range(NT)])
            turn_all("kr", [lat[:, t, QR + KVR:C_W] for t in range(NT)])
            pairs_freed("oa.3")

            def turn_mq(h):
                turn_all(f"mq{h}", [qh[t][:, h, 0:NOPE] for t in range(NT)]
                         + [kvb[t][:, 2 * P * h:2 * P * h + P] for t in range(NT)])

            turn_mq(0)
            turn_mq(1)
            for i in range(HEADS + 2):
                if i + 2 < HEADS:
                    turn_mq(i + 2)
                if i < HEADS:
                    n = HEADS + i
                    pe.wait_ge(freed["act"], TURNS[f"mq{i}"][2])
                    pe.wait_ge(expd, HEADS if i < 2 else n - 1)
                    b = sco[:, n % 2, :]
                    q, k = qk_t[:, i, 0:S], qk_t[:, i, S:2 * S]
                    for t, c, keys in ((0, slice(0, P), slice(0, P)), (1, slice(P, SC_W), slice(0, S))):
                        qt = slice(t * P, (t + 1) * P)
                        pe.matmul(b[:, c], q[:, qt], k[:, keys], start=True, stop=False)
                        m = pe.matmul(b[:, c], qr_t[i][:, qt], kr_t[:, keys], start=False, stop=True)
                    m.then_inc(scored, 1)
                fill(MLA_FILL[i])
                if 1 <= i <= HEADS:
                    pe.wait_ge(expd, HEADS + i)
                    turn_probs(f"mp{i - 1}", probs[:, (i - 1) % 2, 0, :])
                if i >= 2:
                    h = i - 2
                    pe.wait_ge(freed["act"], TURNS[f"mp{h}"][2])
                    weigh(f"mo{h}", probs_t[:, h % 2, :], [kvb[t][:, 2 * P * h + P:2 * P * (h + 1)] for t in range(NT)],
                          P)
            pe.wait_ge(freed["dve"], TURNS["mo7"][2])
            turn_rows("ob", lambda t, k: head_out[:, t, k, :])
            pairs_freed("ob.3")
            fill(0, "pb1")
            pe.wait_ge(merged, 2 * NT)
            turn_rows("mg", lambda t, k: col(gate1[:, t, :], k))
            pairs_freed("mg.3")
            fill(0, "wo0")
            bank_free("wo1")
            block_by_rows("wo1")
            unit_at[0] += 4
            pe.wait_ge(xn_ready, NT + 1)
            turn_first("x2", 0)

            def mlp(name, label, n, hid0, between):
                u = BLOCKS[name][1]
                turn0, _, freed0 = TURNS[f"{label}0"]

                def gate_up(u, shift=0):
                    for half in range(2):
                        pe.wait_ge(lo_ready, u + 2 * half + 2 + shift)
                        s = (u + 2 * half) % NSLOT
                        for k in range(4):
                            kt = 4 * half + k
                            rh, rl = (v[:, s:s + 2, k * EW:(k + 1) * EW] for v in (w_hi, w_lo))
                            for t in range(NT):
                                c = slice(t * P, (t + 1) * P)
                                i = three(lin[:, t, :].rearrange("p (a n) -> p a n", a=2), a_hi[:, kt, c],
                                          a_lo[:, kt, c], rh, rl, kt == 0, kt == DK - 1)
                        i.then_inc(used, 2)

                def first_gate_up(u):
                    for t in range(NT):
                        for half in range(2):
                            pe.wait_ge(lo_ready, u + 2 * half + 2)
                            s = (u + 2 * half) % NSLOT
                            for k in range(4):
                                kt = 4 * half + k
                                c = slice(t * P, (t + 1) * P)
                                rh, rl = (v[:, s:s + 2, k * EW:(k + 1) * EW] for v in (w_hi, w_lo))
                                i = three(lin[:, t, :].rearrange("p (a n) -> p a n", a=2), a_hi[:, kt, c],
                                          a_lo[:, kt, c], rh, rl, kt == 0, kt == DK - 1)
                            if t == 1:
                                i.then_inc(used, 2)
                        if t == 0:
                            between()

                def last_down(e, u):
                    pe.wait_ge(freed["dve"], freed0 + e)
                    pe.wait_ge(lo_ready, u + 2)
                    for t in range(NT):
                        c = slice(t * P, (t + 1) * P)
                        for k in range(2):
                            s = (u + k) % NSLOT
                            for n_ in range(2):
                                wc = slice(n_ * W, (n_ + 1) * W)
                                i = three(y_bank[t][n_], b_hi[:, k, c], b_lo[:, k, c], w_hi[:, s, wc], w_lo[:, s, wc],
                                          False, k == 1)
                            if t == 1:
                                i.then_inc(used, 1)
                        if t == 0:
                            i.then_inc(first_rows, 1)

                def turn_hidden(e, shift_e=0):
                    pe.wait_ge(hid_ready, hid0 + e + 1 + shift_e)
                    for k in range(2):
                        for t in range(NT):
                            at = k * S + t * P
                            i = pe.transpose(turn[:, 0, at:at + P], hid[:, t, k * P:(k + 1) * P], ident)
                    i.then_inc(turned, 1)

                def down(e, u, first=False, shift=0, shift_e=0):
                    pe.wait_ge(freed["dve"], freed0 + e + shift_e)
                    for k in range(2):
                        pe.wait_ge(lo_ready, u + k + 1 + shift)
                        s = (u + k) % NSLOT
                        for n_ in range(2):
                            wc = slice(n_ * W, (n_ + 1) * W)
                            for t in range(NT):
                                c = slice(t * P, (t + 1) * P)
                                i = three(y_bank[t][n_], b_hi[:, k, c], b_lo[:, k, c], w_hi[:, s, wc], w_lo[:, s, wc],
                                          first and k == 0, False)
                        i.then_inc(used, 1)

                first_gate_up(u)
                assert turn_at[0] == turn0
                u += 4
                turn_hidden(0)
                gate_up(u)
                down(0, u + 4, first=True)
                u += 6
                pairs = (n - 3) // 2
                with pe.Fori(0, pairs) as i:
                    for j in range(2):
                        turn_hidden(1 + j, i * 2)
                        gate_up(u + 6 * j, i * 12)
                        down(1 + j, u + 6 * j + 4, shift=i * 12, shift_e=i * 2)
                u += 12 * pairs
                for e in range(1 + 2 * pairs, n):
                    turn_hidden(e)
                    if e + 1 < n:
                        gate_up(u)
                        u += 4
                        down(e, u)
                    else:
                        last_down(e, u)
                    u += 2
                turn_at[0] += n
                unit_at[0] = u

            def banks_free(last):
                for engine in ("act", "dve"):
                    done = [BLOCKS[n][4] for n in BLOCK_NAMES if BLOCKS[n][3] == engine
                            and BLOCKS[n][1] <= BLOCKS[last][1]]
                    pe.wait_ge(evac[engine], max(done))
                    pe.wait_ge(freed[engine], max(TURNS[n][2] for n in TURN_NAMES[:turn_at[0]]
                                                  if TURNS[n][1] == engine))

            banks_free("pb1")
            mlp("FFN", "ffn", N_FFN, 0, lambda: turn_second("x2", 2 * NT))
            pe.wait_ge(one_hot_in, 16)
            b = turn_bank("bv")
            pe.matmul(b[0:HEADS, 0:SC_W], rel_bias[:, :], mix[0:BUCKETS, :], start=True, stop=True).then_inc(turned, 1)
            pe.wait_ge(xn_ready, 2 * NT + 1)
            turn_first("u", 0)
            block_loop("jn0", 4, lambda: turn_second("u", 3 * NT))
            ada_sums(4, 8)
            fill(0, "jn8")
            ada_sums(8, 12)
            pe.wait_ge(lat_ready, 3 * NT)
            turn_all("lt", [zz[:, t, DKV:DKV + P] for t in range(NT)])
            pe.wait_ge(freed["act"], TURNS["lt"][2])
            b = turn_bank("lat")
            for t in range(NT):
                m = pe.matmul(b[:, t * P:(t + 1) * P], idk_t[:, t * P:(t + 1) * P], kv_up[:, :], start=True, stop=True)
            m.then_inc(turned, 1)
            pe.wait_ge(roped_qk, 2)
            for g in range(4):
                turn_all(f"rt{g}", [col(zz[:, t, c:c + W], g) for c in (RQ, RK) for t in range(NT)])
            for g in range(4):
                c = IQ if g < 2 else DQ
                turn_all(f"dt{g}", [col(zz[:, t, c:c + W], 2 * (g % 2) + a) for a in range(2) for t in range(NT)])
            pe.wait_ge(freed["act"], TURNS["lat"][2])
            turn_all("dt4", [probs_t[:, t, 0:P] for t in range(NT)] + [zz[:, t, DKV:DKV + P] for t in range(NT)])
            for i in range(HEADS + 1):
                if i < HEADS:
                    pe.wait_ge(freed["act"], TURNS[f"rt{i // 2}"][2])
                    if i >= 2:
                        pe.wait_ge(decayed, i - 1)
                    r = slice(64 * (i % 2), 64 * (i % 2) + 64)
                    q, k = rt_t[r, i // 2, 0:S], rt_t[r, i // 2, S:2 * S]
                    b = sco[:, i % 2, :]
                    pe.matmul(b[:, 0:S], k[:, 0:P], q[:, 0:S], start=True, stop=True)
                    pe.matmul(b[:, S:SC_W], k[:, P:S], q[:, P:S], start=True, stop=True).then_inc(ret_scored, 1)
                fill(RET_FILL[i])
                if i >= 1:
                    h = i - 1
                    pe.wait_ge(decayed, i)
                    weigh(f"rto{h}", probs_t[:, h % 2, :], [zz[:, t, RV + h * P:RV + (h + 1) * P] for t in range(NT)],
                          P)
            pe.wait_ge(freed["act"], TURNS["dt4"][2])
            for i in range(HEADS):
                if i >= 2:
                    pe.wait_ge(relud, i - 1)
                r = slice(64 * (i % 2), 64 * (i % 2) + 64)
                scores(sco[:, i % 2, :], idq_t[r, i // 2, :], idk_t[r, 0:S]).then_inc(idx_scored, 1)
                fill(IDX_FILL[i])
            pe.wait_ge(dve_ret, 1)
            turn_rows("re", lambda t, k: col(zz[:, t, RV:RV + D], k))
            pairs_freed("re.3")
            for i in range(HEADS + 2):
                if i == 0:
                    fill(TOPK_FILL)
                fill(DSA_FILL[i])
                if i < HEADS:
                    pe.wait_ge(relud, HEADS)
                    if i >= 2:
                        pe.wait_ge(copied, i - 1)
                    r = slice(64 * (i % 2), 64 * (i % 2) + 64)
                    scores(sco[:, i % 2, :], idq_t[r, 4 + i // 2, :], idk_t[r, S:2 * S]).then_inc(scored, 1)
                if 1 <= i <= HEADS:
                    pe.wait_ge(expd, 2 * HEADS + i)
                    turn_probs(f"dsp{i - 1}", probs[:, (i - 1) % 2, 0, :])
                if i >= 2:
                    h = i - 2
                    pe.wait_ge(freed["act"], TURNS[f"dsp{h}"][2])
                    weigh(f"dso{h}", probs_t[:, h % 2, :], [dv[:, t, :] for t in range(NT)], 64)
            pe.wait_ge(freed["dve"], TURNS["dso7"][2])
            turn_rows("de", lambda t, k: col(zz[:, t, DQ:DQ + W], k), 4)
            pairs_freed("de.1")
            fill(0, "do1")
            pe.wait_ge(merged, 4 * NT)
            turn_rows("mh", lambda t, k: col(gate2[:, t, :], k))
            pairs_freed("mh.3")
            fill(0, "xo0")
            bank_free("xo1")
            block_by_rows("xo1")
            unit_at[0] += 4
            pe.wait_ge(xn_ready, 3 * NT + 1)
            turn_first("v", 0)
            pe.wait_ge(route_lo, 1)
            pe.wait_ge(copied, HEADS)

            def route(t):
                c = slice(t * P, (t + 1) * P)
                for k in range(DK):
                    m = three(sco[:, 0, t * 20:t * 20 + 20], a_hi[:, k, c], a_lo[:, k, c], router_hi[:, k, :],
                              router_lo[:, k, :], k == 0, k == DK - 1)
                return m

            def second_rows():
                turn_second("v", 4 * NT)
                route(1).then_inc(routed, 1)

            route(0)
            banks_free("xo0")
            mlp("MOE", "moe", N_EXP, N_FFN, second_rows)


_WEIGHTS = ["x", "positions", "w_in", "w_uq", "w_ukv", "w_proj_a", "w_proj_b", "w_o", "w_ffn_gate", "w_ffn_up",
            "w_ffn_down", "ln_mix_pre", "ln_mix_post", "ln_ffn_pre", "ln_ffn_post", "c_2", "w_ada_2", "b_ada_2",
            "norm_mix_g_2", "w_in_2", "ret_gn_g_2", "w_dsa_kv_up_2", "rel_bias_2", "w_ret_out_2", "w_dsa_out_2",
            "w_gate_2", "b_gate_2", "w_o_2", "norm_ffn_g_2", "w_exp_gate_2", "w_exp_up_2", "w_exp_down_2",
            "norm_final_g_2"]


def kernel(**inputs):
    import concourse.bacc as _bacc
    from concourse.bass_utils import run_bass_kernel_spmd as _run

    nc = _bacc.Bacc("TRN2", target_bir_lowering=False, num_devices=1)
    a = {name: np.ascontiguousarray(value) for name, value in inputs.items()}
    consts, one_hot = shape_constants()
    packed = {
        "constants": consts,
        "bucket_choice": one_hot,
        "small_gains": np.concatenate([a[n].reshape(1, -1) for n in (
            "da_subln", "q_a_norm", "kv_a_norm", "dsa_kv_norm_g_2", "b_group_router_2", "b_expert_router_2")], axis=1),
        "lambdas": np.concatenate([a[n].reshape(1, -1) for n in (
            "lambda_q1", "lambda_k1", "lambda_q2", "lambda_k2")], axis=1),
        "router": np.concatenate([a["w_group_router_2"][0], a["w_expert_router_2"][0]], axis=1),
    }
    arrays, aps = {}, {}
    for name, value in [(n, a[n]) for n in _WEIGHTS] + list(packed.items()):
        arrays[f"in_{name}_dram"] = value
        aps[name] = nc.dram_tensor(f"in_{name}_dram", value.shape, mybir.dt.from_np(value.dtype),
                                   kind="ExternalInput").ap()
    rel_rows = nc.dram_tensor("relative_rows", (HEADS, P, REL_W), F32).ap()
    out = nc.dram_tensor("out_0_dram", (1, S, D), F32, kind="ExternalOutput").ap()
    two_blocks(nc, aps, aps["constants"], aps["bucket_choice"], aps["small_gains"], aps["lambdas"], aps["router"],
               rel_rows, out)
    r = _run(nc, [arrays], core_ids=[0])
    return r.results[0]["out_0_dram"]
```

```python
from contextlib import ExitStack

import numpy as np

import concourse.bass as bass
from concourse import mybir

F32 = mybir.dt.float32
F32R = mybir.dt.float32r
I32 = mybir.dt.int32
ALU = mybir.AluOpType
ACT = mybir.ActivationFunctionType
AX = mybir.AxisListType

P = 128
D = 1024
S = 256
NT = S // P
DK = D // P
CHUNK = 64
HEADS = 8
W = 512
UK = 2
UW = UK * W
NSLOT = 4
LEAD = 3
NEG = -1e30
TAKEN = -3e38
EPS = 1e-6
GN_EPS = 1e-5
LAMBDA_INIT = 0.8 - 0.6
DA_HD = 64
QR, KVR, ROPE, NOPE = 384, 256, 64, 128
MLA_QK = NOPE + ROPE
C_W = QR + KVR + ROPE
QKV_W = 3 * D
DFF = 2816
EW = 256
N_FFN = DFF // EW
N_EXP = 16
GROUPS, PER_GROUP = 4, 4
IN2_W = 4296
RQ, RK, RV, RG, DQ, DKV, IQ, IK, IW = 0, 512, 1024, 2048, 3072, 3584, 3712, 4224, 4288
TOPK = 64
N_ARENA = 14736
N_STAT = 300
BUCKETS = 32
REL_W = 384
SC_W = P + S
TWO_PI_PARTS = (6.28125, 0.0019350051879882812, 3.01991598819e-07)
ROUND = 12582912.0
SM_DA, SM_CQ, SM_CKV, SM_LT, SM_B, SM_END = 0, 128, 512, 768, 896, 916
JOBS = [("x1", D, EPS, 2, 2), ("cq", QR, EPS, 2, 2), ("ckv", KVR, EPS, 2, 2)]
JOBS += [(f"da{n}", 2 * DA_HD, EPS, 2, 2) for n in range(HEADS)]
JOBS += [("wo.0", D, EPS, 2, 1), ("wo.1", D, EPS, 2, 1), ("x2", D, EPS, 2, 2)]
JOBS += [("ffn.0", D, EPS, 2, 1), ("ffn.1", D, EPS, 2, 1), ("u.0", D, EPS, 1, 1), ("u.1", D, EPS, 1, 1)]
JOBS += [("lt", P, EPS, 2, 2)]
JOBS += [(f"ret{n}", 1, GN_EPS, 4, 2) for n in range(HEADS)]
JOBS += [("v.0", D, EPS, 1, 1), ("v.1", D, EPS, 1, 1), ("fin.0", D, EPS, 1, 1), ("fin.1", D, EPS, 1, 1)]
JOB_NAMES = [j[0] for j in JOBS]
DA_FILL = [(1, 1, 1)] * 5 + [(1, 2, 1), (0, 0, 1)] + [(0, 1, 1)] * 3
MLA_FILL = [1] * 6 + [0, 1, 1, 0]
IDX_FILL = [1] * 5 + [0] * 3
RET_FILL = [1] * 9
DSA_FILL = [2, 1, 0, 1, 0, 2, 1, 1, 1, 1]
ROTATED_AT = (7, 8)

C_ID, C_DIST, C_COS2, C_SIN2, C_FREQ, C_W4, C_W16, C_END = 0, 128, 512, 576, 640, 672, 676, 692


def shape_constants():
    c = np.zeros((P, C_END), np.float32)
    c[:, C_ID:C_ID + P] = np.eye(P, dtype=np.float32)
    k = np.arange(P)[:, None]
    q = np.arange(S)[None, :]
    d0 = np.abs(q - k).astype(np.float32)
    d0[(k // CHUNK) > (q // CHUNK)] = 1e30
    c[:, C_DIST:C_DIST + S] = d0
    d1 = np.abs(q[:, :P] - k).astype(np.float32)
    d1[(k // CHUNK) > (q[:, :P] // CHUNK)] = 1e30
    c[:, C_DIST + S:C_DIST + SC_W] = d1
    half = np.arange(32, dtype=np.float32)
    f2 = np.power(np.float32(10000.0), -(half * np.float32(2.0)) / np.float32(64)).astype(np.float32)
    for t in range(NT):
        ang = (np.arange(P, dtype=np.float32) + np.float32(t * P))[:, None] * f2[None, :]
        c[:, C_COS2 + 32 * t:C_COS2 + 32 * t + 32] = np.cos(ang.astype(np.float64))
        c[:, C_SIN2 + 32 * t:C_SIN2 + 32 * t + 32] = np.sin(ang.astype(np.float64))
    inv = np.float32(1.0) / np.power(np.float32(10000.0), half * np.float32(2.0 / 64)).astype(np.float32)
    c[:, C_FREQ:C_FREQ + 32] = inv
    c[:, C_W4:C_W4 + 4] = np.arange(4, 0, -1)
    c[:, C_W16:C_W16 + 16] = np.arange(16, 0, -1)
    rel = np.arange(REL_W) - (S - 1)
    nb = BUCKETS // 2
    n = np.abs(rel)
    ex = nb // 2
    nf = np.maximum(n, 1).astype(np.float32)
    large = ex + (np.log(nf / np.float32(ex)) / np.float32(np.log(128 / ex)) * np.float32(nb - ex)).astype(np.int32)
    bucket = (rel > 0) * nb + np.where(n < ex, n, np.minimum(large, nb - 1))
    one_hot = (bucket[None, :] == np.arange(BUCKETS)[:, None]).astype(np.float32)
    return c, one_hot


def plan_blocks():
    order = [(f"in{n}", DK, "act") for n in range(11)]
    order += [(f"uq{n}", QR // P, "act") for n in range(3)]
    order += [(f"ukv{n}", KVR // P, "act") for n in range(4)]
    order += [("in11", DK, "act")]
    order += [(f"{n}", DK, "dve") for n in ("pa0", "pa1", "pb0", "pb1", "wo0", "wo1")]
    order += [("FFN", 6 * N_FFN, None)]
    order += [(f"jn{n}", DK, "act") for n in range(9)]
    order += [(f"gt{n}", DK, "dve") for n in range(4)]
    order += [("ro0", DK, "dve"), ("ro1", DK, "dve"), ("do0", DK // 2, "dve"), ("do1", DK // 2, "dve")]
    order += [("xo0", DK, "dve"), ("xo1", DK, "dve")]
    order += [("MOE", 6 * N_EXP, None)]
    blocks, number, unit, count = {}, 0, 0, {"act": 0, "dve": 0}
    names = []
    for name, nk, engine in order:
        if engine is None:
            blocks[name] = (None, unit, nk, None, None)
            unit += nk
            continue
        units = -(-nk // UK)
        count[engine] += 1
        blocks[name] = (number, unit, units, engine, count[engine])
        names.append(name)
        number += 1
        unit += units
    return blocks, names, unit


def plan_turns():
    order = [(f"x1.{g}", "dve") for g in range(4)]
    order += [(f"qk{h}", "act") for h in range(2)]
    order += [(f"cl.{g}", "dve") for g in range(3)]
    for h in range(HEADS + 2):
        if h + 2 < HEADS:
            order.append((f"qk{h + 2}", "act"))
        if 1 <= h <= HEADS:
            order.append((f"dap{h - 1}", "act"))
        if 2 <= h:
            order.append((f"dao{h - 2}", "dve"))
    order += [(f"ad{n}", "act") for n in range(4)]
    order += [(f"oa.{g}", "dve") for g in range(4)]
    order += [(f"mr{g}", "act") for g in range(4)]
    order += [("kr", "act")]
    order += [(f"mq{h}", "act") for h in range(2)]
    for h in range(HEADS + 2):
        if h + 2 < HEADS:
            order.append((f"mq{h + 2}", "act"))
        if 1 <= h <= HEADS:
            order.append((f"mp{h - 1}", "act"))
        if 2 <= h:
            order.append((f"mo{h - 2}", "dve"))
    order += [(f"ob.{g}", "dve") for g in range(4)]
    order += [(f"mg.{g}", "dve") for g in range(4)]
    order += [(f"x2.{g}", "dve") for g in range(4)]
    order += [(f"ffn{e}", "dve") for e in range(N_FFN)]
    order += [("ad4", "act"), ("ad5", "act"), ("bv", "act")]
    order += [(f"u.{g}", "dve") for g in range(4)]
    order += [(f"ad{n}", "act") for n in range(6, 12)]
    order += [("lt", "act"), ("lat", "act")]
    order += [(f"rt{g}", "act") for g in range(4)]
    order += [(f"dt{g}", "act") for g in range(5)]
    order += [(f"rto{h}", "act") for h in range(HEADS)]
    for h in range(HEADS + 2):
        if h == 0:
            order += [(f"re.{g}", "dve") for g in range(4)]
        if 1 <= h <= HEADS:
            order.append((f"dsp{h - 1}", "act"))
        if 2 <= h:
            order.append((f"dso{h - 2}", "dve"))
    order += [(f"de.{g}", "dve") for g in range(2)]
    order += [(f"mh.{g}", "dve") for g in range(4)]
    order += [(f"v.{g}", "dve") for g in range(4)]
    order += [(f"moe{e}", "dve") for e in range(N_EXP)]
    turns, count, names = {}, {"act": 0, "dve": 0}, []
    for number, (name, engine) in enumerate(order):
        count[engine] += 1
        turns[name] = (number, engine, count[engine])
        names.append(name)
    return turns, names


BLOCKS, BLOCK_NAMES, N_UNITS = plan_blocks()
TURNS, TURN_NAMES = plan_turns()


class Counted:

    def __init__(self, engine, done):
        self.engine, self.done, self.n = engine, done, 0

    def __call__(self, instruction):
        self.mark(instruction)
        self.wait()

    def mark(self, instruction):
        self.n += 1
        instruction.then_inc(self.done, 1)

    def wait(self):
        self.engine.wait_ge(self.done, self.n)


def two_blocks(nc, ins, consts, one_hot_d, small_d, lambda_d, router_d, rel_rows, out):
    ctx = ExitStack()
    with ctx:
        def sb(name, shape, dt=F32):
            return ctx.enter_context(nc.sbuf_tensor(name, shape, dt))

        def psum(name, shape):
            return ctx.enter_context(nc.psum_tensor(name, shape, F32))

        def sem(name):
            return ctx.enter_context(nc.semaphore(name))

        raw = sb("raw", [P, NSLOT, UW])
        w_hi = sb("w_hi", [P, NSLOT, UW], F32R)
        w_lo = sb("w_lo", [P, NSLOT, UW], F32R)
        x = sb("x", [P, NT, D])
        a_hi = sb("a_hi", [P, DK, S], F32R)
        a_lo = sb("a_lo", [P, DK, S], F32R)
        b_hi = sb("b_hi", [P, 5, S], F32R)
        b_lo = sb("b_lo", [P, 5, S], F32R)
        c_col = sb("c_col", [P, DK])
        ones = sb("ones", [P, 1])
        mod = sb("mod", [P, 6 * D])
        rows = sb("rows", [P, 4, D])
        cst = sb("cst", [P, C_END])
        small = sb("small", [P, SM_END])
        probs = sb("probs", [P, 2, 2, SC_W])
        mix = sb("mix", [P, SC_W])
        probs_t = sb("probs_t", [P, 2, SC_W])
        dv = sb("dv", [P, NT, 64])
        router = sb("router", [P, DK, 20])
        router_hi = sb("router_hi", [P, DK, 20], F32R)
        router_lo = sb("router_lo", [P, DK, 20], F32R)
        trig = sb("trig", [P, 4, NT, 32])
        stat = sb("stat", [P, N_STAT])
        rel_bias = sb("rel_bias", [BUCKETS, HEADS])
        kv_up = sb("kv_up", [P, P])
        idk_t = sb("idk_t", [P, 2 * S])
        act_junk = idk_t[:, :].bitcast(mybir.dt.bfloat16)
        pos_i = sb("pos_i", [P, NT], I32)
        tmp = sb("tmp", [P, 2, W])
        arena = sb("arena", [P, N_ARENA])

        lin = psum("lin", [P, 4, W])
        turn = psum("turn", [P, 2, W])
        sco = psum("sco", [P, 2, W])

        ident = cst[:, C_ID:C_ID + P]

        def carve(at, *dims):
            n = int(np.prod(dims))
            v = arena[:, at:at + n]
            if len(dims) == 2:
                v = v.rearrange("p (a b) -> p a b", b=dims[1])
            return v, at + n

        xn, _ = carve(0, NT, D)

        qkv, at1 = carve(0, NT, QKV_W)
        qk_t, at2 = carve(at1, HEADS, 2 * S)
        lat, at3 = carve(at2, NT, C_W)
        qb, at4 = carve(at3, NT, HEADS * MLA_QK)
        head_out = qk_t[:, :, 0:S].rearrange("p h (t d) -> p t h d", t=NT)
        kvb = [qkv[:, t, 0:2 * D] for t in range(NT)]
        va = [qkv[:, t, 2 * D:3 * D] for t in range(NT)]
        kr_t = mix[0:ROPE, 0:S]
        qr_t = [va[h // 4][0:ROPE, (h % 4) * S:(h % 4 + 1) * S] for h in range(HEADS)]
        gate1 = mod[:, 2 * D:6 * D].rearrange("p (t n) -> p t n", t=NT)

        zz, bt1 = carve(0, NT, IN2_W)
        rt_t, bt2 = carve(bt1, 4, 2 * S)
        gate2, bt3 = carve(bt2, NT, 2 * D)
        idq_t = mod[:, 0:2 * D].rearrange("p (g n) -> p g n", g=8)
        assert max(at4, bt3) <= N_ARENA
        sel_mask = zz[:, 0, IQ:IQ + SC_W]
        rel_b = [zz[:, h // 4, h % 4 * S:(h % 4 + 1) * S] for h in range(HEADS)]

        act_s, _ = carve(4096, NT, EW)
        hid, _ = carve(4608, NT, EW)
        y_bank = [[lin[:, 2, :], lin[:, 3, :]], [sco[:, 0, :], sco[:, 1, :]]]

        cols = {}
        for name, n in (("neg_half", 4), ("ms", 4), ("lam", 12), ("pos", 2), ("nmax", 8), ("rsum", 8), ("rinv", 8),
                        ("best", 8), ("bn", 12), ("route", 32), ("gates", 32), ("half_r", 2)):
            at = sum(cols[c][1] for c in cols)
            cols[name] = (at, n)
        ss_at = sum(n for _, n in cols.values())

        def st(name, a=0, n=None):
            at, size = cols[name]
            return stat[:, at + a:at + (size if n is None else a + n)]

        jobs = {}
        at, n_act, n_dve = ss_at, 0, 0
        for name, width, eps, n, tokens in JOBS:
            if name.startswith("ret"):
                n_dve += 1
            else:
                n_act += n
            jobs[name] = (len(jobs), at, width, eps, n, n_act, n_dve, tokens)
            at += n + tokens
        assert at <= N_STAT, at

        logit = arena[:, 5120:5160].rearrange("p (t n) -> p t n", t=NT)
        r_em, r_oh = arena[:, 5160:5192], arena[:, 5192:5224]
        route_y, route_x, r_eq4 = st("route", 8, 2), st("route", 14, 8), st("route", 22, 8)

        def ss(name, a):
            return stat[:, jobs[name][1] + a:jobs[name][1] + a + 1]

        def rstd(name, t):
            if name not in jobs:
                name, t = f"{name}.{t}", 0
            at = jobs[name][1] + jobs[name][4] + t
            return stat[:, at:at + 1]

        landed = [sem(f"unit_landed{s}") for s in range(NSLOT)]
        hi_ready = sem("unit_hi_ready")
        lo_ready = sem("unit_lo_ready")
        used = sem("units_used")
        evac = {"act": sem("blocks_evacuated_by_act"), "dve": sem("blocks_evacuated_by_dve")}
        turned = sem("turn_bank_filled")
        freed = {"act": sem("turn_bank_freed_by_act"), "dve": sem("turn_bank_freed_by_dve")}
        turn_hi = sem("turned_hi_ready")
        consts_in = sem("constants_landed")
        x_in = [sem(f"x_rows{t}_landed") for t in range(NT)]
        rows_in = [sem(f"rows{r}_landed") for r in range(3)]
        mod_clear = sem("modulation_rows_cleared")
        pool_rows_in = [sem(f"second_rows{r}_landed") for r in range(2)]
        bias_in = sem("b_ada_landed")
        ada_in = [sem(f"ada_weights{n}_landed") for n in range(8)]
        ada_done = sem("ada_products_accumulated")
        tables_in = sem("tables_landed")
        one_hot_in = sem("bucket_choice_landed")
        rows_used = sem("gaproducts_used")
        merged = sem("merged_rows_ready")
        mean_ready = sem("scaled_means_ready")
        ret_scaled = sem("retention_rows_scaled")
        ret_done = sem("retention_rows_ready")
        tanh_ready = sem("gates_tanh_ready")
        sq_act = sem("squares_by_act")
        var_dve = sem("variances_by_dve")
        rstd_ready = sem("rstd_ready")
        silu_c = sem("silu_c_ready")
        half_ready = sem("half_rstd_ready")
        tables_ready = sem("rotation_tables_ready")
        angles = sem("angles_ready")
        sines = sem("sines_ready")
        lam_in = sem("lambda_products_ready")
        lam_exp = sem("lambda_exponentials_ready")
        x_ready = sem("residual_updated")
        xn_ready = sem("normalised_rows_ready")
        lat_ready = sem("normalised_latents_ready")
        roped_qk = sem("rotations_by_pool_ready")
        roped = sem("rotations_ready")
        scored = sem("attention_scores_ready")
        masked = sem("row_maxima_ready")
        expd = sem("exponentials_ready")
        mixed = sem("row_normalisers_ready")
        copied = sem("biased_scores_ready")
        ret_scored = sem("retention_scores_ready")
        decay = sem("retention_decays_ready")
        decayed = sem("decayed_scores_ready")
        idx_scored = sem("index_scores_ready")
        relud = sem("index_scores_rectified")
        idx_acc = sem("index_scores_summed")
        bv_in = sem("relative_rows_stored")
        rel_in = sem("relative_tiles_landed")
        bm_ready = sem("biased_mask_ready")
        mask_ready = sem("selection_ready")
        silud = sem("silu_ready")
        hid_ready = sem("hidden_ready")
        route_hi = sem("router_hi_ready")
        route_lo = sem("router_lo_ready")
        route_in = sem("router_exponents_wanted")
        route_e = sem("router_exponentials_ready")
        first_rows = sem("sums_of_first_token_block")
        routed = sem("router_logits_ready")
        routed_out = sem("router_logits_out")
        dve_step = sem("dve_step")
        act_step = sem("act_step")
        pool_step = sem("pool_step")
        stored = sem("output_stored")

        block = ctx.enter_context(nc.Block())

        def row_source(name):
            v = ins[name]
            return bass.AP(v.tensor, 0, [[0, P], [1, D]])

        def k_tiles(name):
            return ins[name][0].rearrange("(k p) n -> p k n", p=P)

        IN1 = [(n * W, W) for n in range(6)] + [(QKV_W, W), (QKV_W + W, C_W - W)] \
            + [(QKV_W + C_W + n * W, W) for n in range(4)]
        LOADS = {}
        for n in range(12):
            LOADS[f"in{n}"] = ("w_in", *IN1[n], DK)
        for n in range(3):
            LOADS[f"uq{n}"] = ("w_uq", n * W, W, QR // P)
        for n in range(4):
            LOADS[f"ukv{n}"] = ("w_ukv", n * W, W, KVR // P)
            LOADS[f"gt{n}"] = ("w_gate_2", n * W, W, DK)
        for n in range(9):
            LOADS[f"jn{n}"] = ("w_in_2", n * W, min(W, IN2_W - n * W), DK)
        for n in range(2):
            LOADS[f"pa{n}"] = ("w_proj_a", n * W, W, DK)
            LOADS[f"pb{n}"] = ("w_proj_b", n * W, W, DK)
            LOADS[f"wo{n}"] = ("w_o", n * W, W, DK)
            LOADS[f"ro{n}"] = ("w_ret_out_2", n * W, W, DK)
            LOADS[f"do{n}"] = ("w_dsa_out_2", n * W, W, DK // 2)
            LOADS[f"xo{n}"] = ("w_o_2", n * W, W, DK)

        @block.sync
        def _(sp):
            def free_slot(u, shift=0, looped=False):
                if u >= NSLOT or looped:
                    sp.wait_ge(lo_ready, u - NSLOT + 1 + shift)

            def load(name, col=None, shift=0, first=None, looped=False, parts=None):
                weight, c0, width, nk = LOADS[name]
                u = BLOCKS[name][1] if first is None else first
                src = k_tiles(weight)
                for part in range(-(-nk // UK)):
                    if parts is not None and part not in parts:
                        u += 1
                        continue
                    n = min(UK, nk - part * UK)
                    free_slot(u, shift, looped)
                    where = slice(c0, c0 + width) if col is None else bass.ds(col, width)
                    dst = raw[:, u % NSLOT, :].rearrange("p (k n) -> p k n", k=UK)[:, 0:n, 0:width]
                    sp.dma_start(dst, src[:, part * UK:part * UK + n, where]).then_inc(landed[u % NSLOT], 16)
                    u += 1

            def load_slice(u, e, moe, down, shift=0):
                if not down:
                    for half in range(2):
                        for w in ("w_exp_gate_2", "w_exp_up_2") if moe else ("w_ffn_gate", "w_ffn_up"):
                            free_slot(u, shift)
                            if moe:
                                src = ins[w][0, bass.ds(e, 1)].rearrange("e (k p) n -> p (e k) n", p=P)
                                src = src[:, 4 * half:4 * half + 4, :]
                            else:
                                src = k_tiles(w)[:, 4 * half:4 * half + 4, bass.ds(e * EW, EW)]
                            sp.dma_start(raw[:, u % NSLOT, :].rearrange("p (k n) -> p k n", k=4), src)\
                              .then_inc(landed[u % NSLOT], 16)
                            u += 1
                else:
                    for k in range(2):
                        free_slot(u, shift)
                        if moe:
                            src = ins["w_exp_down_2"][0, bass.ds(e, 1)].rearrange("e f n -> (e f) n")
                            src = src[k * P:(k + 1) * P, :]
                        else:
                            src = ins["w_ffn_down"][0, bass.ds(e * EW + k * P, P), :]
                        sp.dma_start(raw[:, u % NSLOT, :], src).then_inc(landed[u % NSLOT], 16)
                        u += 1
                return u

            def load_mlp(name, n, moe):
                u = load_slice(BLOCKS[name][1], 0, moe, False)
                u = load_slice(u, 1, moe, False)
                u = load_slice(u, 0, moe, True)
                pairs = (n - 3) // 2
                with sp.Fori(0, pairs) as i:
                    for j in range(2):
                        load_slice(u + 6 * j, i * 2 + (2 + j), moe, False, i * 12)
                        load_slice(u + 6 * j + 4, i * 2 + (1 + j), moe, True, i * 12)
                u += 12 * pairs
                for e in range(1 + 2 * pairs, n):
                    if e + 1 < n:
                        u = load_slice(u, e + 1, moe, False)
                    u = load_slice(u, e, moe, True)

            sp.dma_start(x[:, 0, :], ins["x"][0, 0:P, :]).then_inc(x_in[0], 16)
            sp.dma_start(rows[:, 0, :], row_source("ln_mix_pre")).then_inc(rows_in[0], 16)
            load("in0", parts=(0,))
            sp.dma_start(x[:, 1, :], ins["x"][0, P:S, :]).then_inc(x_in[1], 16)
            load("in0", parts=(1, 2, 3))
            load("in1")
            with sp.Fori(1, 3) as i:
                for j in range(2):
                    load("in0", i * (2 * W) + j * W, i * 8, BLOCKS["in0"][1] + 4 * j, True)
            for name in BLOCK_NAMES[BLOCK_NAMES.index("in6"):BLOCK_NAMES.index("pb1") + 1]:
                load(name)
            sp.dma_start(rows[:, 1, :], row_source("ln_mix_post")).then_inc(rows_in[1], 16)
            sp.wait_ge(roped_qk, 1)
            sp.dma_start(rows[:, 2, :], row_source("ln_ffn_pre")).then_inc(rows_in[2], 16)
            sp.dma_start(rows[:, 3, :], row_source("ln_ffn_post")).then_inc(rows_in[2], 16)
            load("wo0")
            load("wo1")
            load_mlp("FFN", N_FFN, False)
            with sp.Fori(0, 4) as i:
                for j in range(2):
                    load("jn0", i * (2 * W) + j * W, i * 8, BLOCKS["jn0"][1] + 4 * j)
            load("jn8")
            sp.wait_ge(rows_used, 4)
            gate_src = bass.AP(ins["b_gate_2"].tensor, 0, [[0, P], [1, 2 * D]])
            sp.dma_start(rows[:, 2:4, :].rearrange("p a n -> p (a n)"), gate_src).then_inc(rows_in[2], 16)
            for n in range(4):
                load(f"gt{n}")
            sp.wait_ge(rows_used, 5)
            sp.dma_start(rows[:, 0, :], row_source("norm_ffn_g_2")).then_inc(rows_in[0], 16)
            sp.dma_start(rows[:, 1, :], row_source("norm_final_g_2")).then_inc(rows_in[1], 16)
            for name in ("ro0", "ro1", "do0", "do1", "xo0", "xo1"):
                load(name)
            load_mlp("MOE", N_EXP, True)
            out_d = out[0].rearrange("(t p) n -> p t n", p=P)
            for t in range(NT):
                sp.wait_ge(xn_ready, 4 * NT + t + 1)
                sp.dma_start(out_d[:, t, :], xn[:, t, :]).then_inc(stored, 16)
            sp.wait_ge(stored, 16 * NT)

        def rotate(engine, step, temp, v, cos, sin, nsin, groups):
            def over(table, *dims):
                return bass.AP(table.tensor, table.offset, [table.ap[0]] + [[0, n] for n in dims] + [[1, 32]])
            n = groups * 64
            by_cos = temp[:, 0, 0:n].rearrange("p (g a n) -> p g a n", g=groups, a=2)
            by_sin = temp[:, 1, 0:n].rearrange("p (g a n) -> p g a n", g=groups, a=2)
            step.mark(engine.tensor_tensor(by_cos, v, over(cos, groups, 2), ALU.mult))
            step.mark(engine.tensor_tensor(by_sin[:, :, 0, :], v[:, :, 1, :], over(nsin, groups), ALU.mult))
            step(engine.tensor_tensor(by_sin[:, :, 1, :], v[:, :, 0, :], over(sin, groups), ALU.mult))
            step(engine.tensor_tensor(v, by_cos, by_sin, ALU.add))

        def ada_slots(g):
            if g < 2:
                return [carve(at1 + n * D, D)[0] for n in range(8)]
            return [carve(5632 + n * D, D)[0] for n in range(4)]

        @block.gpsimd
        def _(pool):
            pool.dma_start(cst[:, :], consts).then_inc(tables_in, 16)
            with nc.allow_non_contiguous_dma(reason="a column a K tile, a position a partition"):
                pool.dma_start(probs[:, 0, 0, 0:DK], ins["c_2"].rearrange("a (k p) -> p (a k)", p=P))\
                    .then_inc(consts_in, 16)
                pool.dma_start(pos_i[:, :], ins["positions"].rearrange("a (t p) -> p (a t)", p=P))\
                    .then_inc(consts_in, 16)
            pool.dma_start(small[:, :], bass.AP(small_d.tensor, 0, [[0, P], [1, SM_END]])).then_inc(consts_in, 16)
            pool.dma_start(probs[:, 1, 0, 0:S], bass.AP(lambda_d.tensor, 0, [[0, P], [1, S]])).then_inc(consts_in, 16)
            pool.dma_start(router[:, :, :], router_d.rearrange("(k p) n -> p k n", p=P)).then_inc(consts_in, 16)
            pool.dma_start(rel_bias[:, :], ins["rel_bias_2"]).then_inc(consts_in, 16)
            pool.dma_start(kv_up[:, :], ins["w_dsa_kv_up_2"][0]).then_inc(consts_in, 16)
            step = Counted(pool, pool_step)
            step(pool.memset(st("neg_half"), -0.5))
            pool.memset(ones[:, :], 1.0).then_inc(mod_clear, 1)

            def clear_rows(n, c):
                pool.memset(mod[:, c], 0.0).then_inc(mod_clear, 1)
                pool.wait_ge(mod_clear, n)
                pool.dma_start(mod[0:1, c], ins["b_ada_2"][:, c]).then_inc(bias_in, 16)
                pool.wait_ge(bias_in, 16 * (n - 1))

            def ada_source(k, c):
                return ins["w_ada_2"][0, k * P:(k + 1) * P, c]

            def norm_job(name):
                number, at, width, eps, n, n_act, n_dve, tokens = jobs[name]
                source = stat[:, at:at + tokens]
                if name.startswith("ret"):
                    pool.wait_ge(var_dve, n_dve)
                    source = stat[:, at + 1:at + 4:2]
                else:
                    pool.wait_ge(sq_act, n_act)
                    if n > tokens:
                        step(pool.tensor_tensor(st("ms", 2, 1), stat[:, at:at + 1], stat[:, at + 1:at + 2], ALU.add))
                        source = st("ms", 2, 1)
                ms = st("ms", 0, tokens)
                step(pool.tensor_scalar(ms, source, 1.0 / width, eps, ALU.mult, ALU.add))
                pool.tensor_tensor(stat[:, at + n:at + n + tokens], ms, st("neg_half", 0, tokens), ALU.pow)\
                    .then_inc(rstd_ready, 1)
                pool.wait_ge(rstd_ready, number + 1)

            def norm_jobs(first, last):
                for name in JOB_NAMES[JOB_NAMES.index(first):JOB_NAMES.index(last) + 1]:
                    norm_job(name)

            clear_rows(2, slice(0, 2 * D))
            norm_jobs("x1", "x1")
            pool.tensor_scalar(st("half_r"), stat[:, jobs["x1"][1] + 2:jobs["x1"][1] + 4], 0.5, None, ALU.mult)\
                .then_inc(half_ready, 1)
            for n in range(2 * DK):
                if n >= 8:
                    pool.wait_ge(ada_done, n - 7)
                pool.dma_start(ada_slots(0)[n % 8], ada_source(n % DK, slice(n // DK * D, (n // DK + 1) * D)))\
                    .then_inc(ada_in[n % 8], 16)
            pool.wait_ge(tables_ready, 1)
            products = rows[:, 2, :].rearrange("p (a n) -> p a n", a=2)
            for n in range(4):
                pool.wait_ge(evac["act"], n + 1)
                for t in range(NT):
                    rotate(pool, step, products,
                           qkv[:, t, n * W:(n + 1) * W].rearrange("p (g a n) -> p g a n", g=8, a=2),
                           trig[:, 0, t, :], trig[:, 1, t, :], trig[:, 2, t, :], 8)
            pool.nop().then_inc(roped_qk, 1)
            norm_jobs("cq", "da7")
            pool.wait_ge(turned, TURNS["mg.3"][0] + 1)
            clear_rows(3, slice(2 * D, 6 * D))
            norm_jobs("wo.0", "x2")
            pool.wait_ge(rows_used, 3)
            pool.dma_start(rows[:, 0, :], row_source("norm_mix_g_2")).then_inc(pool_rows_in[0], 16)
            pool.dma_start(rows[:, 1, :], row_source("ret_gn_g_2")).then_inc(pool_rows_in[1], 16)
            with pool.Fori(0, 4) as i:
                for k in range(DK):
                    pool.wait_ge(ada_done, i * DK + (2 * DK + k - 3))
                    pool.dma_start(ada_slots(2)[k % 4], ada_source(k, bass.ds(i * D + 2 * D, D)))\
                        .then_inc(ada_in[k % 4], 16)
            pool.dma_start(mix[0:BUCKETS, :], one_hot_d).then_inc(one_hot_in, 16)
            norm_jobs("ffn.0", "u.1")
            pool.wait_ge(freed["act"], TURNS["bv"][2])
            row = probs[0:HEADS, 1, 0, :]
            pool.dma_start(rel_rows, bass.AP(row.tensor, row.offset, [row.ap[0], [0, P], row.ap[1]]))\
                .then_inc(bv_in, 16)
            pool.wait_ge(x_ready, 2 * NT)
            for n in range(2):
                pool.wait_ge(evac["act"], BLOCKS["jn0"][4] + n)
                for t in range(NT):
                    rotate(pool, step, tmp, zz[:, t, n * W:(n + 1) * W].rearrange("p (g a n) -> p g a n", g=8, a=2),
                           cst[:, C_COS2 + 32 * t:C_COS2 + 32 * t + 32], cst[:, C_SIN2 + 32 * t:C_SIN2 + 32 * t + 32],
                           trig[:, 3, t, :], 8)
            pool.nop().then_inc(roped_qk, 1)
            norm_jobs("lt", "lt")
            pool.wait_ge(turned, TURNS["rt3"][0] + 1)
            pool.wait_ge(bv_in, 16)
            for a in range(2):
                tiles = bass.AP(rel_rows.tensor, a * 4 * P * REL_W + P - 1,
                                [[REL_W - 1, P], [P * REL_W, 4], [1, S]])
                pool.dma_start(zz[:, a, 0:4 * S].rearrange("p (h n) -> p h n", h=4), tiles).then_inc(rel_in, 16)
            for n in range(HEADS):
                norm_job(f"ret{n}")
                at = jobs[f"ret{n}"][1]
                pool.tensor_tensor(stat[:, at:at + 4:2], stat[:, at:at + 4:2], stat[:, at + 4:at + 6], ALU.mult)\
                    .then_inc(mean_ready, 1)
            pool.wait_ge(mask_ready, 1)
            pool.wait_ge(rel_in, 32)
            for h in range(HEADS):
                if h >= 2:
                    pool.wait_ge(copied, h - 1)
                b = probs[:, h % 2, 1, :]
                pool.tensor_tensor(b[:, 0:P], rel_b[h][:, P:S], sel_mask[:, 0:P], ALU.add)
                pool.tensor_tensor(b[:, P:SC_W], rel_b[h], sel_mask[:, P:SC_W], ALU.add).then_inc(bm_ready, 1)
            norm_jobs("v.0", "fin.1")

        @block.scalar
        def _(act):
            split_at = [0]
            unit_at = [0]
            sq_at = [0]

            def split(u, shift=0, looped=False):
                s = u % NSLOT
                act.wait_ge(landed[s], 16 * (u // NSLOT + 1) + shift * 4)
                if u >= NSLOT or looped:
                    act.wait_ge(used, u - NSLOT + 1 + shift)
                act.activation(w_hi[:, s, :], raw[:, s, :], ACT.Copy).then_inc(hi_ready, 1)

            def split_to(n):
                while split_at[0] < min(n, N_UNITS):
                    split(split_at[0])
                    split_at[0] += 1

            def fill(n, until=None):
                end = unit_at[0] + n if until is None else BLOCKS[until][1] + BLOCKS[until][2]
                while unit_at[0] < end:
                    split_to(unit_at[0] + LEAD + 1)
                    unit_at[0] += 1
                    for name in BLOCK_NAMES:
                        if BLOCKS[name][1] + BLOCKS[name][2] == unit_at[0]:
                            if BLOCKS[name][3] == "act":
                                evacuate(name)
                        if name in ("gt0", "gt1", "gt2") and sum(BLOCKS[name][1:3]) + 2 == unit_at[0]:
                            gate_tanh(name)

            def evacuate(name):
                number, u0, units, _, _ = BLOCKS[name]
                act.wait_ge(used, u0 + units)
                bank = 2 * (number % 2)
                kind = name.rstrip("0123456789")
                n = int(name[len(kind):])
                for t in range(NT):
                    if kind == "in" and n >= 8:
                        c = (n - 8) * W
                        i = act.activation(gate1[:, t, c:c + W], lin[:, bank + t, :], ACT.Tanh,
                                           scale=st("half_r", t, 1))
                    elif kind == "in":
                        c, w = (n - 6) * W, IN1[n][1]
                        i = act.activation(lat[:, t, c:c + w], lin[:, bank + t, 0:w], ACT.Copy, scale=rstd("x1", t))
                    elif kind == "ukv":
                        i = act.activation(kvb[t][:, n * W:(n + 1) * W], lin[:, bank + t, :], ACT.Copy)
                    elif kind == "uq":
                        i = act.activation(qb[:, t, n * W:(n + 1) * W], lin[:, bank + t, :], ACT.Copy)
                    else:
                        w = LOADS[name][2]
                        i = act.activation(zz[:, t, n * W:n * W + w], lin[:, bank + t, 0:w], ACT.Copy)
                i.then_inc(evac["act"], 1)

            def gate_tanh(name):
                n = int(name[2:])
                act.wait_ge(evac["dve"], BLOCKS[name][4])
                g = gate2[:, :, n * W:(n + 1) * W]
                act.activation(g, g, ACT.Tanh, scale=0.5).then_inc(tanh_ready, 1)

            def block_loop(first, pairs, target, scale=lambda t: 1.0, start=None):
                number, u0, units, _, _ = BLOCKS[first]
                assert u0 + LEAD <= split_at[0] <= u0 + 4 and unit_at[0] == u0

                def pair(i, looped):
                    for j in range(2):
                        for k in range(4):
                            u = u0 + LEAD + 4 * j + k
                            if looped or u >= split_at[0]:
                                split(u, i * 8, looped)
                            if start is not None and not looped:
                                start(4 * j + k)
                        act.wait_ge(used, i * 8 + (u0 + 4 * j + 4))
                        act.nop()
                        bank = 2 * ((number + j) % 2)
                        for t in range(NT):
                            e = act.activation(target[:, t, bass.ds(i * (2 * W) + j * W, W)],
                                               lin[:, bank + t, :], ACT.Copy, scale=scale(t))
                        e.then_inc(evac["act"], 1)

                pair(0, False)
                with act.Fori(1, pairs) as i:
                    pair(i, True)
                split_at[0] = u0 + LEAD + 8 * pairs
                unit_at[0] += 8 * pairs

            def bank_of(name):
                return turn[:, TURNS[name][0] % 2, :]

            def turned_hi(name, hi, k0, nk):
                act.wait_ge(turned, TURNS[name][0] + 1)
                src = bank_of(name)[:, 0:nk * S].rearrange("p (k n) -> p k n", k=nk)
                act.activation(hi[:, k0:k0 + nk, :], src, ACT.Copy).then_inc(turn_hi, 1)

            def rows_hi(label, t, scale=1.0):
                for g in (2 * t, 2 * t + 1):
                    act.wait_ge(turned, TURNS[f"{label}.{g}"][0] + 1)
                    act.activation(a_hi[:, 4 * (g % 2):4 * (g % 2) + 4, t * P:(t + 1) * P],
                                   bank_of(f"{label}.{g}").rearrange("p (k n) -> p k n", k=4), ACT.Copy, scale=scale)\
                        .then_inc(turn_hi, 1)

            def turned_copy(name, targets):
                act.wait_ge(turned, TURNS[name][0] + 1)
                for dst, src, scale in targets:
                    i = act.activation(dst, src, ACT.Copy, scale=scale)
                i.then_inc(freed["act"], 1)

            def squares(name, sources):
                for a, src in enumerate(sources):
                    n = src.shape[-1]
                    if sq_at[0]:
                        act.wait_ge(sq_act, sq_at[0])
                    sq_at[0] += 1
                    act.activation(act_junk[:, 0:n], src, ACT.Square, accum_out=ss(name, a)).then_inc(sq_act, 1)

            def exps(n, comps):
                act.wait_ge(masked, n + 1)
                if n >= 2:
                    act.wait_ge(mixed, n - 1)
                for j in range(comps):
                    for t in range(NT):
                        c = slice(0, P) if t == 0 else slice(P, SC_W)
                        k = 4 * (n % 2) + 2 * t + j
                        dst = probs[:, n % 2, j, c]
                        if comps == 2:
                            src = sco[:, j, c]
                        elif n < 2 * HEADS:
                            src = sco[:, n % 2, c]
                        else:
                            src = dst
                        i = act.activation(dst, src, ACT.Exp, bias=st("nmax", k, 1), accum_out=st("rsum", k, 1))
                i.then_inc(expd, 1)

            def probs_out(name, i, before):
                if i >= 2:
                    act.wait_ge(turned, TURNS[f"{before}{i - 2}"][0] + 1)
                turned_copy(name, [(probs_t[:, i % 2, :], bank_of(name)[:, 0:SC_W], 1.0)])

            rows_hi("x1", 0)
            split_to(4)
            for t in range(NT):
                act.wait_ge(x_in[t], 16)
            squares("x1", [x[:, t, :] for t in range(NT)])
            rows_hi("x1", 1)

            def start_step(k):
                if k == 1:
                    act.wait_ge(consts_in, 112)
                    act.activation(c_col[:, :], probs[:, 0, 0, 0:DK], ACT.Silu).then_inc(silu_c, 1)
                    act.activation(router_hi[:, :, :], router[:, :, :], ACT.Copy).then_inc(route_hi, 1)
                if k == 2:
                    act.wait_ge(angles, 1)
                    act.activation(trig[:, 0:2, :, :].rearrange("p a t n -> p (a t n)"), mix[:, 0:P], ACT.Sin)\
                        .then_inc(sines, 1)
                if k == 4:
                    act.wait_ge(lam_in, 1)
                    act.activation(st("lam", 2, 2), st("lam", 0, 2), ACT.Exp).then_inc(lam_exp, 1)
                if k == 3:
                    act.wait_ge(rstd_ready, 1)
                    act.wait_ge(half_ready, 1)

            block_loop("in0", 3, qkv, lambda t: rstd("x1", t), start_step)
            act.wait_ge(ada_done, 2 * DK)
            fill(0, "in7")
            squares("cq", [lat[:, t, 0:QR] for t in range(NT)])
            squares("ckv", [lat[:, t, QR:QR + KVR] for t in range(NT)])

            def ada_out(n0, n1):
                for n in range(n0, n1):
                    turned_copy(f"ad{n}", [(mod[:, n * W:(n + 1) * W], bank_of(f"ad{n}"), 1.0)])

            def q_and_k_out(name, h, scale):
                b = bank_of(name)
                turned_copy(name, [(qk_t[:, h, 0:S], b[:, 0:S], scale), (qk_t[:, h, S:2 * S], b[:, S:2 * S], 1.0)])

            q_and_k_out("qk0", 0, DA_HD ** -0.5)
            q_and_k_out("qk1", 1, DA_HD ** -0.5)
            turned_hi("cl.0", b_hi, 0, 2)
            turned_hi("cl.1", b_hi, 2, 2)
            turned_hi("cl.2", b_hi, 4, 1)
            for i in range(HEADS + 2):
                if i + 2 < HEADS:
                    q_and_k_out(f"qk{i + 2}", i + 2, DA_HD ** -0.5)
                fill(DA_FILL[i][0])
                if i < HEADS:
                    exps(i, 2)
                fill(DA_FILL[i][1])
                if 1 <= i <= HEADS:
                    probs_out(f"dap{i - 1}", i - 1, "dao")
                if i >= 2:
                    act.wait_ge(turned, TURNS[f"dao{i - 2}"][0] + 1)
                    squares(f"da{i - 2}", [bank_of(f"dao{i - 2}")[:, P * t:P * t + P] for t in range(NT)])
                fill(DA_FILL[i][2])
            ada_out(0, 4)
            for g in range(4):
                turned_hi(f"oa.{g}", a_hi, 2 * g, 2)

            scale = MLA_QK ** -0.5
            for g in range(4):
                b = bank_of(f"mr{g}")
                turned_copy(f"mr{g}", [(qr_t[2 * g + a], b[0:ROPE, a * S:(a + 1) * S], scale) for a in range(2)])
            turned_copy("kr", [(kr_t, bank_of("kr")[0:ROPE, 0:S], 1.0)])
            q_and_k_out("mq0", 0, scale)
            q_and_k_out("mq1", 1, scale)
            for i in range(HEADS + 2):
                if i + 2 < HEADS:
                    q_and_k_out(f"mq{i + 2}", i + 2, scale)
                if i < HEADS:
                    exps(HEADS + i, 1)
                fill(MLA_FILL[i])
                if 1 <= i <= HEADS:
                    probs_out(f"mp{i - 1}", i - 1, "mo")
            for g in range(4):
                turned_hi(f"ob.{g}", a_hi, 2 * g, 2)
            fill(0, "pb0")
            u_next = BLOCKS["wo0"][1]
            split_to(u_next + LEAD)
            rows_hi("mg", 0, 0.5)
            split_to(u_next + 4)
            rows_hi("mg", 1, 0.5)
            unit_at[0] = u_next
            fill(0, "wo0")
            u_next = BLOCKS["FFN"][1]
            split_to(u_next)
            banks = [2 * (BLOCKS[f"wo{n}"][0] % 2) for n in range(2)]
            act.wait_ge(first_rows, 2)
            squares("wo.0", [lin[:, b, :] for b in banks])
            split_to(u_next + LEAD)
            act.wait_ge(used, u_next)
            rows_hi("x2", 0)
            split_to(u_next + 4)
            squares("wo.1", [lin[:, b + 1, :] for b in banks])
            unit_at[0] = u_next
            rows_hi("x2", 1)
            act.wait_ge(x_ready, NT)
            squares("x2", [x[:, t, :] for t in range(NT)])

            def silu_step(scale, u_end, shift=0):
                act.wait_ge(used, u_end + shift)
                for t in range(NT):
                    act.activation(act_s[:, t, :], lin[:, t, 0:EW], ACT.Silu, scale=scale(t)).then_inc(silud, 1)

            def mlp(name, label, n, scale=lambda t: 1.0):
                u = BLOCKS[name][1]
                turn0 = TURNS[f"{label}0"][0]
                assert split_at[0] in (u + LEAD, u + 4)
                if name == "FFN":
                    split_to(u + 6)
                silu_step(scale, u + 4)
                split_to(u + 4 + LEAD)
                u += 4

                def one(e, u, last=False, shift=0, shift_e=0):
                    act.wait_ge(turned, turn0 + e + 1 + shift_e)
                    act.activation(b_hi[:, 0:2, :], turn[:, 0, :].rearrange("p (k n) -> p k n", k=2), ACT.Copy)\
                        .then_inc(turn_hi, 1)
                    for j in range(1 if last else 6):
                        if j == 3:
                            silu_step(scale, u + 4, shift)
                        if u + LEAD + j < N_UNITS:
                            split(u + LEAD + j, shift)

                one(0, u)
                u += 6
                pairs = (n - 3) // 2
                with act.Fori(0, pairs) as i:
                    for j in range(2):
                        one(1 + j, u + 6 * j, False, i * 12, i * 2)
                u += 12 * pairs
                for e in range(1 + 2 * pairs, n):
                    one(e, u, e == n - 1)
                    u += 2 if e == n - 1 else 6
                split_at[0] = min(u + LEAD - 1, N_UNITS)
                unit_at[0] = u

            act.wait_ge(rstd_ready, jobs["x2"][0] + 1)
            mlp("FFN", "ffn", N_FFN, lambda t: rstd("x2", t))
            act.wait_ge(first_rows, 3)
            squares("ffn.0", y_bank[0])
            u_next = BLOCKS["jn0"][1]
            act.wait_ge(used, u_next)
            squares("ffn.1", y_bank[1])
            act.wait_ge(x_ready, NT + 1)
            squares("u.0", [x[:, 0, :]])
            ada_out(4, 6)
            split_to(u_next + LEAD)
            turned_copy("bv", [(probs[0:HEADS, 1, 0, :], bank_of("bv")[0:HEADS, 0:SC_W], 1.0)])
            rows_hi("u", 0)
            act.wait_ge(x_ready, NT + 2)
            squares("u.1", [x[:, 1, :]])
            split_to(u_next + 4)
            rows_hi("u", 1)

            block_loop("jn0", 4, zz)
            act.wait_ge(evac["act"], BLOCKS["jn7"][4])
            squares("lt", [zz[:, t, DKV:DKV + P] for t in range(NT)])
            fill(0, "jn8")
            ada_out(6, 12)
            for t in range(NT):
                act.activation(gate2[:, t, 0:D], zz[:, t, RG:RG + D], ACT.Tanh, scale=0.5).then_inc(tanh_ready, 1)
            turned_copy("lt", [(idk_t[:, 0:S], bank_of("lt")[:, 0:S], 1.0)])
            b = bank_of("lat")[:, 0:S].rearrange("p (t n) -> p t n", t=NT)
            turned_copy("lat", [(zz[:, :, DKV:DKV + 64], b[:, :, 0:64], 1.0),
                                (zz[:, :, DKV + 64:DKV + 128], b[:, :, 0:64], 1.0),
                                (probs_t[:, :, 0:64], zz[:, :, IK:IK + 64], 1.0),
                                (probs_t[:, :, 64:128], zz[:, :, IK:IK + 64], 1.0),
                                (dv[:, :, :], b[:, :, 64:128], 1.0)])
            for g in range(4):
                turned_copy(f"rt{g}", [(rt_t[:, g, :], bank_of(f"rt{g}"), 1.0)])
            for g in range(5):
                name = f"dt{g}"
                dst = idk_t[:, :] if g == 4 else idq_t[:, 2 * g:2 * g + 2, :].rearrange("p a n -> p (a n)")
                turned_copy(name, [(dst, bank_of(name), 1.0)])

            act.wait_ge(bv_in, 16)
            for i in range(HEADS):
                act.wait_ge(idx_scored, i + 1)
                if i >= 2:
                    act.wait_ge(idx_acc, i - 1)
                act.activation(probs[:, i % 2, 0, :], sco[:, i % 2, 0:SC_W], ACT.Relu).then_inc(relud, 1)
                fill(IDX_FILL[i])
            def ret_scale(n):
                act.wait_ge(rstd_ready, jobs[f"ret{n}"][0] + 1)
                b = bank_of(f"rto{n}")
                turned_copy(f"rto{n}", [(zz[:, t, RV + n * P:RV + (n + 1) * P], b[:, P * t:P * t + P],
                                         rstd(f"ret{n}", t)) for t in range(NT)])
                act.wait_ge(freed["act"], TURNS[f"rto{n}"][2])
                act.nop().then_inc(ret_scaled, 1)

            for i in range(HEADS + 2):
                if i < HEADS:
                    if i < 2:
                        act.wait_ge(idx_acc, HEADS)
                    else:
                        act.wait_ge(decayed, i - 1)
                    g = float(np.log(np.float32(1.0 - 2.0 ** (-5.0 - i))))
                    act.activation(probs[:, i % 2, 0, :], cst[:, C_DIST:C_DIST + SC_W], ACT.Exp, scale=g)\
                        .then_inc(decay, 1)
                if i <= HEADS:
                    fill(RET_FILL[i])
                if i >= 2:
                    ret_scale(i - 2)
            for i in range(HEADS + 2):
                if i == 0:
                    for g in range(2):
                        turned_hi(f"re.{g}", a_hi, 2 * g, 2)
                fill(DSA_FILL[i])
                if i == 0:
                    for g in range(2, 4):
                        turned_hi(f"re.{g}", a_hi, 2 * g, 2)
                    gate_tanh("gt3")
                if i < HEADS:
                    exps(2 * HEADS + i, 1)
                if 1 <= i <= HEADS:
                    probs_out(f"dsp{i - 1}", i - 1, "dso")
            turned_hi("de.0", b_hi, 0, 2)
            turned_hi("de.1", b_hi, 2, 2)
            fill(0, "do0")
            u_next = BLOCKS["xo0"][1]
            split_to(u_next + LEAD - 1)
            rows_hi("mh", 0, 0.5)
            split_to(u_next + 4)
            rows_hi("mh", 1, 0.5)
            unit_at[0] = u_next
            fill(0, "xo0")
            u_next = BLOCKS["MOE"][1]
            split_to(u_next)
            act.wait_ge(x_ready, 2 * NT + 1)
            squares("v.0", [x[:, 0, :]])
            split_to(u_next + LEAD)
            rows_hi("v", 0)
            split_to(u_next + 4)
            act.wait_ge(x_ready, 2 * NT + 2)
            squares("v.1", [x[:, 1, :]])
            unit_at[0] = u_next
            rows_hi("v", 1)
            act.wait_ge(routed, 1)
            act.activation(mix[0:20, 0:S], sco[0:20, 0, 0:S], ACT.Copy).then_inc(routed_out, 1)
            act.wait_ge(route_in, 1)
            act.activation(route_x, route_x, ACT.Exp).then_inc(route_e, 1)
            act.wait_ge(route_in, 2)
            act.activation(route_y, route_y, ACT.Exp).then_inc(route_e, 1)
            mlp("MOE", "moe", N_EXP)
            for t in range(NT):
                act.wait_ge(x_ready, 3 * NT + t + 1)
                squares(f"fin.{t}", [x[:, t, :]])

        @block.vector
        def _(dve):
            split_at = [0]
            unit_at = [0]
            step = Counted(dve, dve_step)

            def split(u, shift=0):
                s = u % NSLOT
                dve.wait_ge(hi_ready, u + 1 + shift)
                dve.tensor_tensor(w_lo[:, s, :], raw[:, s, :], w_hi[:, s, :].bitcast(F32), ALU.subtract)\
                   .then_inc(lo_ready, 1)

            def split_to(n):
                while split_at[0] < min(n, N_UNITS):
                    split(split_at[0])
                    split_at[0] += 1

            def fill(n, until=None):
                end = unit_at[0] + n if until is None else BLOCKS[until][1] + BLOCKS[until][2]
                while unit_at[0] < end:
                    split_to(unit_at[0] + LEAD + 1)
                    unit_at[0] += 1
                    for name in BLOCK_NAMES:
                        if BLOCKS[name][1] + BLOCKS[name][2] == unit_at[0] and BLOCKS[name][3] == "dve":
                            evacuate(name)

            def evacuate(name):
                number, u0, units, _, _ = BLOCKS[name]
                dve.wait_ge(used, u0 + units)
                bank = 2 * (number % 2)
                kind = name.rstrip("0123456789")
                n = int(name[len(kind):])
                c = slice(n * W, (n + 1) * W)
                done = evac["dve"]
                if kind == "gt":
                    dve.wait_ge(rows_in[2], 48)
                    bias = rows[:, 2 + n // 2, (n % 2) * W:(n % 2) * W + W]
                    for t in range(NT):
                        i = dve.tensor_tensor(gate2[:, t, c], lin[:, bank + t, :], bias, ALU.add)
                    i.then_inc(done, 1)
                elif kind in ("pa", "ro"):
                    gate = gate1 if kind == "pa" else gate2
                    if kind == "ro":
                        dve.wait_ge(tanh_ready, NT + 4)
                    for t in range(NT):
                        i = dve.scalar_tensor_tensor(out=gate[:, t, c], in0=gate[:, t, c], scalar=1.0,
                                                     in1=lin[:, bank + t, :], op0=ALU.add, op1=ALU.mult)
                    i.then_inc(done, 1)
                elif kind in ("pb", "do"):
                    gate = gate1 if kind == "pb" else gate2
                    for t in range(NT):
                        merge_rows(name, gate, t)
                    dve.nop().then_inc(done, 1)
                elif kind == "wo":
                    pass
                else:
                    for t in range(NT):
                        gated_rows(n, t, done if t == NT - 1 else None)

            def merge_rows(name, gate, t):
                n = int(name[2:])
                c, cb = slice(n * W, (n + 1) * W), slice(D + n * W, D + (n + 1) * W)
                step(dve.scalar_tensor_tensor(out=gate[:, t, cb], in0=gate[:, t, cb], scalar=1.0,
                                              in1=lin[:, 2 * (BLOCKS[name][0] % 2) + t, :], op0=ALU.add, op1=ALU.mult))
                dve.tensor_tensor(gate[:, t, c], gate[:, t, c], gate[:, t, cb], ALU.add).then_inc(merged, 1)

            def merge_last(name, gate, label, next_block, count):
                u_next = BLOCKS[next_block][1]
                split_to(u_next)
                dve.wait_ge(first_rows, count)
                merge_rows(name, gate, 0)
                split_to(u_next + 1)
                dve.wait_ge(used, u_next)
                merge_rows(name, gate, 1)
                rows_lo(label, 0, 0.5)
                split_to(u_next + 4)
                rows_lo(label, 1, 0.5)
                dve.nop().then_inc(evac["dve"], 1)
                unit_at[0] = u_next

            def gated_rows(n, t, done):
                c = slice(n * W, (n + 1) * W)
                bank = 2 * (BLOCKS[f"xo{n}"][0] % 2)
                dve.wait_ge(freed["act"], TURNS["ad5"][2])
                step(dve.tensor_tensor(tmp[:, 0, :], lin[:, bank + t, :], mod[:, 2 * D + n * W:2 * D + (n + 1) * W],
                                       ALU.mult))
                i = dve.tensor_tensor(x[:, t, c], x[:, t, c], tmp[:, 0, :], ALU.add)
                if done is None:
                    step(i)
                else:
                    i.then_inc(done, 1)

            def ada_part(g0, i, k):
                slots = ada_slots(g0)
                n_s = len(slots)
                before = 32 if g0 else 0
                dve.wait_ge(ada_in[k % n_s], i * (16 * DK // n_s) + (before + 16 * (k // n_s + 1)))
                if k:
                    dve.wait_ge(ada_done, i * DK + (g0 * DK + k))
                acc = mod[:, bass.ds(i * D + g0 * D, D)]
                dve.scalar_tensor_tensor(out=acc, in0=slots[k % n_s], scalar=c_col[:, k:k + 1], in1=acc,
                                         op0=ALU.mult, op1=ALU.add).then_inc(ada_done, 1)

            def block_loop(first, pairs, beside=None, start=None):
                u0 = BLOCKS[first][1]
                assert u0 + LEAD <= split_at[0] <= u0 + 4 and unit_at[0] == u0
                for k in range(8):
                    if u0 + LEAD + k >= split_at[0]:
                        split(u0 + LEAD + k)
                    if start is not None:
                        start(k)
                with dve.Fori(1, pairs) as i:
                    for k in range(8):
                        split(u0 + LEAD + k, i * 8)
                        if beside is not None:
                            beside(i - 1, k)
                split_at[0] = u0 + LEAD + 8 * pairs
                unit_at[0] += 8 * pairs

            def bank_of(name):
                return turn[:, TURNS[name][0] % 2, :]

            turn_pairs = [0]

            def turned_lo(name, hi, lo, k0, nk):
                turn_pairs[0] += 1
                dve.wait_ge(turn_hi, turn_pairs[0])
                src = bank_of(name)[:, 0:nk * S].rearrange("p (k n) -> p k n", k=nk)
                up = hi[:, k0:k0 + nk, :].bitcast(F32)
                dve.tensor_tensor(lo[:, k0:k0 + nk, :], src, up, ALU.subtract).then_inc(freed["dve"], 1)

            def rows_lo(label, t, scale=None):
                for g in (2 * t, 2 * t + 1):
                    turn_pairs[0] += 1
                    dve.wait_ge(turn_hi, turn_pairs[0])
                    part = (slice(None), slice(4 * (g % 2), 4 * (g % 2) + 4), slice(t * P, (t + 1) * P))
                    src = bank_of(f"{label}.{g}").rearrange("p (k n) -> p k n", k=4)
                    if scale is None:
                        i = dve.tensor_tensor(a_lo[part], src, a_hi[part].bitcast(F32), ALU.subtract)
                    else:
                        i = dve.scalar_tensor_tensor(out=a_lo[part], in0=src, scalar=scale, in1=a_hi[part].bitcast(F32),
                                                     op0=ALU.mult, op1=ALU.subtract)
                    i.then_inc(freed["dve"], 1)

            def wait_norm(name):
                dve.wait_ge(rstd_ready, jobs[name][0] + 1)

            def rotate1(v, t, groups):
                rotate(dve, step, tmp, v, trig[:, 0, t, :], trig[:, 1, t, :], trig[:, 2, t, :], groups)

            def row_maxima(n, comps):
                dve.wait_ge(scored, n + 1)
                b = slice(0, 2) if comps == 2 else slice(n % 2, n % 2 + 1)
                late = sco[0:CHUNK, b, :].rearrange("p j (b c) -> p j b c", c=S)[:, :, :, CHUNK:P]
                step(dve.memset(late, NEG))
                maxima(n, comps, sco[:, b, 0:SC_W])

            def maxima(n, comps, s):
                k = 4 * (n % 2)
                for t in range(NT):
                    c = slice(0, P) if t == 0 else slice(P, SC_W)
                    i = dve.tensor_reduce(st("nmax", k + 2 * t, comps), s[:, :, c], AX.X, ALU.max, negate=True)
                i.then_inc(masked, 1)

            def head_scaled(name, n, dst, width):
                dve.wait_ge(mixed, n + 1)
                dve.wait_ge(turned, TURNS[name][0] + 1)
                b = bank_of(name)
                for t in range(NT):
                    i = dve.tensor_scalar(dst(t), b[:, width * t:width * t + width],
                                          st("rinv", 4 * (n % 2) + 2 * t, 1), None, ALU.mult)
                i.then_inc(freed["dve"], 1)
                dve.wait_ge(freed["dve"], TURNS[name][2])

            def row_sums(n):
                dve.wait_ge(expd, n + 1)
                k = 4 * (n % 2)
                dve.reciprocal(st("rinv", k, 4)[:, 0:4:2], st("rsum", k, 4)[:, 0:4:2]).then_inc(mixed, 1)

            def gained(t, gain):
                return dve.tensor_tensor(xn[:, t, :], x[:, t, :], gain, ALU.mult)

            def modulated(name, t, shift):
                wait_norm(f"{name}.{t}")
                dve.scalar_tensor_tensor(out=xn[:, t, :], in0=xn[:, t, :], scalar=rstd(name, t), in1=shift,
                                         op0=ALU.mult, op1=ALU.add).then_inc(xn_ready, 1)

            def weighted(t, banks, gain, name=None):
                for n in range(2):
                    if name is not None:
                        dve.wait_ge(sq_act, jobs[f"{name}.{t}"][5] - 1 + n)
                    step.mark(dve.tensor_tensor(xn[:, t, n * W:(n + 1) * W], banks[n], gain[:, n * W:(n + 1) * W],
                                                ALU.mult))

            def add_normed(name, t):
                wait_norm(f"{name}.{t}")
                step.wait()
                dve.scalar_tensor_tensor(out=x[:, t, :], in0=xn[:, t, :], scalar=rstd(name, t), in1=x[:, t, :],
                                         op0=ALU.mult, op1=ALU.add).then_inc(x_ready, 1)

            dve.wait_ge(rows_in[0], 16)
            for t in range(NT):
                dve.wait_ge(x_in[t], 16)
                gained(t, rows[:, 0, :]).then_inc(xn_ready, 1)
                if t == 0:
                    rows_lo("x1", 0)
                    split_to(1)
            split_to(4)
            rows_lo("x1", 1)
            dve.wait_ge(xn_ready, NT)
            dve.nop().then_inc(rows_used, 1)
            dve.wait_ge(tables_in, 16)
            dve.wait_ge(consts_in, 112)
            step(dve.tensor_copy(st("pos"), pos_i[:, :]))
            half, two, whole = mix[:, 0:64], mix[:, 64:128], mix[:, 0:128]
            kmul = tmp[:, 0, 0:P]
            for t in range(NT):
                for a in range(2):
                    step.mark(dve.tensor_scalar(mix[:, 64 * a + 32 * t:64 * a + 32 * t + 32],
                                                cst[:, C_FREQ:C_FREQ + 32], st("pos", t, 1), None, ALU.mult))
            step.wait()
            step.mark(dve.tensor_scalar(kmul[:, 0:64], half, 1.0 / (2 * np.pi), 0.25, ALU.mult, ALU.add))
            step.mark(dve.tensor_scalar(kmul[:, 64:128], two, 1.0 / (2 * np.pi), None, ALU.mult))
            step.wait()
            step(dve.tensor_scalar(kmul, kmul, ROUND, None, ALU.add))
            step(dve.tensor_scalar(kmul, kmul, ROUND, None, ALU.subtract))
            for part in TWO_PI_PARTS:
                step(dve.scalar_tensor_tensor(out=whole, in0=kmul, scalar=-part, in1=whole, op0=ALU.mult,
                                              op1=ALU.add))
            step(dve.tensor_scalar(half, half, float(np.float32(np.pi / 2)), None, ALU.add))
            dve.tensor_scalar(whole, whole, 3.1415925, -3.1415925, ALU.min, ALU.max).then_inc(angles, 1)

            def start_step(k):
                if k == 0:
                    for a in range(2):
                        lq, lk = (probs[:, 1, 0, 128 * a + 64 * b:128 * a + 64 * b + 64] for b in range(2))
                        step(dve.tensor_tensor(tmp[:, 1, 0:64], lq, lk, ALU.mult))
                        i = dve.tensor_reduce(st("lam", a, 1), tmp[:, 1, 0:64], AX.X, ALU.add)
                        if a == 0:
                            step(i)
                        else:
                            i.then_inc(lam_in, 1)
                elif k == 2:
                    dve.wait_ge(route_hi, 1)
                    dve.tensor_tensor(router_lo[:, :, :], router[:, :, :], router_hi[:, :, :].bitcast(F32),
                                      ALU.subtract).then_inc(route_lo, 1)
                elif k == 4:
                    dve.wait_ge(sines, 1)
                    step(dve.tensor_scalar(trig[:, 2, :, :], trig[:, 1, :, :], -1.0, None, ALU.mult))
                    cst_sin2 = cst[:, C_SIN2:C_SIN2 + 64].rearrange("p (t n) -> p t n", t=NT)
                    step(dve.tensor_scalar(trig[:, 3, :, :], cst_sin2, -1.0, None, ALU.mult))
                    dve.nop().then_inc(tables_ready, 1)
                elif k == 6:
                    dve.wait_ge(lam_exp, 1)
                    step(dve.tensor_tensor(st("lam", 4, 1), st("lam", 3, 1), st("lam", 2, 1), ALU.subtract))
                    step(dve.tensor_scalar(st("lam", 5, 1), st("lam", 4, 1), -LAMBDA_INIT, None, ALU.add))
                    step(dve.tensor_scalar(small[:, SM_DA:SM_DA + P], small[:, SM_DA:SM_DA + P], 1.0 - LAMBDA_INIT,
                                           None, ALU.mult))
                elif k == 7:
                    dve.wait_ge(silu_c, 1)
                    dve.wait_ge(bias_in, 16)

            block_loop("in0", 3, lambda i, k: ada_part(0, i, k), start_step)

            fill(0, "in7")
            for name, at, n, gain in (("cq", 0, QR, SM_CQ), ("ckv", QR, KVR, SM_CKV)):
                wait_norm(name)
                for t in range(NT):
                    i = dve.scalar_tensor_tensor(out=lat[:, t, at:at + n], in0=lat[:, t, at:at + n],
                                                 scalar=rstd(name, t), in1=small[:, gain:gain + n], op0=ALU.mult,
                                                 op1=ALU.mult)
                    i.then_inc(lat_ready, 1)
            for t in range(NT):
                rotate1(lat[:, t, QR + KVR:C_W].rearrange("p (g a n) -> p g a n", g=1, a=2), t, 1)
            for g, nk in ((0, 2), (1, 2), (2, 1)):
                turned_lo(f"cl.{g}", b_hi, b_lo, 2 * g, nk)

            for i in range(HEADS + 2):
                fill(DA_FILL[i][0])
                if i < HEADS:
                    row_maxima(i, 2)
                if i in ROTATED_AT:
                    t = ROTATED_AT.index(i)
                    dve.wait_ge(evac["act"], BLOCKS["uq2"][4])
                    v = qb[:, t, :].rearrange("p (h n) -> p h n", h=HEADS)[:, :, NOPE:MLA_QK]
                    rotate1(v.rearrange("p h (a n) -> p h a n", a=2), t, HEADS)
                    if t == 1:
                        dve.nop().then_inc(roped, 1)
                fill(DA_FILL[i][1])
                if i < HEADS:
                    dve.wait_ge(expd, i + 1)
                    k, h = 4 * (i % 2), i % 2
                    step(dve.reciprocal(st("rinv", k, 4), st("rsum", k, 4)))
                    step(dve.tensor_scalar(st("rinv", k, 4)[:, 1:4:2], st("rinv", k, 4)[:, 1:4:2],
                                           st("lam", 5, 1), None, ALU.mult))
                    if i >= 1:
                        dve.wait_ge(turned, TURNS[f"dap{i - 1}"][0] + 1)
                    cs = (slice(0, P), slice(P, SC_W))
                    for t in range(NT):
                        step.mark(dve.tensor_scalar(mix[:, cs[t]], probs[:, h, 0, cs[t]],
                                                    st("rinv", k + 2 * t, 1), None, ALU.mult))
                    step.wait()
                    for t in range(NT):
                        j = dve.scalar_tensor_tensor(out=mix[:, cs[t]], in0=probs[:, h, 1, cs[t]],
                                                     scalar=st("rinv", k + 2 * t + 1, 1), in1=mix[:, cs[t]],
                                                     op0=ALU.mult, op1=ALU.add)
                    j.then_inc(mixed, 1)
                if i >= 2:
                    n = i - 2
                    wait_norm(f"da{n}")
                    b = bank_of(f"dao{n}")
                    for t in range(NT):
                        j = dve.scalar_tensor_tensor(out=head_out[:, t, n, :], in0=b[:, P * t:P * t + P],
                                                     scalar=rstd(f"da{n}", t), in1=small[:, SM_DA:SM_DA + P],
                                                     op0=ALU.mult, op1=ALU.mult)
                    j.then_inc(freed["dve"], 1)
                fill(DA_FILL[i][2])
            for g in range(4):
                turned_lo(f"oa.{g}", a_hi, a_lo, 2 * g, 2)

            for i in range(HEADS + 2):
                if i < HEADS:
                    row_maxima(HEADS + i, 1)
                if 1 <= i <= HEADS:
                    row_sums(HEADS + i - 1)
                fill(MLA_FILL[i])
                if i >= 2:
                    head_scaled(f"mo{i - 2}", HEADS + i - 2, lambda t: head_out[:, t, i - 2, :], P)
            for g in range(4):
                turned_lo(f"ob.{g}", a_hi, a_lo, 2 * g, 2)
            fill(0, "pb0")
            merge_last("pb1", gate1, "mg", "wo0", 1)
            fill(0, "wo0")
            u_next = BLOCKS["FFN"][1]
            split_to(u_next)
            dve.wait_ge(rows_in[1], 16)
            dve.wait_ge(rows_in[2], 32)
            banks = [2 * (BLOCKS[f"wo{n}"][0] % 2) for n in range(2)]

            def wo_rows(t):
                weighted(t, [lin[:, b + t, :] for b in banks], rows[:, 1, :], "wo")
                add_normed("wo", t)
                dve.wait_ge(x_ready, t + 1)
                gained(t, rows[:, 2, :]).then_inc(xn_ready, 1)

            dve.wait_ge(first_rows, 2)
            wo_rows(0)
            split_to(u_next + LEAD - 1)
            rows_lo("x2", 0)
            split_to(u_next + 4)
            dve.wait_ge(used, u_next)
            wo_rows(1)
            rows_lo("x2", 1)
            dve.wait_ge(xn_ready, 2 * NT)
            unit_at[0] = u_next
            for counted in (evac["dve"], evac["dve"], rows_used, rows_used):
                dve.nop().then_inc(counted, 1)

            def hidden(e, gate):
                dve.wait_ge(silud, 2 * e)
                for t in range(NT):
                    i = dve.scalar_tensor_tensor(out=hid[:, t, :], in0=act_s[:, t, :], scalar=gate(t),
                                                 in1=lin[:, t, EW:2 * EW], op0=ALU.mult, op1=ALU.mult)
                i.then_inc(hid_ready, 1)

            def mlp(name, n, e0, gated, beside=None, late=None):
                u = BLOCKS[name][1]
                pairs0 = turn_pairs[0]

                def gate_of(e):
                    if not gated:
                        return lambda t: rstd("x2", t)
                    if isinstance(e, int):
                        return lambda t: st("gates", N_EXP * t + e, 1)
                    return lambda t: stat[:, bass.ds(e + (cols["gates"][0] + N_EXP * t), 1)]

                assert split_at[0] in (u + LEAD, u + 4)
                if not gated:
                    split_to(u + 6)
                hidden(e0 + 1, gate_of(0))
                split_to(u + 6)
                split_to(u + 4 + LEAD)
                u += 4

                def one(e, u, last=False, shift=0, shift_e=0, beside=None):
                    dve.wait_ge(turn_hi, pairs0 + e + 1 + shift_e)
                    dve.tensor_tensor(b_lo[:, 0:2, :], turn[:, 0, :].rearrange("p (k n) -> p k n", k=2),
                                      b_hi[:, 0:2, :].bitcast(F32), ALU.subtract).then_inc(freed["dve"], 1)
                    for j in range(1 if last else 6):
                        if j == 3:
                            hidden(e0 + e + 2 + shift_e, gate_of(shift_e + (e + 1)))
                        if u + LEAD + j < N_UNITS:
                            split(u + LEAD + j, shift)
                        if beside is not None and j in (0, 1, 3, 4):
                            beside((0, 1, None, 2, 3)[j])

                one(0, u)
                if beside is not None:
                    dve.wait_ge(bias_in, 32)
                u += 6
                pairs = (n - 3) // 2
                with dve.Fori(0, pairs) as i:
                    for j in range(2):
                        one(1 + j, u + 6 * j, False, i * 12, i * 2,
                            None if beside is None else lambda k: beside(i, 4 * j + k))
                u += 12 * pairs
                if late is not None:
                    late()
                for e in range(1 + 2 * pairs, n):
                    one(e, u, e == n - 1)
                    u += 2 if e == n - 1 else 6
                turn_pairs[0] += n
                split_at[0] = min(u + LEAD - 1, N_UNITS)
                unit_at[0] = u

            wait_norm("x2")

            def gain_u():
                dve.wait_ge(freed["act"], TURNS["ad3"][2])
                dve.wait_ge(pool_rows_in[0], 16)
                step(dve.scalar_tensor_tensor(out=mod[:, D:2 * D], in0=mod[:, D:2 * D], scalar=1.0, in1=rows[:, 0, :],
                                              op0=ALU.add, op1=ALU.mult))

            mlp("FFN", N_FFN, 0, False, lambda i, k: ada_part(2, i, k), gain_u)
            dve.wait_ge(first_rows, 3)
            u_next = BLOCKS["jn0"][1]

            weighted(0, y_bank[0], rows[:, 3, :], "ffn")
            add_normed("ffn", 0)
            dve.wait_ge(x_ready, NT + 1)
            step(gained(0, mod[:, D:2 * D]))
            dve.wait_ge(used, u_next)
            weighted(1, y_bank[1], rows[:, 3, :], "ffn")
            modulated("u", 0, mod[:, 0:D])
            add_normed("ffn", 1)
            dve.wait_ge(x_ready, 2 * NT)
            step(gained(1, mod[:, D:2 * D]))
            rows_lo("u", 0)
            split_to(u_next + LEAD)
            modulated("u", 1, mod[:, 0:D])
            split_to(u_next + 4)
            dve.nop().then_inc(rows_used, 1)
            rows_lo("u", 1)
            block_loop("jn0", 4)

            fill(0, "jn8")
            wait_norm("lt")
            for t in range(NT):
                dve.scalar_tensor_tensor(out=zz[:, t, DKV:DKV + P], in0=zz[:, t, DKV:DKV + P], scalar=rstd("lt", t),
                                         in1=small[:, SM_LT:SM_LT + P], op0=ALU.mult, op1=ALU.mult)\
                   .then_inc(lat_ready, 1)
            dve.wait_ge(tanh_ready, NT)
            dve.wait_ge(pool_rows_in[1], 16)
            for t in range(NT):
                g = zz[:, t, RG:RG + D]
                step(dve.scalar_tensor_tensor(out=g, in0=gate2[:, t, 0:D], scalar=1.0, in1=g, op0=ALU.add,
                                              op1=ALU.mult))
                step(dve.scalar_tensor_tensor(out=g, in0=g, scalar=0.5, in1=rows[:, 1, :], op0=ALU.mult,
                                              op1=ALU.mult))
            dve.nop().then_inc(rows_used, 1)

            for i in range(HEADS):
                dve.wait_ge(relud, i + 1)
                for t in range(NT):
                    c = slice(0, P) if t == 0 else slice(P, SC_W)
                    w = zz[:, t, IW + i:IW + i + 1]
                    if i == 0:
                        step.mark(dve.tensor_scalar(mix[:, c], probs[:, i % 2, 0, c], w, None, ALU.mult))
                    else:
                        step.mark(dve.scalar_tensor_tensor(out=mix[:, c], in0=probs[:, i % 2, 0, c], scalar=w,
                                                           in1=mix[:, c], op0=ALU.mult, op1=ALU.add))
                step.wait()
                dve.nop().then_inc(idx_acc, 1)
                fill(IDX_FILL[i])
            step(dve.tensor_scalar(mix[:, :], mix[:, :], (64 ** -0.5) * (HEADS ** -0.5), None, ALU.mult))
            for c in (CHUNK, P + P + CHUNK):
                step.mark(dve.memset(mix[0:CHUNK, c:c + CHUNK], NEG))
            step.wait()
            def top_round(t, r):
                c = slice(0, P) if t == 0 else slice(P, SC_W)
                here, there = mix[:, c], probs[:, 0, 1, c]
                if r % 2:
                    here, there = there, here
                step(dve.max(st("best"), here))
                step(dve.match_replace(there, st("best"), here, TAKEN))
                if r == TOPK // 8 - 1:
                    i = dve.tensor_scalar(sel_mask[:, c], mix[:, c], TAKEN / 2, NEG, ALU.is_gt, ALU.mult)
                    if t == 0:
                        step(i)
                    else:
                        i.then_inc(mask_ready, 1)

            dve.wait_ge(turned, TURNS["dt4"][0] + 1)

            def ret_out(n):
                dve.wait_ge(ret_scaled, n + 1)
                dve.wait_ge(mean_ready, n + 1)
                for t in range(NT):
                    v = zz[:, t, RV + n * P:RV + (n + 1) * P]
                    step.mark(dve.scalar_tensor_tensor(out=v, in0=v, scalar=ss(f"ret{n}", 2 * t),
                                                       in1=zz[:, t, RG + n * P:RG + (n + 1) * P], op0=ALU.subtract,
                                                       op1=ALU.mult))

            for i in range(HEADS + 3):
                if i < HEADS:
                    dve.wait_ge(ret_scored, i + 1)
                    dve.wait_ge(decay, i + 1)
                    dve.scalar_tensor_tensor(out=probs_t[:, i % 2, :], in0=sco[:, i % 2, 0:SC_W],
                                             scalar=64 ** -0.5, in1=probs[:, i % 2, 0, :], op0=ALU.mult,
                                             op1=ALU.mult).then_inc(decayed, 1)
                if i < HEADS:
                    for a in (2 * i, 2 * i + 1):
                        top_round(a // (TOPK // 8), a % (TOPK // 8))
                if i <= HEADS:
                    fill(RET_FILL[i])
                if i >= 3:
                    ret_out(i - 3)
                if 1 <= i <= HEADS:
                    n = i - 1
                    dve.wait_ge(turned, TURNS[f"rto{n}"][0] + 1)
                    b = bank_of(f"rto{n}")
                    if n:
                        dve.wait_ge(var_dve, n)
                    for t in range(NT):
                        step.mark(dve.bn_stats(st("bn", 6 * t, 6), b[:, P * t:P * t + P]))
                    step.wait()
                    at = jobs[f"ret{n}"][1]
                    for t in range(NT):
                        j = dve.bn_aggr(stat[:, at + 2 * t:at + 2 * t + 2], st("bn", 6 * t, 6))
                    j.then_inc(var_dve, 1)
            step.wait()
            dve.nop().then_inc(ret_done, 1)

            for i in range(HEADS + 2):
                if i == 0:
                    for g in range(2):
                        turned_lo(f"re.{g}", a_hi, a_lo, 2 * g, 2)
                fill(DSA_FILL[i])
                if i == 0:
                    for g in range(2, 4):
                        turned_lo(f"re.{g}", a_hi, a_lo, 2 * g, 2)
                if i < HEADS:
                    n, h = 2 * HEADS + i, i % 2
                    dve.wait_ge(scored, n + 1)
                    dve.wait_ge(bm_ready, i + 1)
                    if i >= 2:
                        dve.wait_ge(turned, TURNS[f"dsp{i - 2}"][0] + 1)
                    dve.scalar_tensor_tensor(out=probs[:, h, 0, :], in0=sco[:, h, 0:SC_W], scalar=64 ** -0.5,
                                             in1=probs[:, h, 1, :], op0=ALU.mult, op1=ALU.add).then_inc(copied, 1)
                    dve.wait_ge(copied, i + 1)
                    maxima(n, 1, probs[:, h, 0:1, :])
                if 1 <= i <= HEADS:
                    row_sums(2 * HEADS + i - 1)
                if i >= 2:
                    head_scaled(f"dso{i - 2}", 2 * HEADS + i - 2,
                                lambda t: zz[:, t, DQ + 64 * (i - 2):DQ + 64 * (i - 1)], 64)
            turned_lo("de.0", b_hi, b_lo, 0, 2)
            turned_lo("de.1", b_hi, b_lo, 2, 2)
            fill(0, "do0")
            merge_last("do1", gate2, "mh", "xo0", 4)
            dve.wait_ge(rows_in[0], 32)
            dve.wait_ge(freed["act"], TURNS["ad9"][2])
            step(dve.scalar_tensor_tensor(out=mod[:, 4 * D:5 * D], in0=mod[:, 4 * D:5 * D], scalar=1.0,
                                          in1=rows[:, 0, :], op0=ALU.add, op1=ALU.mult))
            fill(0, "xo0")
            u_next = BLOCKS["MOE"][1]
            split_to(u_next)
            dve.wait_ge(evac["dve"], BLOCKS["xo0"][4])
            dve.wait_ge(first_rows, 5)
            for t in range(NT):
                if t == 1:
                    split_to(u_next + LEAD - 1)
                    rows_lo("v", 0)
                    split_to(u_next + 4)
                    dve.wait_ge(used, u_next)
                gated_rows(1, t, x_ready)
                dve.wait_ge(x_ready, 2 * NT + t + 1)
                step(gained(t, mod[:, 4 * D:5 * D]))
                modulated("v", t, mod[:, 3 * D:4 * D])
            unit_at[0] = u_next
            dve.nop().then_inc(evac["dve"], 1)
            rows_lo("v", 1)

            def per(v, n):
                return v.rearrange("p (t n) -> p t n", t=NT)

            def over(v, n):
                return bass.AP(v.tensor, v.offset, [v.ap[0], v.ap[1], [0, n]])

            def first_of(eq, weights, n, m):
                w = bass.AP(weights.tensor, weights.offset, [weights.ap[0], [0, NT], [1, n]])
                step(dve.tensor_tensor(eq, eq, w, ALU.mult))
                step(dve.tensor_reduce(m, eq, AX.X, ALU.max))
                step(dve.tensor_tensor(eq, eq, over(m, n), ALU.is_equal))

            dve.wait_ge(routed, 2)
            b = sco[:, 1, 0:40].rearrange("p (t n) -> p t n", t=NT)
            bias = small[:, SM_B:SM_B + 20]
            dve.tensor_tensor(logit, b, bass.AP(bias.tensor, bias.offset, [bias.ap[0], [0, NT], [1, 20]]), ALU.add)\
               .then_inc(dve_step, 1)
            step.n += 1
            step.wait()
            gl = logit[:, :, 0:4]
            top, m = st("route", 0, 2), st("route", 2, 2)
            step(dve.tensor_reduce(top, gl, AX.X, ALU.max))
            step(dve.tensor_tensor(per(r_eq4, 4), gl, over(top, 4), ALU.is_ge))
            dve.tensor_tensor(per(route_x, 4), gl, over(top, 4), ALU.subtract).then_inc(route_in, 1)
            first_of(per(r_eq4, 4), cst[:, C_W4:C_W4 + 4], 4, m)
            spread = bass.AP(r_eq4.tensor, r_eq4.offset, [r_eq4.ap[0], [4, NT], [1, GROUPS], [0, PER_GROUP]])
            four = "p t (g n) -> p t g n"
            e4 = per(r_em, 16).rearrange(four, g=GROUPS)
            o4 = per(r_oh, 16).rearrange(four, g=GROUPS)
            step.mark(dve.tensor_tensor(e4, logit[:, :, 4:20].rearrange(four, g=GROUPS), spread, ALU.mult))
            step.mark(dve.tensor_scalar(o4, spread, -1.0, -NEG, ALU.add, ALU.mult))
            step.wait()
            step(dve.tensor_tensor(r_em, r_em, r_oh, ALU.add))
            v1, v2 = st("route", 4, 2), st("route", 6, 2)
            step(dve.tensor_reduce(v1, per(r_em, 16), AX.X, ALU.max))
            step(dve.tensor_tensor(per(r_oh, 16), per(r_em, 16), over(v1, 16), ALU.is_equal))
            first_of(per(r_oh, 16), cst[:, C_W16:C_W16 + 16], 16, m)
            step(dve.scalar_tensor_tensor(out=r_em, in0=r_oh, scalar=2 * NEG, in1=r_em, op0=ALU.mult, op1=ALU.add))
            step(dve.tensor_reduce(v2, per(r_em, 16), AX.X, ALU.max))
            step(dve.tensor_tensor(per(r_em, 16), per(r_em, 16), over(v2, 16), ALU.is_equal))
            dve.tensor_tensor(route_y, v2, v1, ALU.subtract).then_inc(route_in, 1)
            first_of(per(r_em, 16), cst[:, C_W16:C_W16 + 16], 16, m)
            dve.wait_ge(route_e, 2)
            total, w1 = st("route", 10, 2), st("route", 12, 2)
            step.mark(dve.tensor_reduce(total, per(route_x, 4), AX.X, ALU.add))
            step.mark(dve.tensor_scalar(w1, route_y, 1.0, None, ALU.add))
            step.wait()
            step(dve.tensor_tensor(w1, w1, total, ALU.mult))
            step(dve.reciprocal(w1, w1))
            step(dve.tensor_tensor(route_y, route_y, w1, ALU.mult))
            step.mark(dve.tensor_tensor(per(r_oh, 16), per(r_oh, 16), over(w1, 16), ALU.mult))
            step.mark(dve.tensor_tensor(per(r_em, 16), per(r_em, 16), over(route_y, 16), ALU.mult))
            step.wait()
            step(dve.tensor_tensor(st("gates"), r_oh, r_em, ALU.add))
            mlp("MOE", N_EXP, N_FFN, True)

            dve.wait_ge(freed["act"], TURNS["ad11"][2])
            dve.wait_ge(first_rows, 6)
            for t in range(NT):
                if t == 1:
                    dve.wait_ge(used, N_UNITS)
                weighted(t, y_bank[t], mod[:, 5 * D:6 * D])
                step.wait()
                dve.tensor_tensor(x[:, t, :], x[:, t, :], xn[:, t, :], ALU.add).then_inc(x_ready, 1)
            dve.wait_ge(x_ready, 4 * NT)
            dve.wait_ge(rows_in[1], 32)
            for t in range(NT):
                wait_norm(f"fin.{t}")
                dve.scalar_tensor_tensor(out=xn[:, t, :], in0=x[:, t, :], scalar=rstd("fin", t), in1=rows[:, 1, :],
                                         op0=ALU.mult, op1=ALU.mult).then_inc(xn_ready, 1)

        @block.tensor
        def _(pe):
            turn_at = [0]
            unit_at = [0]

            def three(dst, l_hi, l_lo, r_hi, r_lo, start, stop):
                pe.matmul(dst, l_hi, r_hi, start=start, stop=False)
                pe.matmul(dst, l_hi, r_lo, start=False, stop=False)
                return pe.matmul(dst, l_lo, r_hi, start=False, stop=stop)

            def bank_free(name):
                number = BLOCKS[name][0]
                if number >= 2:
                    before = BLOCKS[BLOCK_NAMES[number - 2]]
                    pe.wait_ge(evac[before[3]], before[4])

            def left(name):
                kind = name.rstrip("0123456789")
                if kind in ("uq", "ukv", "do"):
                    return b_hi, b_lo, 3 if kind == "ukv" else 0
                return a_hi, a_lo, 0

            def product_unit(name, part, shift=0, first=None, tokens=(0, 1)):
                number, u0, units, _, _ = BLOCKS[name]
                if first is not None:
                    number, u0 = first
                nk_all, width = LOADS[name][3], LOADS[name][2]
                u = u0 + part
                pe.wait_ge(lo_ready, u + 1 + shift)
                hi, lo, k0 = left(name)
                wh = w_hi[:, u % NSLOT, :].rearrange("p (k n) -> p k n", k=UK)
                wl = w_lo[:, u % NSLOT, :].rearrange("p (k n) -> p k n", k=UK)
                for k in range(min(UK, nk_all - part * UK)):
                    kt = part * UK + k
                    start, stop = kt == 0, kt == nk_all - 1
                    for t in tokens:
                        c = slice(t * P, (t + 1) * P)
                        i = three(lin[:, 2 * (number % 2) + t, 0:width], hi[:, k0 + kt, c], lo[:, k0 + kt, c],
                                  wh[:, k, 0:width], wl[:, k, 0:width], start, stop)
                if 1 in tokens:
                    i.then_inc(used, 1)
                return i

            def block_by_rows(name, label=None, *rows_from):
                bank_free(name)
                units = BLOCKS[name][2]
                for part in range(units):
                    if label is not None and part % 2 == 0:
                        pairs_freed(f"{label}.{part // 2}")
                    i = product_unit(name, part, tokens=(0,))
                    if label is not None and part == 2:
                        turn_second(label, *rows_from)
                if label is None:
                    i.then_inc(first_rows, 1)
                for part in range(units):
                    if label is not None and part % 2 == 0:
                        pairs_freed(f"{label}.{2 + part // 2}")
                    product_unit(name, part, tokens=(1,))
                unit_at[0] += units

            def fill(n, until=None):
                end = unit_at[0] + n if until is None else BLOCKS[until][1] + BLOCKS[until][2]
                while unit_at[0] < end:
                    for name in BLOCK_NAMES:
                        _, u0, units, _, _ = BLOCKS[name]
                        if u0 <= unit_at[0] < u0 + units:
                            if unit_at[0] == u0:
                                bank_free(name)
                            product_unit(name, unit_at[0] - u0)
                    unit_at[0] += 1

            def block_loop(first, pairs, label, rows_count):
                number, u0, units, engine, count = BLOCKS[first]
                for before in BLOCK_NAMES[max(0, number - 2):number]:
                    pe.wait_ge(evac[BLOCKS[before][3]], BLOCKS[before][4])
                block_by_rows(first, label, rows_count)
                for part in range(4):
                    product_unit(first, part, 0, (number + 1, u0 + 4))
                with pe.Fori(1, pairs) as i:
                    for j in range(2):
                        pe.wait_ge(evac[engine], i * 2 + (count - 2 + j))
                        for part in range(4):
                            product_unit(first, part, i * 8, (number + j, u0 + 4 * j))
                unit_at[0] += 8 * pairs - 4

            def turn_bank(name):
                number = TURNS[name][0]
                assert number == turn_at[0], (name, number, turn_at[0])
                turn_at[0] += 1
                if number >= 2:
                    _, engine, count = TURNS[TURN_NAMES[number - 2]]
                    pe.wait_ge(freed[engine], count)
                return turn[:, number % 2, :]

            def turn_all(name, sources):
                b = turn_bank(name)
                at = 0
                for src in sources:
                    n, m = src.shape[-1], src.shape[0]
                    i = pe.transpose(b[0:n, at:at + m], src, ident[0:m, 0:m])
                    at += m
                i.then_inc(turned, 1)

            def turn_rows(label, source, n_k=DK):
                for g in range(-(-n_k // 2)):
                    turn_all(f"{label}.{g}", [source(t, k) for k in range(2 * g, min(n_k, 2 * g + 2))
                                              for t in range(NT)])

            def turn_block(label, t, source, ready, count):
                pe.wait_ge(ready, count + t)
                for g in (2 * t, 2 * t + 1):
                    turn_all(f"{label}.{g}", [col(source[:, t, :], k) for k in range(4 * (g % 2), 4 * (g % 2) + 4)])

            def turn_first(label, count, source=xn, ready=xn_ready):
                turn_block(label, 0, source, ready, count)

            def turn_second(label, count, source=xn, ready=xn_ready):
                turn_block(label, 1, source, ready, count)

            def pairs_freed(name):
                _, engine, count = TURNS[name]
                pe.wait_ge(freed[engine], count)

            def col(v, k, n=P):
                return v[:, k * n:(k + 1) * n]

            def scores(bank, q, k):
                pe.matmul(bank[:, 0:P], q[:, 0:P], k[:, 0:P], start=True, stop=True)
                return pe.matmul(bank[:, P:SC_W], q[:, P:S], k[:, 0:S], start=True, stop=True)

            def turn_probs(name, p):
                turn_all(name, [p[:, 0:P], p[:, P:2 * P], p[:, 2 * P:3 * P]])

            def weigh(name, p, v, width):
                b = turn_bank(name)
                pe.matmul(b[:, 0:width], p[:, 0:P], v[0], start=True, stop=True)
                pe.matmul(b[:, width:2 * width], p[:, P:2 * P], v[0], start=True, stop=False)
                pe.matmul(b[:, width:2 * width], p[:, 2 * P:3 * P], v[1], start=False, stop=True).then_inc(turned, 1)

            def ada_sums(n0, n1):
                pe.wait_ge(ada_done, DK * ((n1 + 1) // 2))
                for n in range(n0, n1):
                    pe.matmul(turn_bank(f"ad{n}"), ones[:, :].broadcast_to([P, P]), mod[:, n * W:(n + 1) * W],
                              start=True, stop=True).then_inc(turned, 1)

            pe.wait_ge(tables_in, 16)
            turn_first("x1", 1)
            block_loop("in0", 3, "x1", 1)
            fill(0, "in7")
            pe.wait_ge(roped_qk, 1)
            pe.wait_ge(evac["act"], BLOCKS["in7"][4])

            def turn_qk(h):
                turn_all(f"qk{h}", [qkv[:, t, c + h * P:c + (h + 1) * P] for c in (0, D) for t in range(NT)])

            turn_qk(0)
            turn_qk(1)
            pe.wait_ge(lat_ready, 2 * NT)
            turn_rows("cl", lambda t, k: col(lat[:, t, :], k), 5)
            for i in range(HEADS + 2):
                if i + 2 < HEADS:
                    turn_qk(i + 2)
                fill(DA_FILL[i][0])
                if i < HEADS:
                    pe.wait_ge(freed["act"], TURNS[f"qk{i}"][2])
                    if i >= 1:
                        pe.wait_ge(expd, i)
                    for j in range(2):
                        rows_j = slice(DA_HD * j, DA_HD * (j + 1))
                        m = scores(sco[:, j, :], qk_t[rows_j, i, 0:S], qk_t[rows_j, i, S:2 * S])
                    m.then_inc(scored, 1)
                if i == 3:
                    pairs_freed("cl.2")
                fill(DA_FILL[i][1])
                if 1 <= i <= HEADS:
                    pe.wait_ge(mixed, i)
                    turn_probs(f"dap{i - 1}", mix)
                if i >= 2:
                    h = i - 2
                    pe.wait_ge(freed["act"], TURNS[f"dap{h}"][2])
                    weigh(f"dao{h}", probs_t[:, h % 2, :], [va[t][:, h * P:(h + 1) * P] for t in range(NT)], P)
                fill(DA_FILL[i][2])
            ada_sums(0, 4)
            pe.wait_ge(freed["dve"], TURNS["dao7"][2])
            turn_rows("oa", lambda t, k: head_out[:, t, k, :])
            pe.wait_ge(roped, 1)
            pe.wait_ge(evac["act"], BLOCKS["ukv3"][4])
            qh = [qb[:, t, :].rearrange("p (h n) -> p h n", h=HEADS) for t in range(NT)]
            for g in range(4):
                turn_all(f"mr{g}", [qh[t][:, 2 * g + a, NOPE:MLA_QK] for a in range(2) for t in range(NT)])
            turn_all("kr", [lat[:, t, QR + KVR:C_W] for t in range(NT)])
            pairs_freed("oa.3")

            def turn_mq(h):
                turn_all(f"mq{h}", [qh[t][:, h, 0:NOPE] for t in range(NT)]
                         + [kvb[t][:, 2 * P * h:2 * P * h + P] for t in range(NT)])

            turn_mq(0)
            turn_mq(1)
            for i in range(HEADS + 2):
                if i + 2 < HEADS:
                    turn_mq(i + 2)
                if i < HEADS:
                    n = HEADS + i
                    pe.wait_ge(freed["act"], TURNS[f"mq{i}"][2])
                    pe.wait_ge(expd, HEADS if i < 2 else n - 1)
                    b = sco[:, n % 2, :]
                    q, k = qk_t[:, i, 0:S], qk_t[:, i, S:2 * S]
                    for t, c, keys in ((0, slice(0, P), slice(0, P)), (1, slice(P, SC_W), slice(0, S))):
                        qt = slice(t * P, (t + 1) * P)
                        pe.matmul(b[:, c], q[:, qt], k[:, keys], start=True, stop=False)
                        m = pe.matmul(b[:, c], qr_t[i][:, qt], kr_t[:, keys], start=False, stop=True)
                    m.then_inc(scored, 1)
                fill(MLA_FILL[i])
                if 1 <= i <= HEADS:
                    pe.wait_ge(expd, HEADS + i)
                    turn_probs(f"mp{i - 1}", probs[:, (i - 1) % 2, 0, :])
                if i >= 2:
                    h = i - 2
                    pe.wait_ge(freed["act"], TURNS[f"mp{h}"][2])
                    weigh(f"mo{h}", probs_t[:, h % 2, :], [kvb[t][:, 2 * P * h + P:2 * P * (h + 1)] for t in range(NT)],
                          P)
            pe.wait_ge(freed["dve"], TURNS["mo7"][2])
            turn_rows("ob", lambda t, k: head_out[:, t, k, :])
            pairs_freed("ob.3")
            fill(0, "pb0")
            block_by_rows("pb1")
            turn_first("mg", NT + 1, gate1, merged)
            block_by_rows("wo0", "mg", NT + 1, gate1, merged)
            block_by_rows("wo1")
            turn_first("x2", NT + 1)

            def mlp(name, label, n, hid0, rows_label, count, beside=lambda t, kt: None):
                u = BLOCKS[name][1]
                turn0, _, freed0 = TURNS[f"{label}0"]

                def gate_up(u, shift=0):
                    for half in range(2):
                        pe.wait_ge(lo_ready, u + 2 * half + 2 + shift)
                        s = (u + 2 * half) % NSLOT
                        for k in range(4):
                            kt = 4 * half + k
                            rh, rl = (v[:, s:s + 2, k * EW:(k + 1) * EW] for v in (w_hi, w_lo))
                            for t in range(NT):
                                c = slice(t * P, (t + 1) * P)
                                i = three(lin[:, t, :].rearrange("p (a n) -> p a n", a=2), a_hi[:, kt, c],
                                          a_lo[:, kt, c], rh, rl, kt == 0, kt == DK - 1)
                        i.then_inc(used, 2)

                def first_gate_up(u):
                    for t in range(NT):
                        for half in range(2):
                            pairs_freed(f"{rows_label}.{2 * t + half}")
                            pe.wait_ge(lo_ready, u + 2 * half + 2)
                            s = (u + 2 * half) % NSLOT
                            for k in range(4):
                                kt = 4 * half + k
                                c = slice(t * P, (t + 1) * P)
                                rh, rl = (v[:, s:s + 2, k * EW:(k + 1) * EW] for v in (w_hi, w_lo))
                                i = three(lin[:, t, :].rearrange("p (a n) -> p a n", a=2), a_hi[:, kt, c],
                                          a_lo[:, kt, c], rh, rl, kt == 0, kt == DK - 1)
                                if (t, kt) == (0, 5):
                                    turn_second(rows_label, count)
                                beside(t, kt)
                            if t == 1:
                                i.then_inc(used, 2)

                def last_down(e, u):
                    pe.wait_ge(freed["dve"], freed0 + e)
                    pe.wait_ge(lo_ready, u + 2)
                    for t in range(NT):
                        c = slice(t * P, (t + 1) * P)
                        for k in range(2):
                            s = (u + k) % NSLOT
                            for n_ in range(2):
                                wc = slice(n_ * W, (n_ + 1) * W)
                                i = three(y_bank[t][n_], b_hi[:, k, c], b_lo[:, k, c], w_hi[:, s, wc], w_lo[:, s, wc],
                                          False, k == 1)
                            if t == 1:
                                i.then_inc(used, 1)
                        if t == 0:
                            i.then_inc(first_rows, 1)

                def turn_hidden(e, shift_e=0):
                    pe.wait_ge(hid_ready, hid0 + e + 1 + shift_e)
                    for k in range(2):
                        for t in range(NT):
                            at = k * S + t * P
                            i = pe.transpose(turn[:, 0, at:at + P], hid[:, t, k * P:(k + 1) * P], ident)
                    i.then_inc(turned, 1)

                def down(e, u, first=False, shift=0, shift_e=0):
                    pe.wait_ge(freed["dve"], freed0 + e + shift_e)
                    for k in range(2):
                        pe.wait_ge(lo_ready, u + k + 1 + shift)
                        s = (u + k) % NSLOT
                        for n_ in range(2):
                            wc = slice(n_ * W, (n_ + 1) * W)
                            for t in range(NT):
                                c = slice(t * P, (t + 1) * P)
                                i = three(y_bank[t][n_], b_hi[:, k, c], b_lo[:, k, c], w_hi[:, s, wc], w_lo[:, s, wc],
                                          first and k == 0, False)
                        i.then_inc(used, 1)

                first_gate_up(u)
                assert turn_at[0] == turn0
                u += 4
                turn_hidden(0)
                gate_up(u)
                down(0, u + 4, first=True)
                u += 6
                pairs = (n - 3) // 2
                with pe.Fori(0, pairs) as i:
                    for j in range(2):
                        turn_hidden(1 + j, i * 2)
                        gate_up(u + 6 * j, i * 12)
                        down(1 + j, u + 6 * j + 4, shift=i * 12, shift_e=i * 2)
                u += 12 * pairs
                for e in range(1 + 2 * pairs, n):
                    turn_hidden(e)
                    if e + 1 < n:
                        gate_up(u)
                        u += 4
                        down(e, u)
                    else:
                        last_down(e, u)
                    u += 2
                turn_at[0] += n
                unit_at[0] = u

            def banks_free(last):
                for engine in ("act", "dve"):
                    done = [BLOCKS[n][4] for n in BLOCK_NAMES if BLOCKS[n][3] == engine
                            and BLOCKS[n][1] <= BLOCKS[last][1]]
                    pe.wait_ge(evac[engine], max(done))
                    pe.wait_ge(freed[engine], max(TURNS[n][2] for n in TURN_NAMES[:turn_at[0] - 2]
                                                  if TURNS[n][1] == engine))

            banks_free("pb1")
            mlp("FFN", "ffn", N_FFN, 0, "x2", NT + 1)
            ada_sums(4, 6)
            pe.wait_ge(one_hot_in, 16)
            b = turn_bank("bv")
            pe.matmul(b[0:HEADS, 0:SC_W], rel_bias[:, :], mix[0:BUCKETS, :], start=True, stop=True).then_inc(turned, 1)
            turn_first("u", 2 * NT + 1)
            block_loop("jn0", 4, "u", 2 * NT + 1)
            fill(0, "jn8")
            ada_sums(6, 12)
            pe.wait_ge(lat_ready, 3 * NT)
            turn_all("lt", [zz[:, t, DKV:DKV + P] for t in range(NT)])
            pe.wait_ge(freed["act"], TURNS["lt"][2])
            b = turn_bank("lat")
            for t in range(NT):
                m = pe.matmul(b[:, t * P:(t + 1) * P], idk_t[:, t * P:(t + 1) * P], kv_up[:, :], start=True, stop=True)
            m.then_inc(turned, 1)
            pe.wait_ge(roped_qk, 2)
            for g in range(4):
                turn_all(f"rt{g}", [col(zz[:, t, c:c + W], g) for c in (RQ, RK) for t in range(NT)])
            for g in range(4):
                c = IQ if g < 2 else DQ
                turn_all(f"dt{g}", [col(zz[:, t, c:c + W], 2 * (g % 2) + a) for a in range(2) for t in range(NT)])
            pe.wait_ge(freed["act"], TURNS["lat"][2])
            turn_all("dt4", [probs_t[:, t, 0:P] for t in range(NT)] + [zz[:, t, DKV:DKV + P] for t in range(NT)])
            pe.wait_ge(freed["act"], TURNS["dt4"][2])
            for i in range(HEADS):
                if i >= 2:
                    pe.wait_ge(relud, i - 1)
                r = slice(64 * (i % 2), 64 * (i % 2) + 64)
                scores(sco[:, i % 2, :], idq_t[r, i // 2, :], idk_t[r, 0:S]).then_inc(idx_scored, 1)
                fill(IDX_FILL[i])
            for i in range(HEADS + 1):
                if i < HEADS:
                    pe.wait_ge(freed["act"], TURNS[f"rt{i // 2}"][2])
                    if i < 2:
                        pe.wait_ge(relud, HEADS)
                    else:
                        pe.wait_ge(decayed, i - 1)
                    r = slice(64 * (i % 2), 64 * (i % 2) + 64)
                    q, k = rt_t[r, i // 2, 0:S], rt_t[r, i // 2, S:2 * S]
                    b = sco[:, i % 2, :]
                    pe.matmul(b[:, 0:S], k[:, 0:P], q[:, 0:S], start=True, stop=True)
                    pe.matmul(b[:, S:SC_W], k[:, P:S], q[:, P:S], start=True, stop=True).then_inc(ret_scored, 1)
                fill(RET_FILL[i])
                if i >= 1:
                    h = i - 1
                    pe.wait_ge(decayed, i)
                    weigh(f"rto{h}", probs_t[:, h % 2, :], [zz[:, t, RV + h * P:RV + (h + 1) * P] for t in range(NT)],
                          P)
            for i in range(HEADS + 2):
                if i == 1:
                    pairs_freed("re.3")
                fill(DSA_FILL[i])
                if i < HEADS:
                    if i >= 2:
                        pe.wait_ge(copied, i - 1)
                    r = slice(64 * (i % 2), 64 * (i % 2) + 64)
                    scores(sco[:, i % 2, :], idq_t[r, 4 + i // 2, :], idk_t[r, S:2 * S]).then_inc(scored, 1)
                if i == 0:
                    pe.wait_ge(ret_done, 1)
                    turn_rows("re", lambda t, k: col(zz[:, t, RV:RV + D], k))
                if 1 <= i <= HEADS:
                    pe.wait_ge(expd, 2 * HEADS + i)
                    turn_probs(f"dsp{i - 1}", probs[:, (i - 1) % 2, 0, :])
                if i >= 2:
                    h = i - 2
                    pe.wait_ge(freed["act"], TURNS[f"dsp{h}"][2])
                    weigh(f"dso{h}", probs_t[:, h % 2, :], [dv[:, t, :] for t in range(NT)], 64)
            pe.wait_ge(freed["dve"], TURNS["dso7"][2])
            turn_rows("de", lambda t, k: col(zz[:, t, DQ:DQ + W], k), 4)
            pairs_freed("de.1")
            fill(0, "do0")
            block_by_rows("do1")
            turn_first("mh", 3 * NT + 1, gate2, merged)
            block_by_rows("xo0", "mh", 3 * NT + 1, gate2, merged)
            block_by_rows("xo1")
            turn_first("v", 3 * NT + 1)
            pe.wait_ge(route_lo, 1)
            pe.wait_ge(copied, HEADS)

            def route(t, kt):
                if (t, kt) == (0, DK - 1):
                    pairs_freed("v.3")
                    for k in range(DK):
                        m = three(sco[0:20, 0, 0:S], router_hi[:, k, :], router_lo[:, k, :], a_hi[:, k, :],
                                  a_lo[:, k, :], k == 0, k == DK - 1)
                    m.then_inc(routed, 1)
                if (t, kt) == (1, 1):
                    pe.wait_ge(routed_out, 1)
                    for b in range(NT):
                        m = pe.transpose(sco[:, 1, b * 20:b * 20 + 20], mix[0:20, b * P:(b + 1) * P], ident[0:20, 0:20])
                    m.then_inc(routed, 1)

            banks_free("xo0")
            mlp("MOE", "moe", N_EXP, N_FFN, "v", 3 * NT + 1, route)


_WEIGHTS = ["x", "positions", "w_in", "w_uq", "w_ukv", "w_proj_a", "w_proj_b", "w_o", "w_ffn_gate", "w_ffn_up",
            "w_ffn_down", "ln_mix_pre", "ln_mix_post", "ln_ffn_pre", "ln_ffn_post", "c_2", "w_ada_2", "b_ada_2",
            "norm_mix_g_2", "w_in_2", "ret_gn_g_2", "w_dsa_kv_up_2", "rel_bias_2", "w_ret_out_2", "w_dsa_out_2",
            "w_gate_2", "b_gate_2", "w_o_2", "norm_ffn_g_2", "w_exp_gate_2", "w_exp_up_2", "w_exp_down_2",
            "norm_final_g_2"]


def kernel(**inputs):
    import concourse.bacc as _bacc
    from concourse.bass_utils import run_bass_kernel_spmd as _run

    nc = _bacc.Bacc("TRN2", target_bir_lowering=False, num_devices=1)
    a = {name: np.ascontiguousarray(value) for name, value in inputs.items()}
    consts, one_hot = shape_constants()
    packed = {
        "constants": consts,
        "bucket_choice": one_hot,
        "small_gains": np.concatenate([a[n].reshape(1, -1) for n in (
            "da_subln", "q_a_norm", "kv_a_norm", "dsa_kv_norm_g_2", "b_group_router_2", "b_expert_router_2")], axis=1),
        "lambdas": np.concatenate([a[n].reshape(1, -1) for n in (
            "lambda_q1", "lambda_k1", "lambda_q2", "lambda_k2")], axis=1),
        "router": np.concatenate([a["w_group_router_2"][0], a["w_expert_router_2"][0]], axis=1),
    }
    arrays, aps = {}, {}
    for name, value in [(n, a[n]) for n in _WEIGHTS] + list(packed.items()):
        arrays[f"in_{name}_dram"] = value
        aps[name] = nc.dram_tensor(f"in_{name}_dram", value.shape, mybir.dt.from_np(value.dtype),
                                   kind="ExternalInput").ap()
    rel_rows = nc.dram_tensor("relative_rows", (HEADS, P, REL_W), F32).ap()
    out = nc.dram_tensor("out_0_dram", (1, S, D), F32, kind="ExternalOutput").ap()
    two_blocks(nc, aps, aps["constants"], aps["bucket_choice"], aps["small_gains"], aps["lambdas"], aps["router"],
               rel_rows, out)
    r = _run(nc, [arrays], core_ids=[0])
    return r.results[0]["out_0_dram"]
```
